# Optimizing a Trainium2 kernel written in Bass

```python
import math
import jax, jax.numpy as jnp
from jax import lax
import numpy as np
import jax
import jax.numpy as jnp

D_MODEL = 2048
BATCH = 1
SEQ = 256
DEPTH = 1

N_BRANCH = 4
BRANCH_W = 1024

POOL_W = BRANCH_W
POOL_WINDOWS = (2, 4, 8, 16)
POOL_GROUPS = len(POOL_WINDOWS)
POOL_GW = POOL_W // POOL_GROUPS

SGU_W = BRANCH_W
SGU_HEADS = 8
SGU_HD = SGU_W // SGU_HEADS
CHUNK = 128

N_Q_HEADS = 16
N_KV_HEADS = 2
Q_PER_KV = N_Q_HEADS // N_KV_HEADS
HEAD_DIM = 64
ATTN_W = N_Q_HEADS * HEAD_DIM
KV_W = N_KV_HEADS * HEAD_DIM
WINDOW = 128
BLOCK = 128
NUM_BUCKETS = 32
MAX_DISTANCE = 128

CONV_W = BRANCH_W
CONV_K = 31

ALPHA = (2 * DEPTH) ** 0.25
BETA = (8 * DEPTH) ** -0.25
LN_EPS = 1e-5

IN_SPLITS = (POOL_W, POOL_W,
             SGU_W, SGU_W, SGU_W,
             ATTN_W, KV_W, KV_W, ATTN_W,
             2 * CONV_W, CONV_W,
             N_BRANCH * D_MODEL)
D_IN = sum(IN_SPLITS)
SPLIT_POINTS = [int(p) for p in np.cumsum(IN_SPLITS)[:-1]]


def layer_norm(x, g, b):
    xf = x.astype(jnp.float32)
    mu = jnp.mean(xf, axis=-1, keepdims=True)
    var = jnp.mean(jnp.square(xf - mu), axis=-1, keepdims=True)
    y = (xf - mu) * lax.rsqrt(var + LN_EPS) * g.astype(jnp.float32) + b.astype(jnp.float32)
    return y.astype(x.dtype)

def t5_bucket(n):
    max_exact = NUM_BUCKETS // 2
    nf = jnp.maximum(n, 1).astype(jnp.float32)
    large = max_exact + (jnp.log(nf / max_exact) / math.log(MAX_DISTANCE / max_exact)
                         * (NUM_BUCKETS - max_exact)).astype(jnp.int32)
    large = jnp.minimum(large, NUM_BUCKETS - 1)
    return jnp.where(n < max_exact, n, large)

def band_geometry():
    i = jnp.arange(BLOCK)[:, None]
    j = jnp.arange(2 * BLOCK)[None, :]
    return i + BLOCK - j

def relative_band_bias(rel_bias):
    d = jnp.clip(band_geometry(), 0, WINDOW - 1)
    bias = rel_bias[t5_bucket(d)]
    bias = jnp.transpose(bias, (2, 0, 1)).astype(jnp.float32)
    return bias.reshape(N_KV_HEADS, Q_PER_KV, BLOCK, 2 * BLOCK)

def pool_mixer(xa, w_grp, scale):
    b, s, _ = xa.shape
    xg = xa.reshape(b, s, POOL_GROUPS, POOL_GW)
    cs = jnp.cumsum(xg.astype(jnp.float32), axis=1)
    cs_pad = jnp.concatenate([jnp.zeros_like(cs[:, :1]), cs], axis=1)
    t = jnp.arange(s)[:, None]
    win = jnp.array(POOL_WINDOWS, dtype=jnp.int32)[None, :]
    lo = jnp.maximum(t + 1 - win, 0)
    cnt = jnp.minimum(t + 1, win).astype(jnp.float32)
    gidx = jnp.arange(POOL_GROUPS)[None, :]
    window_sum = cs - cs_pad[:, lo, gidx, :]
    pooled = (window_sum / cnt[None, :, :, None]).astype(xa.dtype)
    mix = pooled - xg
    y = jnp.einsum('bsgc,gcd->bsgd', mix, w_grp).reshape(b, s, POOL_W)
    return y * scale

def spatial_gating(u, v, ln_g, ln_b, w_s, b_s):
    b, s, _ = v.shape
    nc = s // CHUNK
    vn = layer_norm(v, ln_g, ln_b).reshape(b, nc, CHUNK, SGU_HEADS, SGU_HD)
    causal = jnp.tril(jnp.ones((CHUNK, CHUNK), dtype=bool))
    w = jnp.where(causal[None], w_s, jnp.zeros_like(w_s))
    sp = jnp.einsum('hts,bnshd->bnthd', w, vn) + jnp.transpose(b_s)[None, None, :, :, None]
    return u * sp.reshape(b, s, SGU_W)

def sliding_window_attention(q, k, v, sinks, band_bias):
    b, s, _ = q.shape
    nb = s // BLOCK
    qb = q.reshape(b, nb, BLOCK, N_KV_HEADS, Q_PER_KV, HEAD_DIM)
    kb = k.reshape(b, nb, BLOCK, N_KV_HEADS, HEAD_DIM)
    vb = v.reshape(b, nb, BLOCK, N_KV_HEADS, HEAD_DIM)

    def band(t):
        prev = jnp.concatenate([jnp.zeros_like(t[:, :1]), t[:, :-1]], axis=1)
        return jnp.concatenate([prev, t], axis=2)

    k_band, v_band = band(kb), band(vb)
    logits = jnp.einsum('bnqhgd,bnkhd->bnhgqk', qb, k_band).astype(jnp.float32)
    logits = logits * (HEAD_DIM ** -0.5) + band_bias[None, None]
    d = band_geometry()
    in_window = (d >= 0) & (d < WINDOW)
    has_prev = (jnp.arange(nb)[:, None] > 0) | (jnp.arange(2 * BLOCK)[None, :] >= BLOCK)
    mask = in_window[None] & has_prev[:, None, :]
    logits = jnp.where(mask[None, :, None, None], logits, jnp.float32(-1e30))
    sink = jnp.broadcast_to(sinks.astype(jnp.float32).reshape(1, 1, N_KV_HEADS, Q_PER_KV, 1, 1),
                            logits.shape[:-1] + (1,))
    probs = jax.nn.softmax(jnp.concatenate([logits, sink], axis=-1), axis=-1)[..., :-1]
    o = jnp.einsum('bnhgqk,bnkhd->bnqhgd', probs.astype(v.dtype), v_band)
    return o.reshape(b, s, ATTN_W)

def conformer_conv(d_in, conv_w, conv_b, ln_g, ln_b):
    val, gate = jnp.split(d_in, 2, axis=-1)
    glu = val * jax.nn.sigmoid(gate)
    y = lax.conv_general_dilated(glu, conv_w[:, None, :], window_strides=(1,),
                                 padding=[(CONV_K - 1, 0)],
                                 dimension_numbers=('NWC', 'WIO', 'NWC'),
                                 feature_group_count=CONV_W) + conv_b
    return jax.nn.silu(layer_norm(y, ln_g, ln_b))

def first_inputs(seed: int = 0) -> dict:
    key = jax.random.key(seed)
    ks = jax.random.split(key, 20)
    nrm = lambda k, shape: jax.random.normal(k, shape, dtype=jnp.float32)
    return {
        "x": nrm(ks[0], (BATCH, SEQ, D_MODEL)),
        "w_in": nrm(ks[1], (DEPTH, D_MODEL, D_IN)) * D_MODEL ** -0.5,
        "pool_w": nrm(ks[2], (DEPTH, POOL_GROUPS, POOL_GW, POOL_GW)) * POOL_GW ** -0.5,
        "pool_scale": 1.0 + 0.1 * nrm(ks[3], (DEPTH, POOL_W)),
        "sgu_ln_g": 1.0 + 0.1 * nrm(ks[4], (DEPTH, SGU_W)),
        "sgu_ln_b": 0.1 * nrm(ks[5], (DEPTH, SGU_W)),
        "sgu_w": nrm(ks[6], (DEPTH, SGU_HEADS, CHUNK, CHUNK)) * 0.5 * CHUNK ** -0.5,
        "sgu_b": 1.0 + 0.1 * nrm(ks[7], (DEPTH, SGU_HEADS, CHUNK)),
        "attn_sinks": 0.5 * nrm(ks[8], (DEPTH, N_Q_HEADS)),
        "rel_bias": 0.5 * nrm(ks[9], (NUM_BUCKETS, N_Q_HEADS)),
        "conv_w": nrm(ks[10], (DEPTH, CONV_K, CONV_W)) * CONV_K ** -0.5,
        "conv_b": 0.02 * nrm(ks[11], (DEPTH, CONV_W)),
        "conv_ln_g": 1.0 + 0.1 * nrm(ks[12], (DEPTH, CONV_W)),
        "conv_ln_b": 0.1 * nrm(ks[13], (DEPTH, CONV_W)),
        "w_branch": nrm(ks[14], (DEPTH, N_BRANCH, BRANCH_W, D_MODEL)) * BRANCH_W ** -0.5 * BETA,
        "w_out": nrm(ks[15], (DEPTH, D_MODEL, D_MODEL)) * D_MODEL ** -0.5 * BETA,
        "ln_g": 1.0 + 0.1 * nrm(ks[16], (DEPTH, D_MODEL)),
        "ln_b": 0.1 * nrm(ks[17], (DEPTH, D_MODEL)),
    }

def first_block(x, w_in, pool_w, pool_scale, sgu_ln_g, sgu_ln_b, sgu_w, sgu_b, attn_sinks,
              rel_bias, conv_w, conv_b, conv_ln_g, conv_ln_b, w_branch, w_out, ln_g, ln_b):
    b, s, _ = x.shape
    band_bias = relative_band_bias(rel_bias)
    for l in range(DEPTH):
        h = jnp.einsum('bsd,de->bse', x, w_in[l])
        (a_in, a_gate, u, v, b_gate, q, k, vv, c_gate,
         d_in, d_gate, g_logits) = jnp.split(h, SPLIT_POINTS, axis=-1)

        y_a = pool_mixer(a_in, pool_w[l], pool_scale[l]) * jax.nn.silu(a_gate)
        y_b = spatial_gating(u, v, sgu_ln_g[l], sgu_ln_b[l], sgu_w[l], sgu_b[l]) * jax.nn.silu(b_gate)
        y_c = sliding_window_attention(q, k, vv, attn_sinks[l], band_bias) * jax.nn.silu(c_gate)
        y_d = conformer_conv(d_in, conv_w[l], conv_b[l], conv_ln_g[l], conv_ln_b[l]) * jax.nn.silu(d_gate)

        gates = jax.nn.sigmoid(g_logits.reshape(b, s, N_BRANCH, D_MODEL))
        branches = (y_a, y_b, y_c, y_d)
        merged = gates[:, :, 0] * jnp.einsum('bsc,cd->bsd', branches[0], w_branch[l, 0])
        for i in range(1, N_BRANCH):
            merged = merged + gates[:, :, i] * jnp.einsum('bsc,cd->bsd', branches[i], w_branch[l, i])
        out = jnp.einsum('bsd,de->bse', merged, w_out[l])
        x = layer_norm(ALPHA * x + out, ln_g[l], ln_b[l])
    return x


GRID_W = 64
CTX_LEN = 256
HEAD_DIM_2 = 128
N_GROUPS = 4
HEADS_PER_GROUP = D_MODEL // (N_GROUPS * HEAD_DIM_2)
D_MIX = N_GROUPS * HEADS_PER_GROUP * HEAD_DIM_2
Q_BLOCK = 128
ROPE_THETA = 10000.0
EPS = 1e-6
NA_KH_MAX = 8
NA_KW = 16
GQA_KV_HEADS = 2
MLA_Q_RANK = 512
MLA_KV_RANK = 256
MLA_NOPE = 128
MLA_ROPE = 64
MLA_V = 128
DIFF_D = 64
D_FF = -(-8 * D_MODEL // (3 * 256)) * 256

IN_SPLITS_2 = (
    HEADS_PER_GROUP * HEAD_DIM_2, HEADS_PER_GROUP * HEAD_DIM_2, HEADS_PER_GROUP * HEAD_DIM_2,
    HEADS_PER_GROUP * HEAD_DIM_2, GQA_KV_HEADS * HEAD_DIM_2, GQA_KV_HEADS * HEAD_DIM_2,
    MLA_Q_RANK, MLA_KV_RANK, MLA_ROPE,
    HEADS_PER_GROUP * 2 * DIFF_D, HEADS_PER_GROUP * 2 * DIFF_D, HEADS_PER_GROUP * 2 * DIFF_D,
)
D_IN_2 = sum(IN_SPLITS_2)


def rms_norm(x, g):
    xf = x.astype(jnp.float32)
    y = xf * lax.rsqrt(jnp.mean(xf * xf, axis=-1, keepdims=True) + EPS)
    return y.astype(x.dtype) * g

def axial_rope(n_tokens, dim):
    t = jnp.arange(n_tokens, dtype=jnp.int32)
    row = (t // GRID_W).astype(jnp.float32)
    col = (t % GRID_W).astype(jnp.float32)
    d_axis = dim // 2
    inv = 1.0 / (ROPE_THETA ** (jnp.arange(0, d_axis, 2, dtype=jnp.float32) / d_axis))
    ang = jnp.concatenate([row[:, None] * inv, col[:, None] * inv], axis=-1)
    return jnp.cos(ang), jnp.sin(ang)

def apply_rope(x, cos, sin):
    x1, x2 = jnp.split(x, 2, axis=-1)
    return jnp.concatenate([x1 * cos - x2 * sin, x1 * sin + x2 * cos], axis=-1).astype(x.dtype)

def to_heads(a, n_heads):
    b, t, _ = a.shape
    return a.reshape(b, t, n_heads, -1).transpose(0, 2, 1, 3)

def over_query_blocks(fn, q):
    *lead, s, d = q.shape
    nb = s // Q_BLOCK
    qb = jnp.moveaxis(q.reshape(*lead, nb, Q_BLOCK, d), -3, 0)
    out = lax.map(fn, qb)
    out = jnp.moveaxis(out, 0, -3)
    return out.reshape(*out.shape[:-3], s, out.shape[-1])

def softmax_attend(q, k, v, scale):
    s = jnp.einsum('bkgqd,bktd->bkgqt', q, k).astype(jnp.float32) * scale
    p = jax.nn.softmax(s, axis=-1).astype(v.dtype)
    return jnp.einsum('bkgqt,bktd->bkgqd', p, v)

def neighbourhood_attention(q, k, v, k_ctx, v_ctx, rpb):
    b, h, s, d = q.shape
    rows = s // GRID_W
    kh = min(NA_KH_MAX, rows)
    scale = d ** -0.5
    qg = q.reshape(b, h, rows, GRID_W, d)
    kg = k.reshape(b, h, rows, GRID_W, d)
    vg = v.reshape(b, h, rows, GRID_W, d)
    cols = np.arange(GRID_W)
    c_start = np.clip(cols - NA_KW // 2, 0, GRID_W - NA_KW)
    col_idx = c_start[:, None] + np.arange(NA_KW)[None, :]
    dc_idx = col_idx - cols[:, None] + (NA_KW - 1)
    col_bias = rpb[:, :, dc_idx]
    n_win = kh * NA_KW

    def row_block(r):
        r_start = jnp.clip(r - kh // 2, 0, rows - kh)
        q_r = lax.dynamic_index_in_dim(qg, r, axis=2, keepdims=False)
        k_win = lax.dynamic_slice_in_dim(kg, r_start, kh, axis=2)[:, :, :, col_idx]
        v_win = lax.dynamic_slice_in_dim(vg, r_start, kh, axis=2)[:, :, :, col_idx]
        dr_idx = r_start + jnp.arange(kh) - r + (NA_KH_MAX - 1)
        bias = jnp.take(col_bias, dr_idx, axis=1).transpose(0, 2, 1, 3)
        s_win = jnp.einsum('bhcd,bhicjd->bhcij', q_r, k_win).astype(jnp.float32) * scale + bias.astype(jnp.float32)
        s_ctx = jnp.einsum('bhcd,bhtd->bhct', q_r, k_ctx).astype(jnp.float32) * scale
        p = jax.nn.softmax(jnp.concatenate([s_win.reshape(b, h, GRID_W, n_win), s_ctx], axis=-1), axis=-1).astype(v.dtype)
        p_win = p[..., :n_win].reshape(b, h, GRID_W, kh, NA_KW)
        p_ctx = p[..., n_win:]
        return jnp.einsum('bhcij,bhicjd->bhcd', p_win, v_win) + jnp.einsum('bhct,bhtd->bhcd', p_ctx, v_ctx)

    out = lax.map(row_block, jnp.arange(rows))
    return jnp.moveaxis(out, 0, 2).reshape(b, h, s, d)

def na_mixer(q_l, k_l, v_l, q_c, k_c, v_c, rpb, ctx_out):
    H = HEADS_PER_GROUP
    kc, vc = to_heads(k_c, H), to_heads(v_c, H)
    ol = neighbourhood_attention(to_heads(q_l, H), to_heads(k_l, H), to_heads(v_l, H), kc, vc, rpb)
    oc = None
    if ctx_out:
        oc = softmax_attend(to_heads(q_c, H)[:, :, None], kc, vc, HEAD_DIM_2 ** -0.5)[:, :, 0]
    return ol, oc

def gqa_mixer(q_l, k_l, v_l, q_c, k_c, v_c, g_q, g_k, rope, ctx_out):
    H, KV = HEADS_PER_GROUP, GQA_KV_HEADS
    G = H // KV
    cos, sin = rope
    scale = HEAD_DIM_2 ** -0.5

    def grouped(q):
        b, _, t, d = q.shape
        return q.reshape(b, KV, G, t, d)

    ql = grouped(apply_rope(rms_norm(to_heads(q_l, H), g_q), cos, sin))
    kl = apply_rope(rms_norm(to_heads(k_l, KV), g_k), cos, sin)
    kc = rms_norm(to_heads(k_c, KV), g_k)
    vc = to_heads(v_c, KV)
    k_all = jnp.concatenate([kc, kl], axis=2)
    v_all = jnp.concatenate([vc, to_heads(v_l, KV)], axis=2)
    ol = over_query_blocks(lambda qb: softmax_attend(qb, k_all, v_all, scale), ql)
    b, _, _, s, d = ol.shape
    ol = ol.reshape(b, H, s, d)
    oc = None
    if ctx_out:
        qc = grouped(rms_norm(to_heads(q_c, H), g_q))
        oc = softmax_attend(qc, kc, vc, scale).reshape(b, H, -1, d)
    return ol, oc

def mla_mixer(cq_l, ckv_l, kpe_l, cq_c, ckv_c, kpe_c, g_q, g_kv, w_uq, w_ukv, rope, ctx_out):
    H = HEADS_PER_GROUP
    cos, sin = rope
    scale = (MLA_NOPE + MLA_ROPE) ** -0.5

    def queries(cq, rot):
        q = to_heads(rms_norm(cq, g_q) @ w_uq, H)
        q_nope, q_pe = q[..., :MLA_NOPE], q[..., MLA_NOPE:]
        if rot:
            q_pe = apply_rope(q_pe, cos, sin)
        return jnp.concatenate([q_nope, q_pe], axis=-1)[:, :, None]

    def keys_values(ckv, kpe, rot):
        kv = to_heads(rms_norm(ckv, g_kv) @ w_ukv, H)
        k_nope, v = kv[..., :MLA_NOPE], kv[..., MLA_NOPE:]
        k_pe = kpe[:, None]
        if rot:
            k_pe = apply_rope(k_pe, cos, sin)
        k_pe = jnp.broadcast_to(k_pe, k_nope.shape[:-1] + (MLA_ROPE,))
        return jnp.concatenate([k_nope, k_pe], axis=-1), v

    kl, vl = keys_values(ckv_l, kpe_l, True)
    kc, vc = keys_values(ckv_c, kpe_c, False)
    k_all = jnp.concatenate([kc, kl], axis=2)
    v_all = jnp.concatenate([vc, vl], axis=2)
    ol = over_query_blocks(lambda qb: softmax_attend(qb, k_all, v_all, scale), queries(cq_l, True))[:, :, 0]
    oc = None
    if ctx_out:
        oc = softmax_attend(queries(cq_c, False), kc, vc, scale)[:, :, 0]
    return ol, oc

def diff_mixer(q_l, k_l, v_l, q_c, k_c, v_c, lq1, lk1, lq2, lk2, g_sub, lam_init, rope, ctx_out):
    H = HEADS_PER_GROUP
    cos, sin = rope
    scale = DIFF_D ** -0.5
    f32 = jnp.float32
    lam = (jnp.exp(jnp.sum(lq1.astype(f32) * lk1.astype(f32)))
           - jnp.exp(jnp.sum(lq2.astype(f32) * lk2.astype(f32))) + lam_init)

    def pair_heads(a):
        b, t, _ = a.shape
        return a.reshape(b, t, H, 2, DIFF_D).transpose(0, 2, 3, 1, 4)

    def attend(q, k, v):
        s = jnp.einsum('bhiqd,bhitd->bhiqt', q, k).astype(f32) * scale
        p = jax.nn.softmax(s, axis=-1)
        w = (p[:, :, 0] - lam * p[:, :, 1]).astype(v.dtype)
        return jnp.einsum('bhqt,bhtd->bhqd', w, v)

    def finish(o):
        return rms_norm(o, g_sub) * (1.0 - lam_init)

    ql = apply_rope(pair_heads(q_l), cos, sin)
    kl = apply_rope(pair_heads(k_l), cos, sin)
    kc = pair_heads(k_c)
    vc = to_heads(v_c, H)
    k_all = jnp.concatenate([kc, kl], axis=3)
    v_all = jnp.concatenate([vc, to_heads(v_l, H)], axis=2)
    ol = finish(over_query_blocks(lambda qb: attend(qb, k_all, v_all), ql))
    oc = None
    if ctx_out:
        oc = finish(attend(pair_heads(q_c), kc, vc))
    return ol, oc

def hybrid_mixer(h, hc, w_in, w_out, rpb, gqa_gq, gqa_gk, mla_gq, mla_gkv, mla_wuq, mla_wukv,
                 lq1, lk1, lq2, lk2, g_sub, lam_init, rope128, rope64, ctx_out):
    offsets = np.cumsum(IN_SPLITS_2)[:-1].tolist()
    pl = jnp.split(h @ w_in, offsets, axis=-1)
    pc = jnp.split(hc @ w_in, offsets, axis=-1)
    oa, oac = na_mixer(*pl[0:3], *pc[0:3], rpb, ctx_out)
    ob, obc = gqa_mixer(*pl[3:6], *pc[3:6], gqa_gq, gqa_gk, rope128, ctx_out)
    oc, occ = mla_mixer(*pl[6:9], *pc[6:9], mla_gq, mla_gkv, mla_wuq, mla_wukv, rope64, ctx_out)
    od, odc = diff_mixer(*pl[9:12], *pc[9:12], lq1, lk1, lq2, lk2, g_sub, lam_init, rope64, ctx_out)

    def merge(parts):
        o = jnp.concatenate(parts, axis=1)
        b, n, t, d = o.shape
        return o.transpose(0, 2, 1, 3).reshape(b, t, n * d) @ w_out

    out_c = merge([oac, obc, occ, odc]) if ctx_out else None
    return merge([oa, ob, oc, od]), out_c

def swiglu(h, wg, wu, wd):
    return (jax.nn.silu(h @ wg) * (h @ wu)) @ wd

def second_inputs(seed: int = 0) -> dict:
    key = jax.random.key(seed)
    ks = iter(jax.random.split(key, 32))
    L, D, H = DEPTH, D_MODEL, HEADS_PER_GROUP

    def nrm(shape, scale):
        return jax.random.normal(next(ks), shape, jnp.float32) * scale

    def gain(shape):
        return 1.0 + 0.02 * jax.random.normal(next(ks), shape, jnp.float32)

    return {
        'x': nrm((BATCH, SEQ, D), 1.0),
        'c': nrm((BATCH, D), 1.0),
        'ctx': nrm((BATCH, CTX_LEN, D), 1.0),
        'c_ctx': nrm((D,), 1.0),
        'w_ada': nrm((L, D, 6 * D), D ** -0.5),
        'b_ada': nrm((L, 6 * D), 0.02),
        'g_attn': gain((L, D)),
        'g_ffn': gain((L, D)),
        'w_in': nrm((L, D, D_IN_2), D ** -0.5),
        'w_out': nrm((L, D_MIX, D), D_MIX ** -0.5),
        'na_rpb': nrm((L, H, 2 * NA_KH_MAX - 1, 2 * NA_KW - 1), 0.1),
        'gqa_gq': gain((L, HEAD_DIM_2)),
        'gqa_gk': gain((L, HEAD_DIM_2)),
        'mla_gq': gain((L, MLA_Q_RANK)),
        'mla_gkv': gain((L, MLA_KV_RANK)),
        'mla_wuq': nrm((L, MLA_Q_RANK, H * (MLA_NOPE + MLA_ROPE)), MLA_Q_RANK ** -0.5),
        'mla_wukv': nrm((L, MLA_KV_RANK, H * (MLA_NOPE + MLA_V)), MLA_KV_RANK ** -0.5),
        'diff_lq1': nrm((L, DIFF_D), 0.1),
        'diff_lk1': nrm((L, DIFF_D), 0.1),
        'diff_lq2': nrm((L, DIFF_D), 0.1),
        'diff_lk2': nrm((L, DIFF_D), 0.1),
        'diff_gsub': gain((L, 2 * DIFF_D)),
        'ffn_wg': nrm((L, D, D_FF), D ** -0.5),
        'ffn_wu': nrm((L, D, D_FF), D ** -0.5),
        'ffn_wd': nrm((L, D_FF, D), D_FF ** -0.5),
        'g_final': gain((D,)),
    }

def second_block(x, c, ctx, c_ctx, w_ada, b_ada, g_attn, g_ffn, w_in, w_out, na_rpb, gqa_gq, gqa_gk,
              mla_gq, mla_gkv, mla_wuq, mla_wukv, diff_lq1, diff_lk1, diff_lq2, diff_lk2, diff_gsub,
              ffn_wg, ffn_wu, ffn_wd, g_final):
    s = x.shape[1]
    rope128 = axial_rope(s, HEAD_DIM_2)
    rope64 = axial_rope(s, MLA_ROPE)
    silu_c = jax.nn.silu(c)
    silu_cc = jax.nn.silu(c_ctx)
    xc = ctx
    for l in range(DEPTH):
        ctx_out = l < DEPTH - 1
        lam_init = 0.8 - 0.6 * math.exp(-0.3 * l)
        mod = (silu_c @ w_ada[l] + b_ada[l])[:, None, :]
        mod_c = silu_cc @ w_ada[l] + b_ada[l]
        sh_a, sc_a, gt_a, sh_f, sc_f, gt_f = jnp.split(mod, 6, axis=-1)
        csh_a, csc_a, cgt_a, csh_f, csc_f, cgt_f = jnp.split(mod_c, 6, axis=-1)
        h = rms_norm(x, g_attn[l]) * (1.0 + sc_a) + sh_a
        hc = rms_norm(xc, g_attn[l]) * (1.0 + csc_a) + csh_a
        o_l, o_c = hybrid_mixer(h, hc, w_in[l], w_out[l], na_rpb[l], gqa_gq[l], gqa_gk[l],
                                mla_gq[l], mla_gkv[l], mla_wuq[l], mla_wukv[l],
                                diff_lq1[l], diff_lk1[l], diff_lq2[l], diff_lk2[l], diff_gsub[l],
                                lam_init, rope128, rope64, ctx_out)
        x = x + gt_a * o_l
        h = rms_norm(x, g_ffn[l]) * (1.0 + sc_f) + sh_f
        x = x + gt_f * swiglu(h, ffn_wg[l], ffn_wu[l], ffn_wd[l])
        if ctx_out:
            xc = xc + cgt_a * o_c
            hc = rms_norm(xc, g_ffn[l]) * (1.0 + csc_f) + csh_f
            xc = xc + cgt_f * swiglu(hc, ffn_wg[l], ffn_wu[l], ffn_wd[l])
    return rms_norm(x, g_final)


def setup_inputs(seed=0):
    out = dict(first_inputs(seed))
    for name, value in second_inputs(seed + 1).items():
        if name != "x":
            out[name + "_2"] = value
    return out


def reference(
    x, w_in, pool_w, pool_scale, sgu_ln_g, sgu_ln_b, sgu_w, sgu_b, attn_sinks, rel_bias, conv_w,
    conv_b, conv_ln_g, conv_ln_b, w_branch, w_out, ln_g, ln_b, c_2, ctx_2, c_ctx_2, w_ada_2,
    b_ada_2, g_attn_2, g_ffn_2, w_in_2, w_out_2, na_rpb_2, gqa_gq_2, gqa_gk_2, mla_gq_2,
    mla_gkv_2, mla_wuq_2, mla_wukv_2, diff_lq1_2, diff_lk1_2, diff_lq2_2, diff_lk2_2,
    diff_gsub_2, ffn_wg_2, ffn_wu_2, ffn_wd_2, g_final_2,
):
    x = first_block(
        x, w_in, pool_w, pool_scale, sgu_ln_g, sgu_ln_b, sgu_w, sgu_b, attn_sinks, rel_bias,
        conv_w, conv_b, conv_ln_g, conv_ln_b, w_branch, w_out, ln_g, ln_b,
    )
    return second_block(
        x, c_2, ctx_2, c_ctx_2, w_ada_2, b_ada_2, g_attn_2, g_ffn_2, w_in_2, w_out_2, na_rpb_2,
        gqa_gq_2, gqa_gk_2, mla_gq_2, mla_gkv_2, mla_wuq_2, mla_wukv_2, diff_lq1_2, diff_lk1_2,
        diff_lq2_2, diff_lk2_2, diff_gsub_2, ffn_wg_2, ffn_wu_2, ffn_wd_2, g_final_2,
    )


_drawn_inputs = setup_inputs


def setup_inputs(seed=0):
    import zlib

    import numpy as np

    out = dict(_drawn_inputs(seed))
    spreads = {}
    factors = {'pool_scale': 6.865,
     'sgu_ln_g': 8.0,
     'sgu_ln_b': 8.0,
     'sgu_b': 5.784,
     'attn_sinks': 8.0,
     'rel_bias': 6.721,
     'conv_b': 8.0,
     'conv_ln_g': 8.0,
     'conv_ln_b': 8.0,
     'g_attn_2': 8.0,
     'g_ffn_2': 4.424,
     'na_rpb_2': 8.0,
     'gqa_gq_2': 8.0,
     'gqa_gk_2': 8.0,
     'mla_gq_2': 8.0,
     'mla_gkv_2': 8.0,
     'diff_lq1_2': 3.697,
     'diff_lk1_2': 3.157,
     'diff_lq2_2': 5.384,
     'diff_lk2_2': 8.0,
     'diff_gsub_2': 8.0,
     'g_final_2': 2.735}
    for name, (base, spread) in spreads.items():
        noise = np.random.default_rng([zlib.crc32(name.encode()), seed]).standard_normal(out[name].shape)
        drawn = base * np.exp(spread * noise) if base else spread * noise
        out[name] = jnp.asarray(drawn.astype(out[name].dtype))
    for name, factor in factors.items():
        out[name] = (out[name] * factor).astype(out[name].dtype)
    return out
```

```python
import math
from contextlib import ExitStack

import numpy as np
import concourse.bass as bass
from concourse import mybir

F32 = mybir.dt.float32
F32R = mybir.dt.float32r
ALU = mybir.AluOpType
ACT = mybir.ActivationFunctionType
AX = mybir.AxisListType.X

BASE = 16512
KB = 1024
NRAW = 4
NSPL = 5
LEAD = 4
NMAIN = 4
NEG = -1e30
ALPHA = 2 ** 0.25
EPS_LN = 1e-5
EPS_RMS = 1e-6
LAM0 = 0.8 - 0.6 * math.exp(-0.3 * 0)


class DmaSlot:

    def __init__(self, sem):
        self.sem, self.n = sem, 0


class Queues:

    def __init__(self, sems):
        self.sems = sems
        self.cnt = {e: 0 for e in sems}
        self.q = {e: [] for e in sems}
        self.seen = {e: {} for e in sems}

    def _waits(self, e, waits):
        for w in waits:
            if w is None:
                continue
            if isinstance(w, list):
                self._waits(e, w)
                continue
            sem, v = w
            if self.seen[e].get(id(sem), 0) < v:
                self.seen[e][id(sem)] = v
                self.q[e].append(("wait", sem, v))

    def op(self, e, fn, *waits, sig=None):
        self._waits(e, waits)
        if sig is None:
            sig = e != "P"
        if sig:
            self.cnt[e] += 1
            self.q[e].append(("op", fn, self.sems[e], 1))
            return (self.sems[e], self.cnt[e])
        self.q[e].append(("op", fn, None, 0))
        return None

    def dma(self, e, dst, src, slot, *waits):
        self._waits(e, waits)
        slot.n += 16
        self.q[e].append(("op", lambda g: g.dma_start(dst, src), slot.sem, 16))
        return (slot.sem, slot.n)

    def wait(self, e, *waits):
        self._waits(e, waits)

    def run(self, e, eng):
        for item in self.q[e]:
            if item[0] == "wait":
                eng.wait_ge(item[1], item[2])
            else:
                ins = item[1](eng)
                if item[2] is not None:
                    ins.then_inc(item[2], item[3])


def t5_buckets():
    n = np.arange(128)
    nf = np.maximum(n, 1).astype(np.float32)
    large = 16 + (np.log(nf / np.float32(16)) / np.float32(math.log(8)) * np.float32(16)).astype(np.int32)
    return np.where(n < 16, n, np.minimum(large, 31))


def constants():
    c = {}
    pm = np.zeros((256, 4, 256), np.float32)
    for g, w in enumerate((2, 4, 8, 16)):
        for t in range(256):
            lo = max(t + 1 - w, 0)
            pm[lo:t + 1, g, t] = np.float32(1.0) / np.float32(min(t + 1, w))
            pm[t, g, t] -= np.float32(1.0)
    c["k_pool"] = pm
    oh = np.zeros((32, 128), np.float32)
    oh[t5_buckets()[127 - np.arange(128)], np.arange(128)] = 1.0
    c["k_bucket"] = oh
    q = np.arange(64)[:, None]
    k = np.arange(64)[None, :]
    st = np.clip(q - 8, 0, 48)
    m = np.where((k >= st) & (k < st + 16), 0.0, NEG).astype(np.float32)
    c["k_namask"] = np.concatenate([m, m], 0)

    def rope(dim):
        t = np.arange(256)
        row, col = (t // 64).astype(np.float32), (t % 64).astype(np.float32)
        da = dim // 2
        inv = (1.0 / (np.float32(10000.0) ** (np.arange(0, da, 2, dtype=np.float32) / np.float32(da)))).astype(np.float32)
        ang = np.concatenate([row[:, None] * inv, col[:, None] * inv], -1).astype(np.float32)
        co, si = np.cos(ang), np.sin(ang)
        return np.stack([np.concatenate([co, co], -1), np.concatenate([-si, si], -1)], 1).astype(np.float32)

    c["k_rope128"] = rope(128)
    c["k_rope64"] = rope(64)
    return c


def program(nc, I, out, stage=0, dbg=None):
    ctx = ExitStack()
    with ctx:
        def sem(name):
            return ctx.enter_context(nc.semaphore(name))

        def at(name, off, shape, dt=F32):
            n = 4
            for s in shape[1:]:
                n *= s
            assert off % 32 == 0
            return nc.alloc_sbuf_tensor_at(name, shape, dt, offset=BASE + off)

        o = 0
        oRAW = o; o += NRAW * 8 * KB
        oHI = o; o += NSPL * 4 * KB
        oLO = o; o += NSPL * 4 * KB
        oFX = o; o += 32 * KB
        oFY = o; o += 16 * KB
        oMG = o; o += 16 * KB
        oR1 = o; o += 26 * KB
        oR2 = o; o += 20 * KB
        oSG = o; o += 4 * KB
        oSW = o; o += 4 * KB
        oEX = o; o += 4 * KB
        oAC = o; o += 4 * KB
        oSM = o

        raw = at("raw", oRAW, [128, NRAW, 4, 512])
        whi = at("whi", oHI, [128, NSPL, 2, 512], F32R)
        wlo = at("wlo", oLO, [128, NSPL, 2, 512], F32R)
        sg = at("sg", oSG, [128, 2, 512])
        acc = at("acc", oAC, [128, 2, 512])

        sm = [oSM]

        def small(name, shape, dt=F32):
            n = 4
            for s in shape[1:]:
                n *= s
            r = at(name, sm[0], shape, dt)
            sm[0] += -(-n // 32) * 32
            return r

        ident = small("ident", [128, 128])
        ones = small("ones", [128, 128])
        par = small("par", [128, 112])
        mod = small("mod", [128, 6, 16])
        brow = small("brow", [128, 512])
        rope_off = sm[0]
        ropeA = small("ropeA", [128, 2, 2, 128])
        ropeB = small("ropeB", [128, 2, 2, 64])
        cw = at("cw", rope_off, [128, 8, 31])
        grow = small("grow", [128, 3, 128])
        nam = small("nam", [128, 64])
        st = small("st", [128, 4, 6])
        mv = small("mv", [128, 2])
        rs = small("rs", [128, 24])
        mhalf = small("half", [128, 24])
        silc = small("silc", [128, 2, 16])
        lamt = small("lamt", [128, 8])
        snk = small("snk", [128, 16])
        smx = small("smx", [128, 8, 8])
        assert BASE + sm[0] <= 229368, (BASE + sm[0] - 229368)

        banks = [ctx.enter_context(nc.psum_tensor(f"pb{i}", [128, 512], F32)) for i in range(8)]
        sems = {e: sem("e" + e) for e in "PVAGS"}
        Q = Queues(sems)
        rawslot = [DmaSlot(sem(f"dw{i}")) for i in range(NRAW)]
        nslots = [0]

        def slot():
            nslots[0] += 1
            return DmaSlot(sem(f"dm{nslots[0]}"))

        def dram(name, shape):
            return nc.dram_tensor(name, shape, F32, kind="Internal").ap()

        scr_band = dram("scr_band", [128 * 16 * 384])
        scr_na = dram("scr_na", [64 * 60 * 128])
        scr_x1 = dram("scr_x1", [128, 2, 2048])

        def V(fn, *w): return Q.op("V", fn, *w)
        def A(fn, *w): return Q.op("A", fn, *w)
        def G(fn, *w): return Q.op("G", fn, *w)
        def P(fn, *w, sig=False): return Q.op("P", fn, *w, sig=sig)

        def act(dst, src, f, *w, **kw):
            return A(lambda e: e.activation(dst, src, f, **kw), *w)

        def copyA(dst, src, *w):
            return act(dst, src, ACT.Copy, *w)

        def copyV(dst, src, *w):
            return V(lambda e: e.tensor_copy(dst, src), *w)

        def tt(dst, a, b, op, *w):
            return V(lambda e: e.tensor_tensor(dst, a, b, op), *w)

        def ts(dst, a, s1, s2, o1, o2, *w):
            return V(lambda e: e.tensor_scalar(dst, a, s1, s2, o1, o2), *w)

        def ts1(dst, a, s1, o1, *w):
            return V(lambda e: e.tensor_scalar(dst, a, s1, None, o1), *w)

        def stt(dst, a, s, b, o1, o2, *w):
            return V(lambda e: e.scalar_tensor_tensor(dst, a, s, b, o1, o2), *w)

        def mm(dst, l, r, start, stop, *w, sig=False):
            return P(lambda e: e.matmul(dst, l, r, start=start, stop=stop), *w, sig=sig)

        def tr(dst, src, *w, sig=False):
            n = src.shape[0]
            return P(lambda e: e.transpose(dst, src, ident[0:n, 0:n]), *w, sig=sig)

        def f32(ap):
            return ap.bitcast(F32)

        sidefree = {b: None for b in range(NMAIN, 8)}
        held = set()

        def take():
            while True:
                for b in sidefree:
                    if b not in held:
                        held.add(b)
                        return b
                yield False

        def give(b, tok):
            held.discard(b)
            sidefree[b] = tok

        ready = {}

        def rstd(dst, src, scale, eps, *w):
            n = src.shape[1]
            t = ts(dst, src, scale, eps, ALU.mult, ALU.add, *w)
            return G(lambda e: e.tensor_tensor(dst, dst, mhalf[:, 0:n], ALU.pow), t, ready["half"])

        main_free = [None] * NMAIN
        main_next = [0]
        spl_free = [None] * NSPL
        raw_free = [None] * NRAW
        raw_tok = {}

        loads = []
        subs = []
        jobs = []

        def gemm(src, kts, ncols, stat, tbs, evac, need=(), ktneed=None, evneed=()):
            j = dict(kts=kts, ncols=ncols, stat=stat, tbs=tbs, evac=evac, need=need, kind="mm",
                     ktneed=ktneed or {}, evneed=evneed)
            jobs.append(j)
            n = len(kts)
            for a in range(0, n, 4):
                c = min(4, n - a)
                r = kts[a] * 128
                assert list(kts[a:a + c]) == list(range(kts[a], kts[a] + c))
                loads.append((src[r:r + c * 128, :], c, ncols))
                for b in range(0, c, 2):
                    d = min(2, c - b)
                    subs.append((len(loads) - 1, b, d, j, a + b, a + b + d == n, b + d == c))

        def ada(col0, two, fin, need=()):
            j = dict(kind="ada", two=two, fin=fin, col0=col0, need=need)
            for a in range(0, 16, 4):
                loads.append((I["w_ada_2"][0, a * 128:(a + 4) * 128, col0:col0 + 512], 4, 512))
                subs.append((len(loads) - 1, 0, 4, j, a, a == 12, True))

        emitted_loads = [0]

        def emit_load():
            l = emitted_loads[0]
            if l >= len(loads):
                return
            src, c, n = loads[l]
            s = l % NRAW
            raw_tok[l] = Q.dma("S", raw[:, s, 0:c, 0:n], src.rearrange("(k p) n -> p k n", p=128),
                               rawslot[s], raw_free[s])
            emitted_loads[0] += 1

        adafree = [None]
        brow_slot = slot()

        def emit_split(i):
            l, b, d, j, k0, last, lastofload = subs[i]
            s = l % NRAW
            n = loads[l][2]
            if j["kind"] == "mm":
                u = split_no[i] % NSPL
                h = whi[:, u, 0:d, 0:n]
                lo = wlo[:, u, 0:d, 0:n]
                r = raw[:, s, b:b + d, 0:n]
                ta = copyA(h, r, raw_tok[l], spl_free[u])
                tv = tt(lo, r, f32(h), ALU.subtract, ta, raw_tok[l], spl_free[u])
                split_tok[i] = [ta, tv]
                if lastofload:
                    raw_free[s] = [ta, tv]
            else:
                if k0 == 0:
                    drain_need(j["need"])
                    j["brow"] = Q.dma("G", brow[0:1, :], I["b_ada_2"][0:1, j["col0"]:j["col0"] + 512],
                                      brow_slot, adafree[0])
                prev = j.get("acc", adafree[0])
                for k in range(4):
                    toks = []
                    for m in range(2 if j["two"] else 1):
                        a = acc[:, m, :]
                        r = raw[:, s, k, 0:n]
                        c = silc[:, m, k0 + k:k0 + k + 1]
                        if k0 + k == 0:
                            toks.append(ts1(a, r, c, ALU.mult, raw_tok[l], prev, ready["silc"]))
                        else:
                            toks.append(stt(a, r, c, a, ALU.mult, ALU.add, raw_tok[l], prev))
                    prev = toks
                j["acc"] = prev
                raw_free[s] = prev
                if last:
                    adapend.append(j)
                    adafree[0] = "open"
            if lastofload:
                emit_load()

        adapend = []

        def ada_side():
            while True:
                if not adapend:
                    yield False
                    continue
                j = adapend.pop(0)
                yield True
                yield from j["fin"](j)

        def ada_cols(row):
            def fin(j):
                b = yield from take()
                n = 2 if j["two"] else 1
                blk = (j["col0"] % 2048) // 128
                first = True
                for m in range(n):
                    for q in range(4):
                        d = banks[b][:, 4 * m + q:4 * m + q + 1]
                        mm(d, acc[:, m, q * 128:(q + 1) * 128], ones[:, 0:1], True, False,
                           j["acc"], sidefree[b] if first else None, ready["ones"], j["brow"])
                        t = mm(d, brow[0:1, q * 128:(q + 1) * 128], ones[0:1, 0:1], False, True, sig=True)
                        first = False
                adafree[0] = t
                yield True
                toks = []
                for m in range(n):
                    toks.append(copyV(mod[:, row[m], blk:blk + 4], banks[b][:, 4 * m:4 * m + 4], t))
                give(b, toks[-1])
                ready[("mod", row[0], blk // 4)] = toks
                yield True
            return fin

        def ada_rows(dst, key, war, after=()):
            def fin(j):
                while any(k not in ready for k in after):
                    yield False
                b = yield from take()
                mm(banks[b][:, :], ones[:, :], acc[:, 0, :], True, False, j["acc"], sidefree[b], ready["ones"], j["brow"])
                t = mm(banks[b][:, :], ones[0:1, :], brow[0:1, :], False, True, sig=True)
                adafree[0] = t
                yield True
                tv = copyV(dst, banks[b][:, :], t, war() if war else None)
                give(b, tv)
                ready[key] = tv
                yield True
            return fin

        split_no = {}
        split_tok = {}
        sides = []

        def step():
            for g in list(sides):
                try:
                    if next(g):
                        return True
                except StopIteration:
                    sides.remove(g)
                    return True
            return False

        def drain_need(keys):
            for k in keys:
                n = 0
                while k not in ready:
                    if not step():
                        n += 1
                        if n > 3:
                            raise RuntimeError(f"nothing can bring {k}")

        def toks_of(keys):
            return [ready[k] for k in keys if not isinstance(ready[k], bool)]

        def pe_sub(i):
            l, b, d, j, k0, last, _ = subs[i]
            if j["kind"] != "mm":
                return
            n = j["ncols"]
            if k0 == 0:
                drain_need(j["need"])
                Q.wait("P", toks_of(j["need"]))
                j["banks"] = {}
                for tb in j["tbs"]:
                    m = main_next[0] % NMAIN
                    main_next[0] += 1
                    j["banks"][tb] = m
                    Q.wait("P", main_free[m])
            u = split_no[i] % NSPL
            Q.wait("P", split_tok[i])
            t = None
            ntb = len(j["tbs"])
            for kk in range(d):
                kt = j["kts"][k0 + kk]
                if kt in j["ktneed"]:
                    drain_need((j["ktneed"][kt],))
                    Q.wait("P", ready[j["ktneed"][kt]])
                for x, tb in enumerate(j["tbs"]):
                    hi, lo = j["stat"](kt, tb)
                    dst = banks[j["banks"][tb]][:, 0:n]
                    H, L = whi[:, u, kk, 0:n], wlo[:, u, kk, 0:n]
                    s = k0 + kk == 0
                    e = last and kk == d - 1
                    mm(dst, hi, H, s, False)
                    mm(dst, hi, L, False, False)
                    t = mm(dst, lo, H, False, e, sig=e or (kk == d - 1 and x == ntb - 1))
                    if e:
                        j.setdefault("done", {})[tb] = t
            spl_free[u] = t
            if last:
                drain_need(j["evneed"])
                for tb in j["tbs"]:
                    m = j["banks"][tb]
                    main_free[m] = j["evac"](tb, banks[m][:, 0:n], j["done"][tb])

        def main():
            k = 0
            for i, s in enumerate(subs):
                if s[3]["kind"] == "mm":
                    split_no[i] = k
                    k += 1
            for _ in range(NRAW):
                emit_load()
            done = 0
            for i in range(len(subs)):
                while done < len(subs):
                    if subs[done][3]["kind"] == "mm":
                        if split_no[done] > (split_no[i] if i in split_no else last_no) + LEAD:
                            break
                    elif done > i + 6:
                        break
                    elif subs[done][4] == 0 and adafree[0] == "open":
                        while adafree[0] == "open" and step():
                            pass
                        if adafree[0] == "open":
                            if done > i:
                                break
                            raise RuntimeError("a strip of w_ada waits for what comes after it")
                    emit_split(done)
                    done += 1
                if i in split_no:
                    last_no = split_no[i]
                    pe_sub(i)
                    step()
                    if len(subs[i][3]["tbs"]) > 2:
                        step()

        sgfree = [None, None]

        def ev_copy(dst, war=(), key=None, engine=None):
            def f(tb, ps, t):
                w = toks_of(war)
                eng = engine or ("A" if tb % 2 == 0 else "V")
                r = (copyA if eng == "A" else copyV)(dst(tb), ps, t, w)
                if key:
                    ready.setdefault(key + "_", []).append(r)
                    if len(ready[key + "_"]) == key_n[key]:
                        ready[key] = ready[key + "_"]
                return r
            return f

        key_n = {}

        def note(key, tok):
            ready.setdefault(key + "_", []).append(tok)
            if len(ready[key + "_"]) == key_n[key]:
                ready[key] = ready[key + "_"]

        def ev_sig(dst, mul, war=(), key=None):
            def f(tb, ps, t):
                n = ps.shape[1]
                g = sg[:, tb, 0:n]
                a = act(g, ps, ACT.Sigmoid, t, sgfree[tb])
                w = toks_of(war)
                if mul == "silu":
                    r = tt(dst(tb), g, ps, ALU.mult, a, w)
                elif mul == "glu":
                    r = tt(dst(tb), g, dst(tb), ALU.mult, a, w)
                else:
                    r0 = tt(g, g, ps, ALU.mult, a, w)
                    r = tt(dst(tb), g, dst(tb), ALU.mult, r0)
                sgfree[tb] = r
                if key:
                    note(key, r)
                return [a, r]
            return f

        t = V(lambda e: e.memset(ones[:, :], 1.0))
        ready["ones"] = t
        ready["half"] = V(lambda e: e.memset(mhalf[:, :], -0.5))
        t = G(lambda e: e.memset(ident[:, :], 0.0))
        ready["ident"] = G(lambda e: e.affine_select(out=ident[:, :], in_=ident[:, :], compare_op=ALU.not_equal,
                                                     fill=1.0, base=0, pattern=[[-1, 128]],
                                                     channel_multiplier=1), t)
        xn = at("xn", oMG, [128, 2, 2048])
        xh = at("xh", oFX, [128, 16, 256], F32R)
        xl = at("xl", oFX + 16 * KB, [128, 16, 256], F32R)
        xv = I["x"][0].rearrange("(b p) d -> p b d", p=128)
        sx = [slot() for _ in range(4)]
        tx = [Q.dma("S", xn[:, b, c * 1024:(c + 1) * 1024], xv[:, b, c * 1024:(c + 1) * 1024], sx[2 * b + c])
              for b in range(2) for c in range(2)]

        prow = at("prow", oSG, [128, 128])
        sp = slot()
        col = {}
        r = 0
        tp = None
        for name, src, n in (("c", I["c_2"].rearrange("a (r p) -> (a r) p", p=128), 16),
                             ("cc", I["c_ctx_2"].rearrange("(r p) -> r p", p=128), 16),
                             ("ga", I["g_attn_2"].rearrange("a (r p) -> (a r) p", p=128), 16),
                             ("gf", I["g_ffn_2"].rearrange("a (r p) -> (a r) p", p=128), 16),
                             ("cb", I["conv_b"].rearrange("a (r p) -> (a r) p", p=128), 8),
                             ("sb", I["sgu_b"][0], 8),
                             ("mq", I["mla_gq_2"].rearrange("a (r p) -> (a r) p", p=128), 4),
                             ("mk", I["mla_gkv_2"].rearrange("a (r p) -> (a r) p", p=128), 2)):
            tp = Q.dma("A", prow[r:r + n, :], src, sp, tp)
            col[name] = r
            r += n
        NPR = r
        cwn = at("cwn", oEX, [31, 1024])
        scw = slot()
        tcw = Q.dma("A", cwn[:, :], I["conv_w"][0], scw)
        swn = at("swn", oR2 + 16 * KB, [128, 8, 128])
        swT = at("swT", oSW, [128, 8, 128])
        ssw = slot()
        tsw = Q.dma("A", swn[:, :, :], I["sgu_w"][0].rearrange("h t s -> t h s"), ssw)
        for h in range(8):
            tsw = G(lambda e, h=h: e.affine_select(out=swn[:, h, :], in_=swn[:, h, :], compare_op=ALU.is_ge,
                                                   fill=0.0, base=0, pattern=[[-1, 128]],
                                                   channel_multiplier=1), tsw)
        bandt = at("bandt", oR1, [128, 16, 384])
        tband0 = G(lambda e: e.memset(bandt[:, :, :], NEG))
        ssk = slot()
        tsk = Q.dma("G", snk[:, :], I["attn_sinks"][0].partition_broadcast(128), ssk)
        relb = at("relb", oAC, [32, 16])
        relx = at("relx", oR2, [32, 16, 128])
        buck = at("buck", oAC + 512, [32, 128])
        srb = slot()
        trb = Q.dma("A", relb[:, :], I["rel_bias"], srb)
        trb = Q.dma("A", buck[:, :], I["k_bucket"], srb, trb)
        nat = at("nat", oFY, [64, 30, 128])
        tn0 = G(lambda e: e.memset(nat[:, :, :], 0.0))
        sna = slot()
        lrow = at("lrow", oFY + 15 * KB, [128, 4, 64])
        sl = [slot() for _ in range(4)]
        tlam = [Q.dma("A", lrow[:, i, :], I[n][0].partition_broadcast(128), sl[i])
                for i, n in enumerate(("diff_lq1_2", "diff_lk1_2", "diff_lq2_2", "diff_lk2_2"))]
        rpb = I["na_rpb_2"][0].rearrange("h m x -> (h m) x")
        tn = None
        sna2 = slot()
        P60 = 60 * 128
        sv = scr_na.rearrange("(c x) -> c x", x=P60)
        for hh in range(2):
            tn = Q.dma("G", nat[:, :, 48:79], rpb[30 * hh:30 * hh + 30, :].partition_broadcast(64), sna, tn0, tn)
            tn = Q.dma("G", sv[:, hh * 3840:hh * 3840 + 3840], nat[:, :, :].rearrange("p a b -> p (a b)"), sna2, tn)
        ready["scr_na"] = tn

        def start_side():
            toks = []
            for kp in range(8):
                b = yield from take()
                for k in range(2):
                    for tb in range(2):
                        kt = 2 * kp + k
                        t = tr(banks[b][:, (2 * k + tb) * 128:(2 * k + tb + 1) * 128], xn[:, tb, kt * 128:(kt + 1) * 128],
                               tx, ready["ident"], sidefree[b], sig=(k == 1 and tb == 1))
                h = xh[:, 2 * kp:2 * kp + 2, :].rearrange("p a b -> p (a b)")
                l = xl[:, 2 * kp:2 * kp + 2, :].rearrange("p a b -> p (a b)")
                ta = copyA(h, banks[b][:, :], t)
                tv = tt(l, banks[b][:, :], f32(h), ALU.subtract, ta)
                toks += [ta, tv]
                give(b, tv)
            ready["xT"] = toks
            ready["xn_free"] = t
            yield True

        def start_side2():
            b = yield from take()
            t = tr(banks[b][:, 0:NPR], prow[0:NPR, :], tp, ready["ident"], sidefree[b], sig=True)
            yield True
            tv = copyV(par[:, 0:NPR], banks[b][:, 0:NPR], t)
            sgfree[0] = sgfree[1] = tv
            give(b, tv)
            ready["par"] = tv
            a = act(silc[:, :, :].rearrange("p a b -> p (a b)"), par[:, 0:32], ACT.Sigmoid, tv)
            ready["silc"] = tt(silc[:, :, :].rearrange("p a b -> p (a b)"),
                               silc[:, :, :].rearrange("p a b -> p (a b)"), par[:, 0:32], ALU.mult, a)
            lv = lrow[:, :, :].rearrange("p (a b) d -> p a b d", b=2)
            t = tt(lv[:, :, 0, :], lv[:, :, 0, :], lv[:, :, 1, :], ALU.mult, tlam)
            t = V(lambda e: e.tensor_reduce(lamt[:, 0:2], lv[:, :, 0, :], AX, ALU.add), t)
            t = act(lamt[:, 2:4], lamt[:, 0:2], ACT.Exp, t)
            t = tt(lamt[:, 4:5], lamt[:, 3:4], lamt[:, 2:3], ALU.subtract, t)
            ready["lam"] = ts1(lamt[:, 0:1], lamt[:, 4:5], LAM0, ALU.subtract, t)
            for g in range(2):
                b = yield from take()
                for h in range(4):
                    t = tr(banks[b][:, h * 128:(h + 1) * 128], swn[:, 4 * g + h, :], tsw, sidefree[b], sig=h == 3)
                yield True
                tv = copyA(swT[:, 4 * g:4 * g + 4, :].rearrange("p a b -> p (a b)"), banks[b][:, :], t)
                give(b, tv)
            ready["swT"] = tv
            ready["swn_free"] = t
            b = yield from take()
            for f in range(8):
                t = tr(banks[b][:, f * 31:(f + 1) * 31], cwn[:, f * 128:(f + 1) * 128], tcw, sidefree[b], sig=f == 7)
            yield True
            tv = copyV(cw[:, :, :].rearrange("p a b -> p (a b)"), banks[b][:, 0:248], t)
            give(b, tv)
            ready["cw"] = tv
            ready["ex_free"] = t
            tv = copyV(relx[:, :, :], relb[:, :].unsqueeze(2).broadcast_to([32, 16, 128]), trb)
            yield True
            toks = []
            for g in range(4):
                b = yield from take()
                for h in range(4):
                    t = mm(banks[b][:, h * 128:(h + 1) * 128], relx[:, 4 * g + h, :], buck[:, :], True, True,
                           tv, sidefree[b], sig=h == 3)
                yield True
                ta = copyV(bandt[:, 4 * g:4 * g + 4, 128:256], banks[b][:, :].rearrange("p (h d) -> p h d", h=4),
                           t, tband0)
                give(b, ta)
                toks.append(ta)
            ready["relx_free"] = t
            adafree[0] = t
            sb = slot()
            ready["scr_band"] = Q.dma("G", scr_band.rearrange("(p x) -> p x", x=6144),
                                      bandt[:, :, :].rearrange("p a b -> p (a b)"), sb, toks)
            ready["r1_free0"] = ready["scr_band"]
            yield True

        sides.append(start_side())
        sides.append(start_side2())
        sides.append(ada_side())

        W1 = I["w_in"][0]

        def stx(kt, tb):
            return (xh[:, kt, tb * 128:(tb + 1) * 128], xl[:, kt, tb * 128:(tb + 1) * 128])

        def win(c0, n, evac, need=("xT",)):
            gemm(W1[:, c0:c0 + n], list(range(16)), n, stx, (0, 1), evac, need)

        merged = at("merged", oMG, [128, 2, 2048])
        yh = at("yh", oFY, [128, 8, 256], F32R)
        yl = at("yl", oFY + 8 * KB, [128, 8, 256], F32R)
        exb = at("exb", oEX, [128, 1024])
        ext = [None]
        sex = slot()

        def load_ex(src, *w):
            ext[0] = Q.dma("G", exb[:, :], src.partition_broadcast(128), sex, ready["ex_free"], *w)
            return ext[0]

        def to_yT(src, key, toks, need):
            while need and need not in ready:
                yield False
            w = ready[need] if need else None
            out_ = []
            for kp in range(4):
                b = yield from take()
                for k in range(2):
                    for tb in range(2):
                        kt = 2 * kp + k
                        t = tr(banks[b][:, (2 * k + tb) * 128:(2 * k + tb + 1) * 128],
                               src(tb)[:, kt * 128:(kt + 1) * 128], toks, sidefree[b], sig=(k == 1 and tb == 1))
                yield True
                h = yh[:, 2 * kp:2 * kp + 2, :].rearrange("p a b -> p (a b)")
                l = yl[:, 2 * kp:2 * kp + 2, :].rearrange("p a b -> p (a b)")
                ta = copyA(h, banks[b][:, :], t, w)
                tv = tt(l, banks[b][:, :], f32(h), ALU.subtract, ta, w)
                out_ += [ta, tv]
                give(b, tv)
                yield True
            ready[key] = out_
            ready[key + "_src"] = t

        a_in = at("a_in", oR1, [128, 2, 1024])
        a_gt = at("a_gt", oR1 + 8 * KB, [128, 2, 1024])
        pgw = at("pgw", oR1 + 16 * KB, [128, 4, 2, 256])
        pm = at("pm", oMG, [128, 2, 4, 256])
        mixT = at("mixT", oMG + 8 * KB, [128, 8, 256])
        key_n.update(a_in=4, a_gt=4)
        for s in range(2):
            win(512 * s, 512, ev_copy(lambda tb, s=s: a_in[:, tb, 512 * s:512 * s + 512], ("r1_free0",), "a_in"),
                ("xT", "r1_free0"))
        for s in range(2):
            win(1024 + 512 * s, 512, ev_sig(lambda tb, s=s: a_gt[:, tb, 512 * s:512 * s + 512], "silu",
                                            ("r1_free0",), "a_gt"))

        def side_a():
            spm, spg = slot(), slot()
            while "xn_free" not in ready or "r1_free0" not in ready:
                yield False
            t1 = Q.dma("G", pm[:, :, :, :].rearrange("p k g t -> p k (g t)"),
                       I["k_pool"].rearrange("(k p) g t -> p k (g t)", p=128), spm, ready["xn_free"])
            t2 = Q.dma("G", pgw[:, :, :, :].rearrange("p g k n -> p (g k) n"),
                       I["pool_w"][0].rearrange("g (k p) n -> p (g k) n", p=128), spg, ready["r1_free0"])
            yield True
            while "a_in" not in ready:
                yield False
            toks = []
            for fp in range(4):
                b = yield from take()
                for f in range(2):
                    fb = 2 * fp + f
                    for k in range(2):
                        t = mm(banks[b][:, f * 256:(f + 1) * 256], a_in[:, k, fb * 128:(fb + 1) * 128],
                               pm[:, k, fb // 2, :], k == 0, k == 1, ready["a_in"], t1, sidefree[b],
                               sig=(f == 1 and k == 1))
                yield True
                tv = copyV(mixT[:, 2 * fp:2 * fp + 2, :].rearrange("p a b -> p (a b)"), banks[b][:, :], t)
                toks.append(tv)
                give(b, tv)
                yield True
            te = load_ex(I["pool_scale"][0])
            while "a_gt" not in ready:
                yield False
            rr = []
            for tb in range(2):
                for gp in range(2):
                    b = yield from take()
                    for g in range(2):
                        for k in range(2):
                            gg = 2 * gp + g
                            t = mm(banks[b][:, g * 256:(g + 1) * 256],
                                   mixT[:, 2 * gg + k, tb * 128:(tb + 1) * 128], pgw[:, gg, k, :], k == 0, k == 1,
                                   toks, t2, sidefree[b], sig=(g == 1 and k == 1))
                    yield True
                    d = a_in[:, tb, gp * 512:(gp + 1) * 512]
                    e = a_gt[:, tb, gp * 512:(gp + 1) * 512]
                    tv = tt(d, banks[b][:, :], exb[:, gp * 512:(gp + 1) * 512], ALU.mult, t, te)
                    give(b, tv)
                    rr.append(tt(d, d, e, ALU.mult, tv, ready["a_gt"]))
                    yield True
            ready["ex_free"] = rr[-1]
            ready["mg_free"] = t
            yield from to_yT(lambda tb: a_in[:, tb, :], "yA", rr, None)

        v_n = at("v_n", oR2, [128, 2, 1024])
        u_n = at("u_n", oR2 + 8 * KB, [128, 2, 1024])
        key_n.update(v_n=4, u_n=4, u_g=4)

        def layer_norm(x, n, tok, eps, ga, ba):
            toks = []
            for c in range(n // 512):
                toks.append(V(lambda e, c=c: e.bn_stats(st[:, c, :], x[:, c * 512:(c + 1) * 512]), tok, stfree[0]))
            t = V(lambda e: e.bn_aggr(mv[:, :], st[:, 0:n // 512, :].rearrange("p a b -> p (a b)")), toks)
            t = rstd(rs[:, 0:1], mv[:, 1:2], 1.0, eps, t)
            t = ts(x, x, mv[:, 0:1], rs[:, 0:1], ALU.subtract, ALU.mult, t)
            stfree[0] = t
            return t

        stfree = [None]

        def ln_ex(xs, tok, g_src, b_src):
            tg = load_ex(g_src)
            yield True
            ts_ = []
            for tb in range(2):
                ts_.append(layer_norm(xs(tb), 1024, tok, EPS_LN, None, None))
                yield True
            t2 = [tt(xs(tb), xs(tb), exb[:, :], ALU.mult, ts_, tg) for tb in range(2)]
            ready["ex_free"] = t2[-1]
            yield True
            tb_ = load_ex(b_src)
            yield True
            yield True
            t3 = [tt(xs(tb), xs(tb), exb[:, :], ALU.add, t2, tb_) for tb in range(2)]
            ready["ex_free"] = t3[-1]
            yield True
            return t3

        for s in range(2):
            win(3072 + 512 * s, 512, ev_copy(lambda tb, s=s: v_n[:, tb, 512 * s:512 * s + 512],
                                             ("relx_free", "swn_free"), "v_n"), ("relx_free", "swn_free"))
        for s in range(2):
            win(2048 + 512 * s, 512, ev_copy(lambda tb, s=s: u_n[:, tb, 512 * s:512 * s + 512],
                                             ("relx_free", "swn_free"), "u_n"))
        for s in range(2):
            win(4096 + 512 * s, 512, ev_sig(lambda tb, s=s: u_n[:, tb, 512 * s:512 * s + 512], "silumul",
                                            ("u_n",), "u_g"))

        def side_b():
            while "v_n" not in ready or "yA" not in ready:
                yield False
            tn_ = yield from ln_ex(lambda tb: v_n[:, tb, :], ready["v_n"], I["sgu_ln_g"][0], I["sgu_ln_b"][0])
            res = []
            while "u_g" not in ready:
                yield False
            for tb in range(2):
                for hp in range(2):
                    b = yield from take()
                    for h in range(4):
                        hh = 4 * hp + h
                        t = mm(banks[b][:, h * 128:(h + 1) * 128], swT[:, hh, :],
                               v_n[:, tb, hh * 128:(hh + 1) * 128], True, True,
                               tn_, ready["swT"], sidefree[b], sig=h == 3)
                    yield True
                    for h in range(4):
                        hh = 4 * hp + h
                        u = u_n[:, tb, hh * 128:(hh + 1) * 128]
                        tv = stt(u, banks[b][:, h * 128:(h + 1) * 128], par[:, col["sb"] + hh:col["sb"] + hh + 1],
                                 u, ALU.add, ALU.mult, t, ready["u_g"], ready["par"])
                    res.append(tv)
                    give(b, tv)
                    yield True
            ready["swT_free"] = t
            yield from to_yT(lambda tb: u_n[:, tb, :], "yB", res, "mA")

        def merge(i, key, extra=()):
            key_n["m" + key] = 8
            ready_g = {}

            def sty(kt, tb):
                return (yh[:, kt, tb * 128:(tb + 1) * 128], yl[:, kt, tb * 128:(tb + 1) * 128])

            for n in range(4):
                def evg(tb, ps, t):
                    a = act(sg[:, tb, :], ps, ACT.Sigmoid, t, sgfree[tb])
                    sgfree[tb] = a
                    ready_g[tb] = a
                    return a

                def evb(tb, ps, t, n=n):
                    d = merged[:, tb, n * 512:(n + 1) * 512]
                    if i == 0:
                        r = tt(d, sg[:, tb, :], ps, ALU.mult, t, ready_g[tb], ready["mg_free"])
                    else:
                        r0 = tt(sg[:, tb, :], sg[:, tb, :], ps, ALU.mult, t, ready_g[tb])
                        r = tt(d, d, sg[:, tb, :], ALU.add, r0, ready.get(("mer", n, tb)))
                    ready[("mer", n, tb)] = r
                    sgfree[tb] = r
                    note("m" + key, [r, t])
                    return r

                win(10496 + 2048 * i + 512 * n, 512, evg)
                gemm(I["w_branch"][0, i, :, n * 512:(n + 1) * 512], list(range(8)), 512, sty, (0, 1), evb,
                     ("y" + key, "mg_free"))

        def ada_two(ch, n, rows):
            ada(2048 * ch + 512 * n, True, ada_cols(rows), ("silc", "relx_free"))

        sides.append(side_a())
        merge(0, "A")
        sides.append(side_b())

        d_n = at("d_n", oR1, [128, 2, 1024])
        glT = at("glT", oR1 + 8 * KB, [128, 8, 286])
        d_o = at("d_o", oR1, [128, 8, 256])
        d_y = at("d_y", oR1 + 8 * KB, [128, 2, 1024])
        d_g = at("d_g", oR1 + 8 * KB + 9152, [128, 2, 1024])
        key_n.update(d_v=4, d_n=4, d_g=4)
        for s in range(2):
            win(7424 + 512 * s, 512, ev_copy(lambda tb, s=s: d_n[:, tb, 512 * s:512 * s + 512], ("yA_src",), "d_v"),
                ("yA_src", "xT"))
        for s in range(2):
            win(8448 + 512 * s, 512, ev_sig(lambda tb, s=s: d_n[:, tb, 512 * s:512 * s + 512], "glu", ("d_v",), "d_n"))
        for s in range(2):
            win(9472 + 512 * s, 512, ev_sig(lambda tb, s=s: d_g[:, tb, 512 * s:512 * s + 512], "silu", ("yA_src",), "d_g"))
        ada_two(0, 0, (0, 2))

        def side_d():
            while "d_n" not in ready or "yB" not in ready or "cw" not in ready or "yA_src" not in ready:
                yield False
            t0 = V(lambda e: e.memset(glT[:, :, 0:30], 0.0), ready["yA_src"])
            tg_ = []
            for f in range(8):
                b = yield from take()
                for tb in range(2):
                    t = tr(banks[b][:, tb * 128:(tb + 1) * 128], d_n[:, tb, f * 128:(f + 1) * 128],
                           ready["d_n"], sidefree[b], sig=tb == 1)
                yield True
                tv = copyA(glT[:, f, 30:286], banks[b][:, 0:256], t)
                give(b, tv)
                tg_.append(tv)
            yield True
            prev = [None] * 8
            for k in range(31):
                for f in range(8):
                    w = cw[:, f, k:k + 1]
                    if k == 0:
                        prev[f] = ts1(d_o[:, f, :], glT[:, f, k:k + 256], w, ALU.mult, tg_, t0, ready["cw"], t)
                    else:
                        prev[f] = stt(d_o[:, f, :], glT[:, f, k:k + 256], w, d_o[:, f, :], ALU.mult, ALU.add, prev[f])
                    if f % 4 == 3:
                        yield True
            ready["cw_free"] = list(prev)
            for f in range(8):
                prev[f] = ts1(d_o[:, f, :], d_o[:, f, :], par[:, col["cb"] + f:col["cb"] + f + 1], ALU.add, prev[f])
            yield True
            ty = []
            for tb in range(2):
                for fp in range(2):
                    b = yield from take()
                    for f in range(4):
                        t = tr(banks[b][:, f * 128:(f + 1) * 128], d_o[:, 4 * fp + f, tb * 128:(tb + 1) * 128],
                               prev, sidefree[b], sig=f == 3)
                    yield True
                    tv = copyA(d_y[:, tb, fp * 512:(fp + 1) * 512], banks[b][:, :], t, prev)
                    give(b, tv)
                    ty.append(tv)
            t3 = yield from ln_ex(lambda tb: d_y[:, tb, :], ty, I["conv_ln_g"][0], I["conv_ln_b"][0])
            res = []
            for tb in range(2):
                for s in range(2):
                    y = d_y[:, tb, s * 512:(s + 1) * 512]
                    g = d_o[:, 4 * tb + 2 * s:4 * tb + 2 * s + 2, :].rearrange("p a b -> p (a b)")
                    a = act(g, y, ACT.Sigmoid, t3, t)
                    r = tt(y, y, g, ALU.mult, a)
                    r = tt(y, y, d_g[:, tb, s * 512:(s + 1) * 512], ALU.mult, r, ready["d_g"])
                    res.append(r)
                    yield True
            yield from to_yT(lambda tb: d_y[:, tb, :], "yD", res, "mB")

        sides.append(side_d())
        merge(1, "B")
        ada_two(0, 1, (0, 2))

        q_n = at("q_n", oR2, [128, 2, 8, 128])
        c_g = at("c_g", oR2 + 8 * KB, [128, 2, 1024])
        kd = at("kd", oR2 + 16 * KB, [128, 2, 2, 2, 64])
        vv = at("vv", oR2 + 18 * KB, [128, 2, 128])
        key_n.update(c_kv=2, c_q=4, c_g=4)

        def ev_kv(tb, ps, t):
            k = ps[:, 0:128].rearrange("p (k d) -> p k d", k=2)
            w = ready["yB_src"]
            a = copyA(kd[:, tb, :, 0, :], k, t, w)
            a = copyA(kd[:, tb, :, 1, :], k, t, w)
            a = copyA(vv[:, tb, :], ps[:, 128:256], t, w)
            note("c_kv", a)
            return a

        win(6144, 256, ev_kv, ("yB_src",))
        for s in range(2):
            win(5120 + 512 * s, 512, ev_copy(
                lambda tb, s=s: q_n[:, tb, 4 * s:4 * s + 4, :].rearrange("p a b -> p (a b)"), ("yB_src",), "c_q"))
        for s in range(2):
            win(6400 + 512 * s, 512, ev_sig(lambda tb, s=s: c_g[:, tb, 512 * s:512 * s + 512], "silu", ("yB_src",), "c_g"))
        ada_two(0, 2, (0, 2))

        band = at("band", oR1, [128, 16, 256])
        pb1 = at("pb1", oR1 + 16 * KB, [128, 4, 384])
        pt1 = at("pt1", oR1 + 22 * KB, [128, 2, 384])

        def side_c():
            while "c_q" not in ready or "c_kv" not in ready or "yD" not in ready or "scr_band" not in ready:
                yield False
            sband = slot()
            src = bass.AP(tensor=scr_band.tensor, offset=127, ap=[[6143, 128], [384, 16], [1, 256]])
            tb_ = Q.dma("G", band[:, :, :], src, sband, ready["scr_band"], ready["yD_src"])
            tt_ = []
            for fb in range(10):
                b = yield from take()
                for tb in range(2):
                    s = q_n[:, tb, fb, :] if fb < 8 else kd[:, tb, fb - 8, :, :].rearrange("p a b -> p (a b)")
                    t = tr(banks[b][:, tb * 128:(tb + 1) * 128], s, ready["c_q"], ready["c_kv"], sidefree[b],
                           sig=tb == 1)
                yield True
                dst = q_n[:, :, fb, :] if fb < 8 else kd[:, :, fb - 8, :, :].rearrange("p t a b -> p t (a b)")
                tv = copyA(dst, banks[b][:, 0:256].rearrange("p (t c) -> p t c", t=2), t)
                give(b, tv)
                tt_.append(tv)
                yield True
            res = []
            pfree = None
            ptfree = [None, None]
            for g in range(4):
                tl = []
                for hh in range(4):
                    h = 4 * g + hh
                    kv, fb, off = h // 8, h // 2, (h % 2) * 64
                    b = yield from take()
                    mm(banks[b][:, 0:128], q_n[off:off + 64, 0, fb, :],
                       kd[off:off + 64, 0, kv, :, :].rearrange("p a b -> p (a b)"), True, True, tt_, sidefree[b])
                    t = mm(banks[b][:, 128:384], q_n[off:off + 64, 1, fb, :],
                           kd[off:off + 64, :, kv, :, :].rearrange("p t a b -> p t (a b)"), True, True, sig=True)
                    yield True
                    tl.append(stt(pb1[:, hh, 0:128], banks[b][:, 0:128], 0.125, band[:, h, 128:256],
                                  ALU.mult, ALU.add, t, tb_, pfree, ready["yD_src"]))
                    tv = stt(pb1[:, hh, 128:384], banks[b][:, 128:384], 0.125, band[:, h, :],
                             ALU.mult, ALU.add, t, tb_, pfree)
                    tl.append(tv)
                    give(b, tv)
                m = smx[:, 0, :].rearrange("p (b h) -> p b h", b=2)
                t1 = V(lambda e: e.tensor_reduce(m[:, 0, :], pb1[:, :, 0:128], AX, ALU.max), tl, pfree)
                t2 = V(lambda e: e.tensor_reduce(m[:, 1, :], pb1[:, :, 128:384], AX, ALU.max), tl)
                sk = snk[:, 4 * g:4 * g + 4].unsqueeze(1).broadcast_to([128, 2, 4])
                t3 = tt(m, m, sk, ALU.max, t1, t2, tsk)
                t4 = ts1(smx[:, 1, :], smx[:, 0, :], -1.0, ALU.mult, t3)
                t5 = tt(smx[:, 3, :].rearrange("p (b h) -> p b h", b=2), sk, m, ALU.subtract, t3)
                yield True
                te = []
                for bq in range(2):
                    for hh in range(4):
                        p = pb1[:, hh, 0:128] if bq == 0 else pb1[:, hh, 128:384]
                        n = 4 * bq + hh
                        te.append(act(p, p, ACT.Exp, t4, bias=smx[:, 1, n:n + 1], scale=1.0,
                                      accum_out=smx[:, 2, n:n + 1]))
                te.append(act(smx[:, 3, :], smx[:, 3, :], ACT.Exp, t5))
                t6 = tt(smx[:, 2, :], smx[:, 2, :], smx[:, 3, :], ALU.add, te)
                t7 = V(lambda e: e.reciprocal(smx[:, 4, :], smx[:, 2, :]), t6)
                yield True
                bo = yield from take()
                for hh in range(4):
                    h = 4 * g + hh
                    kv = h // 8
                    b = yield from take()
                    for c in range(3):
                        t = tr(banks[b][:, c * 128:(c + 1) * 128], pb1[:, hh, c * 128:(c + 1) * 128], te,
                               sidefree[b], sig=c == 2)
                    yield True
                    s = h % 2
                    ta = copyA(pt1[:, s, :], banks[b][:, 0:384], t, ptfree[s])
                    give(b, ta)
                    yield True
                    vk = slice(kv * 64, kv * 64 + 64)
                    mm(banks[bo][:, hh * 64:hh * 64 + 64], pt1[:, s, 0:128], vv[:, 0, vk], True, True, ta,
                       sidefree[bo], ready["c_kv"])
                    mm(banks[bo][:, 256 + hh * 64:256 + hh * 64 + 64], pt1[:, s, 128:256], vv[:, 0, vk], True, False)
                    t = mm(banks[bo][:, 256 + hh * 64:256 + hh * 64 + 64], pt1[:, s, 256:384], vv[:, 1, vk],
                           False, True, sig=True)
                    ptfree[s] = t
                yield True
                pfree = t
                while "c_g" not in ready:
                    yield False
                for bq in range(2):
                    ob = banks[bo][:, 256 * bq:256 * bq + 256].rearrange("p (h d) -> p h d", h=4)
                    ri = smx[:, 4, 4 * bq:4 * bq + 4].unsqueeze(2).broadcast_to([128, 4, 64])
                    od = pb1[:, bq, 0:256].rearrange("p (h d) -> p h d", h=4)
                    tv = tt(od, ob, ri, ALU.mult, t, t7)
                    cg = c_g[:, bq, 256 * g:256 * g + 256]
                    r = tt(cg, cg, pb1[:, bq, 0:256], ALU.mult, tv, ready["c_g"])
                    res.append(r)
                give(bo, tv)
                pfree = r
                yield True
            yield from to_yT(lambda tb: c_g[:, tb, :], "yC", res, "mD")

        sides.append(side_c())
        merge(3, "D")
        ada_two(0, 3, (0, 2))
        merge(2, "C")
        for n in range(4):
            ada_two(1, n, (1, 3))

        mh = at("mh", oFX, [128, 16, 256], F32R)
        ml = at("ml", oFX + 16 * KB, [128, 16, 256], F32R)
        x1 = at("x1", oR1, [128, 2, 2048])
        lnr = at("lnr", oR2, [128, 2, 2048])

        def side_m():
            while "mC" not in ready:
                yield False
            toks = []
            w = ready["mC"]
            for kp in range(8):
                b = yield from take()
                for k in range(2):
                    for tb in range(2):
                        kt = 2 * kp + k
                        t = tr(banks[b][:, (2 * k + tb) * 128:(2 * k + tb + 1) * 128],
                               merged[:, tb, kt * 128:(kt + 1) * 128], w, sidefree[b], sig=(k == 1 and tb == 1))
                h = mh[:, 2 * kp:2 * kp + 2, :].rearrange("p a b -> p (a b)")
                l = ml[:, 2 * kp:2 * kp + 2, :].rearrange("p a b -> p (a b)")
                ta = copyA(h, banks[b][:, :], t)
                tv = tt(l, banks[b][:, :], f32(h), ALU.subtract, ta)
                toks += [ta, tv]
                give(b, tv)
            ready["mT"] = toks
            ready["merged_free"] = t
            yield True

        def side_x():
            while "yC_src" not in ready:
                yield False
            s = slot()
            ready["x_again"] = Q.dma("G", x1[:, :, :], xv, s, ready["yC_src"])
            yield True

        sides.append(side_x())
        sides.append(side_m())

        def stm(kt, tb):
            return (mh[:, kt, tb * 128:(tb + 1) * 128], ml[:, kt, tb * 128:(tb + 1) * 128])

        key_n["z"] = 8
        for n in range(4):
            def evz(tb, ps, t, n=n):
                d = x1[:, tb, n * 512:(n + 1) * 512]
                r = stt(d, d, ALPHA, ps, ALU.mult, ALU.add, t, ready["x_again"])
                note("z", [r, t])
                return r
            gemm(I["w_out"][0, :, n * 512:(n + 1) * 512], list(range(16)), 512, stm, (0, 1), evz, ("mT", "x_again"))

        mod_keys = [("mod", 0, n) for n in range(4)] + [("mod", 1, n) for n in range(4)]

        def to_hT(src, tok, Ac, Bc, hi, lo, tbs, war):
            toks = []
            nb = len(tbs)
            for kp in range(8):
                b = yield from take()
                for k in range(2):
                    for x, tb in enumerate(tbs):
                        kt = 2 * kp + k
                        t = tr(banks[b][:, (nb * k + x) * 128:(nb * k + x + 1) * 128],
                               src(tb)[:, kt * 128:(kt + 1) * 128], tok, sidefree[b], sig=(k == 1 and x == nb - 1))
                w = nb * 128
                g = kp % 2
                for k in range(2):
                    kt = 2 * kp + k
                    tv = ts(sg[:, g, k * w:(k + 1) * w], banks[b][:, k * w:(k + 1) * w], Ac[:, kt:kt + 1],
                            Bc[:, kt:kt + 1], ALU.mult, ALU.add, t, sgfree[g])
                give(b, tv)
                s = sg[:, g, 0:2 * w].rearrange("p (k c) -> p k c", k=2)
                h = hi[:, 2 * kp:2 * kp + 2, tbs[0] * 128:tbs[0] * 128 + w]
                l = lo[:, 2 * kp:2 * kp + 2, tbs[0] * 128:tbs[0] * 128 + w]
                ta = copyA(h, s, tv, war)
                tl = tt(l, s, f32(h), ALU.subtract, ta, tv, war)
                sgfree[g] = tl
                toks += [ta, tl]
                yield True
            return toks, t

        hch = at("hch", oFY, [128, 16, 256], F32R)
        hcl = at("hcl", oFY + 16 * KB, [128, 16, 256], F32R)
        hxh, hxl = mh, ml
        acx = small("acx", [128, 2, 16])
        ctn = at("ctn", oR2, [128, 2048])
        sqt = at("sqt", oR2 + 8 * KB, [128, 2048])

        def side_hc():
            while "yC_src" not in ready or "merged_free" not in ready or "mC" not in ready \
                    or any(k not in ready for k in mod_keys):
                yield False
            tm = [ready[k] for k in mod_keys]
            ga = par[:, col["ga"]:col["ga"] + 16]
            a1 = stt(acx[:, 0, :], mod[:, 1, :], 1.0, ga, ALU.add, ALU.mult, tm, ready["ex_free"])
            a2 = stt(acx[:, 1, :], mod[:, 3, :], 1.0, ga, ALU.add, ALU.mult, tm, ready["ex_free"])
            ready["acx"] = [a1, a2]
            s = slot()
            free = ready["yC_src"]
            alltoks = []
            for tb in range(2):
                tc = Q.dma("G", ctn[:, :], I["ctx_2"][0, tb * 128:(tb + 1) * 128, :], s, free, alltoks)
                yield True
                yield True
                t = act(sqt[:, :], ctn[:, :], ACT.Square, tc, stfree[0], accum_out=rs[:, 1:2])
                t = rstd(rs[:, 2:3], rs[:, 1:2], 1.0 / 2048, EPS_RMS, t)
                t = ts1(ctn[:, :], ctn[:, :], rs[:, 2:3], ALU.mult, t)
                stfree[0] = t
                yield True
                tk, free = yield from to_hT(lambda _: ctn[:, :], t, acx[:, 1, :], mod[:, 2, :], hch, hcl, (tb,),
                                            [ready["merged_free"], ready["mC"], ready["acx"]])
                alltoks += tk
            ready["hc"] = alltoks
            ready["ctn_free"] = [free, t]

        def side_ln1():
            while "ctn_free" not in ready:
                yield False
            s1, s2 = slot(), slot()
            ready["lnr"] = [Q.dma("G", lnr[:, 0, :], I["ln_g"][0].partition_broadcast(128), s1, ready["ctn_free"]),
                            Q.dma("G", lnr[:, 1, :], I["ln_b"][0].partition_broadcast(128), s2, ready["ctn_free"])]
            yield True

        def side_x1():
            while "z" not in ready or "lnr" not in ready or "hc" not in ready:
                yield False
            tl = []
            for tb in range(2):
                x = x1[:, tb, :]
                t = layer_norm(x, 2048, ready["z"], EPS_LN, None, None)
                t = tt(x, x, lnr[:, 0, :], ALU.mult, t, ready["lnr"])
                t = tt(x, x, lnr[:, 1, :], ALU.add, t)
                tl.append(t)
            s = slot()
            td = Q.dma("G", scr_x1, x1[:, :, :], s, tl)
            ready["scr_x1"] = td
            tn_ = []
            for tb in range(2):
                t = act(lnr[:, tb, :], x1[:, tb, :], ACT.Square, tl, accum_out=rs[:, 4 + tb:5 + tb])
                t = rstd(rs[:, 6 + tb:7 + tb], rs[:, 4 + tb:5 + tb], 1.0 / 2048, EPS_RMS, t)
                tn_.append(ts1(lnr[:, tb, :], x1[:, tb, :], rs[:, 6 + tb:7 + tb], ALU.mult, t))
            tk, t = yield from to_hT(lambda tb: lnr[:, tb, :], tn_, acx[:, 0, :], mod[:, 0, :], hxh, hxl, (0, 1),
                                     [ready["z"], ready["acx"]])
            ready["x1_done"] = tk
            ready["hx"] = tk
            ready["r12_free"] = [t, tn_, td]

        sides.append(side_hc())
        sides.append(side_ln1())
        sides.append(side_x1())

        if stage == 1:
            main()
            drain_need(("hx",))
            so = slot()
            t = Q.dma("G", out[0].rearrange("(b p) d -> p b d", p=128), x1[:, :, :], so, ready["hx"])
            if dbg:
                for nm, ap in (("hx", hxh), ("hxl", hxl), ("hc", hch), ("hcl", hcl)):
                    t = [t, Q.dma("G", dbg[nm], f32(ap[:, :, :]), slot(), ready["hx"], ready["hc"])]
                t = [t, Q.dma("G", dbg["mod"], mod[:, 0:4, :], slot(), ready["hx"])]
            fin(nc, ctx, Q, t)
            return
        W2 = I["w_in_2"][0]

        def st2(kt, tb):
            if tb < 2:
                return (hxh[:, kt, tb * 128:(tb + 1) * 128], hxl[:, kt, tb * 128:(tb + 1) * 128])
            return (hch[:, kt, (tb - 2) * 128:(tb - 1) * 128], hcl[:, kt, (tb - 2) * 128:(tb - 1) * 128])

        def win2(c0, n, tbs, evac, need=("hx", "hc")):
            gemm(W2[:, c0:c0 + n], list(range(16)), n, st2, tbs, evac, need)

        XT, ALL = (0, 1), (0, 1, 2, 3)
        ot = at("ot", oSW, [128, 8, 256])
        nb_ = [at(f"nab{i}", oSW + (4 + 2 * i) * KB, [128, 2, 4, 64]) for i in range(2)]
        pp = at("pp", oR1 + 20 * KB, [128, 2, 512])
        rt = at("rt", oR1 + 24 * KB, [128, 512])
        pT = at("pT", oSG, [128, 4, 256])
        oh = at("oh", oFX, [128, 16, 256], F32R)
        ol = at("ol", oFX + 16 * KB, [128, 16, 256], F32R)

        M0, M1 = oR1, oR2
        na_q = at("na_q", M0, [128, 2, 4, 128])
        na_k = at("na_k", M0 + 4 * KB, [128, 4, 4, 128])
        na_v = at("na_v", M0 + 12 * KB, [128, 4, 512])
        gq_q = at("gq_q", M1, [128, 2, 4, 128])
        gq_kv = at("gq_kv", M1 + 4 * KB, [128, 4, 4, 128])
        ml_q = at("ml_q", M0, [128, 2, 512])
        ml_c = at("ml_c", M0 + 4 * KB, [128, 4, 320])
        cqh = at("cqh", M0 + 9 * KB, [128, 4, 256], F32R)
        cql = at("cql", M0 + 13 * KB, [128, 4, 256], F32R)
        ckh = at("ckh", M0, [128, 2, 512], F32R)
        ckl = at("ckl", M0 + 4 * KB, [128, 2, 512], F32R)
        kpT = at("kpT", M0 + 17 * KB, [64, 512])
        df_q = at("df_q", M1, [128, 2, 4, 128])
        df_k = at("df_k", M1 + 4 * KB, [128, 4, 4, 128])
        df_v = at("df_v", M1 + 12 * KB, [128, 4, 512])
        mq = at("mq", oFY, [128, 2, 768])
        mkv = at("mkv", oFY + 6 * KB, [128, 4, 1024])
        mqp = at("mqp", oFY + 22 * KB, [64, 4, 256])

        def flat(ap):
            return ap.rearrange("p a b -> p (a b)")

        def cp(view, key, n, war):
            key_n[key] = n
            return ev_copy(view, war, key)

        win2(0, 512, XT, cp(lambda tb: flat(na_q[:, tb, :, :]), "na_q", 2, ("r12_free",)))
        win2(512, 512, ALL, cp(lambda tb: flat(na_k[:, tb, :, :]), "na_k", 4, ("r12_free",)))
        win2(1024, 512, ALL, cp(lambda tb: na_v[:, tb, :], "na_v", 4, ("r12_free",)))
        win2(1536, 512, XT, cp(lambda tb: flat(gq_q[:, tb, :, :]), "gq_q", 2, ("r12_free",)))
        win2(2048, 512, ALL, cp(lambda tb: flat(gq_kv[:, tb, :, :]), "gq_kv", 4, ("r12_free",)))
        ada(2048 * 3, False, ada_cols((4,)), ("silc", "relx_free"))
        win2(2560, 512, XT, cp(lambda tb: ml_q[:, tb, :], "ml_q", 2, ("o_na",)), ("hx", "hc", "o_na"))
        ada(2048 * 3 + 512, False, ada_cols((4,)))
        win2(3072, 320, ALL, cp(lambda tb: ml_c[:, tb, :], "ml_c", 4, ("o_na",)))
        win2(3392, 512, XT, cp(lambda tb: flat(df_q[:, tb, :, :]), "df_q", 2, ("o_gq",)), ("o_gq",))
        ada(2048 * 3 + 1024, False, ada_cols((4,)))
        win2(3904, 512, ALL, cp(lambda tb: flat(df_k[:, tb, :, :]), "df_k", 4, ("o_gq",)))
        ada(2048 * 3 + 1536, False, ada_cols((4,)))
        win2(4416, 512, ALL, cp(lambda tb: df_v[:, tb, :], "df_v", 4, ("o_gq",)))

        def stq(kt, tb):
            return (cqh[:, kt, tb * 128:(tb + 1) * 128], cql[:, kt, tb * 128:(tb + 1) * 128])

        def stk(kt, tb):
            return (ckh[:, kt, tb * 128:(tb + 1) * 128], ckl[:, kt, tb * 128:(tb + 1) * 128])

        gemm(I["mla_wukv_2"][0][:, 0:512], [0, 1], 512, stk, ALL,
             cp(lambda tb: mkv[:, tb, 0:512], "mkv0", 4, ("df_v",)), ("ml_T", "df_v"))
        gemm(I["mla_wukv_2"][0][:, 512:1024], [0, 1], 512, stk, ALL,
             cp(lambda tb: mkv[:, tb, 512:1024], "mkv1", 4, ("df_v",)))
        gemm(I["mla_wuq_2"][0][:, 0:512], [0, 1, 2, 3], 512, stq, XT,
             cp(lambda tb: mq[:, tb, 0:512], "mq0", 2, ("df_v",)))
        gemm(I["mla_wuq_2"][0][:, 512:768], [0, 1, 2, 3], 256, stq, XT,
             cp(lambda tb: mq[:, tb, 512:768], "mq1", 2, ("df_v",)))

        def in_place(blocks, tok, rows=128):
            toks = []
            for src, dst in blocks:
                b = yield from take()
                n = len(src)
                for x, s in enumerate(src):
                    t = tr(banks[b][0:s.shape[1], x * 128:(x + 1) * 128], s, tok, sidefree[b], sig=x == n - 1)
                yield True
                r = src[0].shape[1]
                tv = copyA(dst, banks[b][0:r, 0:n * 128].rearrange("p (t c) -> p t c", t=n), t)
                give(b, tv)
                toks.append(tv)
            return toks

        rtfree = [None]

        def rope(x, cs, d, tok):
            g = x.shape[1]
            hd = d // 2
            tmp = rt[:, 0:g * d].rearrange("p (g d) -> p g d", g=g)
            s1 = cs[:, 1, 0:hd].unsqueeze(1).broadcast_to([128, g, hd])
            s2 = cs[:, 1, hd:d].unsqueeze(1).broadcast_to([128, g, hd])
            co = cs[:, 0, 0:d].unsqueeze(1).broadcast_to([128, g, d])
            a = tt(tmp[:, :, 0:hd], x[:, :, hd:d], s1, ALU.mult, tok, rtfree[0], ready["rope"])
            b = tt(tmp[:, :, hd:d], x[:, :, 0:hd], s2, ALU.mult, tok)
            c = tt(x, x, co, ALU.mult, a, b)
            r = tt(x, x, tmp, ALU.add, c)
            rtfree[0] = r
            return r

        def head_norm(x, g, grow_, tok, w):
            tmp = rt[:, 0:g * 128].rearrange("p (g d) -> p g d", g=g)
            a = tt(tmp, x, x, ALU.mult, tok, rtfree[0])
            c = V(lambda e: e.tensor_reduce(rs[:, w:w + g], tmp, AX, ALU.add), a)
            t = rstd(rs[:, w:w + g], rs[:, w:w + g], 1.0 / 128, EPS_RMS, c)
            r = None
            for h in range(g):
                r = stt(x[:, h, :], x[:, h, :], rs[:, w + h:w + h + 1], grow_, ALU.mult, ALU.mult, t, ready["grow"])
            rtfree[0] = r
            return r

        ppfree = [None]
        ptfree2 = [None]

        def softmax(bs, t, scale, bias=None):
            src = [banks[b][:, :] for b in bs]
            lt = [t, t]
            if bias is not None:
                for x in range(2):
                    r0 = stt(pp[:, x, 0:256], src[x][:, 0:256], scale, bias[x], ALU.mult, ALU.add, t, ppfree[0])
                    r1 = ts1(pp[:, x, 256:512], src[x][:, 256:512], scale, ALU.mult, t, ppfree[0])
                    give(bs[x], r1)
                    src[x] = pp[:, x, :]
                    lt[x] = [r0, r1]
            for x in range(2):
                lt[x] = V(lambda e, x=x: e.tensor_reduce(smx[:, 5, x:x + 1], src[x], AX, ALU.max), lt[x], ppfree[0])
            sc = 1.0 if bias is not None else scale
            tn_ = ts1(smx[:, 5, 2:4], smx[:, 5, 0:2], -sc, ALU.mult, lt)
            yield True
            te = []
            for x in range(2):
                te.append(act(pp[:, x, :], src[x], ACT.Exp, tn_, ppfree[0], bias=smx[:, 5, 2 + x:3 + x], scale=sc,
                              accum_out=smx[:, 5, 4 + x:5 + x]))
                if bias is None:
                    give(bs[x], te[-1])
            tr_ = V(lambda e: e.reciprocal(smx[:, 5, 6:8], smx[:, 5, 4:6]), te)
            yield True
            return tr_

        def pT_block(x, src, tok):
            b = yield from take()
            for c in range(4):
                t = tr(banks[b][:, c * 128:(c + 1) * 128], src[:, c * 128:(c + 1) * 128], tok, sidefree[b], sig=c == 3)
            yield True
            ta = copyA(pT[:, :, x * 128:(x + 1) * 128], banks[b][:, :].rearrange("p (c q) -> p c q", c=4), t,
                       ptfree2[0], sgfree)
            give(b, ta)
            return ta, t

        def attend(pairs, scale, vcols, dest, w, bias=None):
            b0 = yield from take()
            b1 = yield from take()
            bs = [b0, b1]
            for x in range(2):
                pr = pairs(x)
                for n, (l, r) in enumerate(pr):
                    t = mm(banks[bs[x]][:, :], l, r, n == 0, n == len(pr) - 1, w, sidefree[bs[x]],
                           sig=n == len(pr) - 1)
            yield True
            tr_ = yield from softmax(bs, t, scale, bias)
            tp_ = []
            for x in range(2):
                tn_ = ts1(pp[:, x, :], pp[:, x, :], smx[:, 5, 6 + x:7 + x], ALU.mult, tr_)
                ta, tl = yield from pT_block(x, pp[:, x, :], tn_)
                tp_.append(ta)
            ppfree[0] = tl
            yield True
            b = yield from take()
            for c in range(4):
                t = mm(banks[b][:, 0:256], vcols(c), pT[:, c, :], c == 0, c == 3, tp_, sidefree[b], sig=c == 3)
            ptfree2[0] = t
            yield True
            give(b, dest(banks[b][:, 0:256], t))
            yield True

        def dest_ot(h):
            def f(ps, t):
                r = copyA(ot[:, h, :], ps, t)
                ready[("ot", h)] = r
                return r
            return f

        def dest_oT(h):
            def f(ps, t):
                a = copyA(oh[:, h, :], ps, t, ready["df_v"])
                r = tt(ol[:, h, :], ps, f32(oh[:, h, :]), ALU.subtract, a, t, ready["df_v"])
                ready[("oT", h)] = [a, r]
                return r
            return f

        def side_tables():
            while "cw_free" not in ready:
                yield False
            s = [slot() for _ in range(6)]
            w = ready["cw_free"]
            ready["rope"] = [
                Q.dma("G", ropeA[:, :, :, :].rearrange("p t a b -> p t (a b)"),
                      I["k_rope128"].rearrange("(t p) a b -> p t (a b)", p=128), s[0], w),
                Q.dma("G", ropeB[:, :, :, :].rearrange("p t a b -> p t (a b)"),
                      I["k_rope64"].rearrange("(t p) a b -> p t (a b)", p=128), s[1], w)]
            tg = [Q.dma("G", grow[:, i, :], I[n][0].partition_broadcast(128), s[2 + i])
                  for i, n in enumerate(("gqa_gq_2", "gqa_gk_2", "diff_gsub_2"))]
            tm = ts1(grow[:, 2, :], grow[:, 2, :], 1.0 - LAM0, ALU.mult, tg)
            ready["grow"] = [tg, tm]
            ready["nam"] = Q.dma("G", nam[:, :], I["k_namask"], s[5])
            yield True

        def side_na():
            while any(k not in ready for k in ("na_q", "na_k", "r12_free", "nam", "ex_free", "x1_done")):
                yield False
            snav = scr_na.tensor

            def load_bias(h):
                n = h % 2
                toks = []
                for r in range(4):
                    src = bass.AP(tensor=snav, offset=(h * 15 + 7 - r) * 128 + 63,
                                  ap=[[P60 - 1, 64], [128, 4], [1, 64]])
                    toks.append(Q.dma("G", nb_[n][(r % 2) * 64:(r % 2) * 64 + 64, r // 2, :, :], src, nbs[n][r],
                                      ready["scr_na"], nbfree[n]))
                v = nb_[n][:, :, :, :].rearrange("p a b c -> p (a b) c")
                return tt(v, v, nam[:, :].unsqueeze(1).broadcast_to([128, 8, 64]), ALU.add, toks, ready["nam"])

            nbs = [[slot() for _ in range(4)] for _ in range(2)]
            nbfree = [[ready["ex_free"], ready["swT_free"], ready["x1_done"]]] * 2
            tq = yield from in_place([([na_q[:, tb, h, :] for tb in XT], na_q[:, :, h, :]) for h in range(4)],
                                     ready["na_q"])
            tk = yield from in_place([([na_k[:, tb, h, :] for tb in ALL], na_k[:, :, h, :]) for h in range(4)],
                                     ready["na_k"])
            while "na_v" not in ready:
                yield False
            for h in range(4):
                tb_ = load_bias(h)
                yield True
                bias = [nb_[h % 2][:, x, :, :].rearrange("p a b -> p (a b)") for x in range(2)]
                yield from attend(lambda x: [(na_q[:, x, h, :], na_k[:, :, h, :])], 128 ** -0.5,
                                  lambda c: na_v[:, c, h * 128:(h + 1) * 128], dest_ot(h),
                                  [tq, tk, tb_, ready["na_v"]], bias)
                nbfree[h % 2] = ready[("ot", h)]
            ready["o_na"] = [ready[("ot", h)] for h in range(4)]
            yield True

        def side_gq():
            while any(k not in ready for k in ("gq_q", "gq_kv", "o_na", "rope", "grow")):
                yield False
            tq = []
            for tb in XT:
                t = head_norm(gq_q[:, tb, :, :], 4, grow[:, 0, :], ready["gq_q"], 0)
                tq.append(rope(gq_q[:, tb, :, :], ropeA[:, tb, :, :], 128, t))
                yield True
            tk = []
            for tb in ALL:
                t = head_norm(gq_kv[:, tb, 0:2, :], 2, grow[:, 1, :], ready["gq_kv"], 4)
                if tb < 2:
                    t = rope(gq_kv[:, tb, 0:2, :], ropeA[:, tb, :, :], 128, t)
                tk.append(t)
                yield True
            tq = yield from in_place([([gq_q[:, tb, h, :] for tb in XT], gq_q[:, :, h, :]) for h in range(4)], tq)
            tk = yield from in_place([([gq_kv[:, tb, h, :] for tb in ALL], gq_kv[:, :, h, :]) for h in range(2)], tk)
            for h in range(4):
                yield from attend(lambda x: [(gq_q[:, x, h, :], gq_kv[:, :, h // 2, :])], 128 ** -0.5,
                                  lambda c: gq_kv[:, c, 2 + h // 2, :], dest_ot(4 + h),
                                  [tq, tk, ready["gq_kv"]])
            ready["o_gq"] = [ready[("ot", 4 + h)] for h in range(4)]
            yield True

        def side_ml1():
            while any(k not in ready for k in ("ml_q", "ml_c", "o_na", "rope")):
                yield False
            tq = []
            for tb in XT:
                a = act(rt[:, :], ml_q[:, tb, :], ACT.Square, ready["ml_q"], rtfree[0], accum_out=rs[:, 8 + tb:9 + tb])
                rtfree[0] = a
                t = rstd(rs[:, 8 + tb:9 + tb], rs[:, 8 + tb:9 + tb], 1.0 / 512, EPS_RMS, a)
                tq.append(ts1(ml_q[:, tb, :], ml_q[:, tb, :], rs[:, 8 + tb:9 + tb], ALU.mult, t))
            yield True
            tc = []
            for tb in ALL:
                x = ml_c[:, tb, 0:256]
                a = act(rt[:, 0:256], x, ACT.Square, ready["ml_c"], rtfree[0], accum_out=rs[:, 10 + tb:11 + tb])
                rtfree[0] = a
                t = rstd(rs[:, 10 + tb:11 + tb], rs[:, 10 + tb:11 + tb], 1.0 / 256, EPS_RMS, a)
                tc.append(ts1(x, x, rs[:, 10 + tb:11 + tb], ALU.mult, t))
                if tb < 2:
                    tc.append(rope(ml_c[:, tb, 256:320].unsqueeze(1), ropeB[:, tb, :, :], 64, ready["ml_c"]))
                yield True
            toks = []
            for kp in range(2):
                b = yield from take()
                for k in range(2):
                    for tb in XT:
                        kt = 2 * kp + k
                        t = tr(banks[b][:, (2 * k + tb) * 128:(2 * k + tb + 1) * 128], ml_q[:, tb, kt * 128:(kt + 1) * 128],
                               tq, sidefree[b], sig=(k == 1 and tb == 1))
                yield True
                def gk(k):
                    kt = 2 * kp + k
                    return kt, par[:, col["mq"] + kt:col["mq"] + kt + 1], banks[b][:, k * 256:(k + 1) * 256]

                a = []
                for k in range(2):
                    kt, g, ps = gk(k)
                    a.append(act(cqh[:, kt, :], ps, ACT.Copy, t, ready["o_na"], scale=g))
                for k in range(2):
                    kt, g, ps = gk(k)
                    r = stt(cql[:, kt, :], ps, g, f32(cqh[:, kt, :]), ALU.mult, ALU.subtract, a, t)
                    toks += [a[k], r]
                give(b, r)
            tq_done = t
            yield True
            bs = []
            for kt in range(3):
                b = yield from take()
                bs.append(b)
                w = 64 if kt == 2 else 128
                for tb in ALL:
                    t = tr(banks[b][0:w, tb * 128:(tb + 1) * 128], ml_c[:, tb, kt * 128:kt * 128 + w],
                           tc, sidefree[b], sig=tb == 3)
            yield True
            for kt in range(2):
                g = par[:, col["mk"] + kt:col["mk"] + kt + 1]
                ps = banks[bs[kt]][:, :]
                a = act(ckh[:, kt, :], ps, ACT.Copy, t, tq_done, scale=g)
                r = stt(ckl[:, kt, :], ps, g, f32(ckh[:, kt, :]), ALU.mult, ALU.subtract, a, t)
                toks += [a, r]
                give(bs[kt], r)
            a = copyA(kpT[:, :], banks[bs[2]][0:64, :], t)
            give(bs[2], a)
            toks.append(a)
            ready["ml_T"] = toks
            yield True

        def side_df():
            while any(k not in ready for k in ("df_q", "df_k", "o_gq", "rope", "lam", "ml_T")):
                yield False
            tq, tk = [], []
            for tb in XT:
                tq.append(rope(df_q[:, tb, :, :].rearrange("p h (i d) -> p (h i) d", i=2), ropeB[:, tb, :, :], 64,
                               ready["df_q"]))
                yield True
                tk.append(rope(df_k[:, tb, :, :].rearrange("p h (i d) -> p (h i) d", i=2), ropeB[:, tb, :, :], 64,
                               ready["df_k"]))
                yield True
            tq = yield from in_place([([df_q[:, tb, h, :] for tb in XT], df_q[:, :, h, :]) for h in range(4)], tq)
            tk = yield from in_place([([df_k[:, tb, h, :] for tb in ALL], df_k[:, :, h, :]) for h in range(4)],
                                     [tk, ready["df_k"]])
            while "df_v" not in ready:
                yield False
            ofree = None
            for h in range(4):
                bo = yield from take()
                for x in range(2):
                    b0 = yield from take()
                    b1 = yield from take()
                    bs = [b0, b1]
                    for i in range(2):
                        p = slice(64 * i, 64 * i + 64)
                        t = mm(banks[bs[i]][:, :], df_q[p, x, h, :], df_k[p, :, h, :], True, True, tq, tk,
                               sidefree[bs[i]], sig=True)
                    yield True
                    tr_ = yield from softmax(bs, t, 0.125)
                    t1 = tt(smx[:, 6, 0:1], smx[:, 5, 7:8], lamt[:, 0:1], ALU.mult, tr_, ready["lam"], ppfree[0])
                    t2 = ts1(pp[:, 0, :], pp[:, 0, :], smx[:, 5, 6:7], ALU.mult, tr_)
                    t3 = stt(pp[:, 0, :], pp[:, 1, :], smx[:, 6, 0:1], pp[:, 0, :], ALU.mult, ALU.add, t1, t2)
                    ta, tl = yield from pT_block(x, pp[:, 0, :], t3)
                    ppfree[0] = [tl, t3]
                    yield True
                    for c in range(4):
                        t = mm(banks[bo][:, x * 128:(x + 1) * 128], pT[:, c, x * 128:(x + 1) * 128],
                               df_v[:, c, h * 128:(h + 1) * 128], c == 0, c == 3, ta, ready["df_v"], sidefree[bo],
                               sig=c == 3)
                    ptfree2[0] = t
                yield True
                tn_ = []
                a = copyA(rt[:, 0:256], banks[bo][:, 0:256], t, rtfree[0], ofree)
                give(bo, a)
                for x in range(2):
                    o_ = rt[:, x * 128:(x + 1) * 128]
                    s = act(rt[:, 256 + x * 128:384 + x * 128], o_, ACT.Square, a, accum_out=rs[:, 14 + x:15 + x])
                    s = rstd(rs[:, 14 + x:15 + x], rs[:, 14 + x:15 + x], 1.0 / 128, EPS_RMS, s)
                    tn_.append(stt(o_, o_, rs[:, 14 + x:15 + x], grow[:, 2, :], ALU.mult, ALU.mult, s, ready["grow"]))
                yield True
                b = yield from take()
                for x in range(2):
                    t = tr(banks[b][:, x * 128:(x + 1) * 128], rt[:, x * 128:(x + 1) * 128], tn_, sidefree[b], sig=x == 1)
                ofree = t
                rtfree[0] = t
                yield True
                give(b, dest_oT(12 + h)(banks[b][:, 0:256], t))
                yield True
            ready["o_df"] = True

        def side_ml2():
            while any(k not in ready for k in ("mkv0", "mkv1", "mq0", "mq1", "o_df")):
                yield False
            mw = [ready[k] for k in ("mkv0", "mkv1", "mq0", "mq1")]
            tr_ = []
            q4 = mq[:, :, :].rearrange("p t (h e) -> p t h e", h=4)
            k4 = mkv[:, :, :].rearrange("p t (h e) -> p t h e", h=4)
            for tb in XT:
                tr_.append(rope(q4[:, tb, :, 128:192], ropeB[:, tb, :, :], 64, mw))
                yield True
            t1 = yield from in_place([([q4[:, tb, h, 0:128] for tb in XT], q4[:, :, h, 0:128]) for h in range(4)], mw)
            t2 = yield from in_place([([q4[:, tb, h, 128:192] for tb in XT],
                                       mqp[:, h, :].rearrange("p (t c) -> p t c", t=2)) for h in range(4)], tr_)
            t3 = yield from in_place([([k4[:, tb, h, 0:128] for tb in ALL], k4[:, :, h, 0:128]) for h in range(4)], mw)
            for h in range(4):
                yield from attend(lambda x: [(q4[:, x, h, 0:128], k4[:, :, h, 0:128]),
                                             (mqp[:, h, x * 128:(x + 1) * 128], kpT[:, :])], 192 ** -0.5,
                                  lambda c: k4[:, c, h, 128:256], dest_oT(8 + h),
                                  [t1, t2, t3, ready["ml_T"], mw])
            ready["mla_free"] = [ready[("oT", 8 + h)] for h in range(4)]
            yield True

        def side_ot():
            while "o_gq" not in ready or "df_v" not in ready:
                yield False
            for h in range(8):
                a = copyA(oh[:, h, :], ot[:, h, :], ready[("ot", h)], ready["df_v"])
                r = tt(ol[:, h, :], ot[:, h, :], f32(oh[:, h, :]), ALU.subtract, a, ready[("ot", h)], ready["df_v"])
                ready[("oT", h)] = [a, r]
                if h % 2:
                    yield True

        sides.append(side_tables())
        sides.append(side_na())
        sides.append(side_gq())
        sides.append(side_ml1())
        sides.append(side_ot())
        sides.append(side_df())
        sides.append(side_ml2())

        x2 = at("x2", oMG, [128, 2, 2048])
        gta = at("gta", M0, [128, 2, 512])
        gtfree = [None, None]

        def side_x2():
            while "mla_free" not in ready:
                yield False
            ready["x2"] = Q.dma("G", x2[:, :, :], scr_x1, slot(), ready["scr_x1"], ready["mla_free"])
            yield True

        sides.append(side_x2())

        def sto(kt, tb):
            return (oh[:, kt, tb * 128:(tb + 1) * 128], ol[:, kt, tb * 128:(tb + 1) * 128])

        key_n["x2o"] = 8

        def out2(n):
            def ev(tb, ps, t):
                d = x2[:, tb, n * 512:(n + 1) * 512]
                r0 = tt(sg[:, tb, :], gta[:, n % 2, :], ps, ALU.mult, t, ready[("gta", n)], ptfree2[0], sgfree[tb])
                r = tt(d, d, sg[:, tb, :], ALU.add, r0, ready["x2"])
                sgfree[tb] = r
                gtfree[n % 2] = r0
                note("x2o", [r, t])
                return r0
            return ev

        order = list(range(8)) + [12, 13, 14, 15, 8, 9, 10, 11]
        for n in range(4):
            ada(2048 * 2 + 512 * n, False,
                ada_rows(gta[:, n % 2, :], ("gta", n), 
                         lambda n=n: [gtfree[n % 2]] + [ready[k] for k in ("mkv0", "mkv1", "mq0", "mq1")],
                         ("mkv0", "mkv1", "mq0", "mq1")))
            ada(2048 * 4 + 512 * n, False, ada_cols((5,)))
            gemm(I["w_out_2"][0][:, n * 512:(n + 1) * 512], order, 512, sto, XT, out2(n),
                 (), ktneed={kt: ("oT", kt) for kt in range(16)},
                 evneed=("x2", ("gta", n)))

        fh, fl = (at("fh", oFX, [128, 16, 256], F32R), at("fl", oFX + 16 * KB, [128, 16, 256], F32R))
        sil = at("sil", oFY, [128, 2, 512])
        hn = at("hn", oFY + 4 * KB, [128, 2, 512])
        gtf = at("gtf", oFY + 8 * KB, [128, 4, 512])
        idh = at("idh", oR1, [128, 24, 256], F32R)
        idl = at("idl", oR1 + 24 * KB, [128, 24, 256], F32R)
        acf = at("acf", oEX, [128, 16])

        def side_h2():
            while "x2o" not in ready or any(("mod", 5, n) not in ready or ("mod", 4, n) not in ready for n in range(4)):
                yield False
            tm = [ready[("mod", c, n)] for c in (4, 5) for n in range(4)]
            a0 = stt(acf[:, :], mod[:, 5, :], 1.0, par[:, col["gf"]:col["gf"] + 16], ALU.add, ALU.mult, tm,
                     [ready[("oT", h)] for h in range(8)])
            toks = []
            free = None
            xn_ = [at("xq0", oFY, [128, 2048]), at("xq1", oFY + 8 * KB, [128, 2048])]
            tn_ = []
            for tb in XT:
                t = act(xn_[tb][:, :], x2[:, tb, :], ACT.Square, ready["x2o"], ready["mla_free"], accum_out=rs[:, 16 + tb:17 + tb])
                t = rstd(rs[:, 18 + tb:19 + tb], rs[:, 16 + tb:17 + tb], 1.0 / 2048, EPS_RMS, t)
                tn_.append(ts1(xn_[tb][:, :], x2[:, tb, :], rs[:, 18 + tb:19 + tb], ALU.mult, t))
            tk, t = yield from to_hT(lambda tb: xn_[tb][:, :], tn_, acf[:, :], mod[:, 4, :], fh, fl, (0, 1),
                                     [ready["x2o"], a0])
            ready["h2"] = tk
            ready["fy_free"] = [t, tk]
            yield True

        sides.append(side_h2())

        def stf(kt, tb):
            return (fh[:, kt, tb * 128:(tb + 1) * 128], fl[:, kt, tb * 128:(tb + 1) * 128])

        def sti(kt, tb):
            return (idh[:, kt % 24, tb * 128:(tb + 1) * 128], idl[:, kt % 24, tb * 128:(tb + 1) * 128])

        silfree = [None, None]
        hnfree = [None]
        gtok = {}

        def ev_gate(s):
            def f(tb, ps, t):
                a = act(sil[:, tb, :], ps, ACT.Sigmoid, t, silfree[tb], ready["fy_free"])
                r = tt(sil[:, tb, :], sil[:, tb, :], ps, ALU.mult, a)
                gtok[s, tb] = r
                return r
            return f

        def ev_up(s):
            key_n[f"hn{s}"] = 2

            def f(tb, ps, t):
                r = tt(hn[:, tb, :], sil[:, tb, :], ps, ALU.mult, t, gtok[s, tb], hnfree[0], ready["fy_free"])
                silfree[tb] = r
                note(f"hn{s}", r)
                return r
            return f

        def side_id():
            for s in range(11):
                while f"hn{s}" not in ready:
                    yield False
                while s >= 6 and "dn0" not in ready:
                    yield False
                w = ready["dn0"] if s >= 6 else [ready["x2o"], ready["mla_free"], ready["h2"]]
                toks = []
                for cp_ in range(2):
                    b = yield from take()
                    for c in range(2):
                        for tb in XT:
                            k = 2 * cp_ + c
                            t = tr(banks[b][:, (2 * c + tb) * 128:(2 * c + tb + 1) * 128],
                                   hn[:, tb, k * 128:(k + 1) * 128], ready[f"hn{s}"], sidefree[b],
                                   sig=(c == 1 and tb == 1))
                    yield True
                    kt = (4 * s + 2 * cp_) % 24
                    h = idh[:, kt:kt + 2, :].rearrange("p a b -> p (a b)")
                    l = idl[:, kt:kt + 2, :].rearrange("p a b -> p (a b)")
                    ta = copyA(h, banks[b][:, :], t, w)
                    tv = tt(l, banks[b][:, :], f32(h), ALU.subtract, ta, w)
                    give(b, tv)
                    toks += [ta, tv]
                hnfree[0] = t
                ready[f"id{s}"] = toks
                yield True

        sides.append(side_id())

        def down(half, n):
            key_n[f"dn{half}"] = 8

            def f(tb, ps, t):
                d = x2[:, tb, n * 512:(n + 1) * 512]
                r0 = tt(sil[:, tb, :], gtf[:, n, :], ps, ALU.mult, t, ready[("gtf", n)], silfree[tb], gtok[10 if half else 5, tb])
                r = tt(d, d, sil[:, tb, :], ALU.add, r0)
                silfree[tb] = r
                note(f"dn{half}", [r, t])
                return r0
            return f

        for half, ss in ((0, range(6)), (1, range(6, 11))):
            for s in ss:
                gemm(I["ffn_wg_2"][0][:, 512 * s:512 * s + 512], list(range(16)), 512, stf, XT, ev_gate(s), ("h2",))
                gemm(I["ffn_wu_2"][0][:, 512 * s:512 * s + 512], list(range(16)), 512, stf, XT, ev_up(s), ())
                if half == 0 and s < 4:
                    ada(2048 * 5 + 512 * s, False, ada_rows(gtf[:, s, :], ("gtf", s), lambda: ready["fy_free"], ("fy_free",)))
            k0 = 4 * ss[0]
            kts = list(range(k0, k0 + 4 * len(ss)))
            for n in range(4):
                gemm(I["ffn_wd_2"][0][:, n * 512:(n + 1) * 512], kts, 512, sti, XT, down(half, n), (),
                     ktneed={kt: f"id{kt // 4}" for kt in kts}, evneed=(("gtf", n),))

        main()
        drain_need(("dn1",))
        gfin = at("gfin", oFX, [128, 2048])
        gfx = at("gfx", oFX + 8 * KB, [128, 2, 2048])
        tg = Q.dma("S", gfin[:, :], I["g_final_2"].partition_broadcast(128), slot(), ready["dn1"])
        last = []
        outv = out[0].rearrange("(b p) d -> p b d", p=128)
        for tb in XT:
            t = act(gfx[:, tb, :], x2[:, tb, :], ACT.Square, ready["dn1"], accum_out=rs[:, 20 + tb:21 + tb])
            t = rstd(rs[:, 22 + tb:23 + tb], rs[:, 20 + tb:21 + tb], 1.0 / 2048, EPS_RMS, t)
            for c in range(2):
                cs = slice(c * 1024, (c + 1) * 1024)
                t2 = stt(gfx[:, tb, cs], x2[:, tb, cs], rs[:, 22 + tb:23 + tb], gfin[:, cs], ALU.mult, ALU.mult, t, tg)
                last.append(Q.dma("S", outv[:, tb, cs], gfx[:, tb, cs], slot(), t2))
        fin(nc, ctx, Q, last)


def fin(nc, ctx, Q, last):
    block = ctx.enter_context(nc.Block())
    Q.wait("S", last)

    @block.sync
    def _(eng):
        Q.run("S", eng)

    @block.gpsimd
    def _(eng):
        Q.run("G", eng)

    @block.scalar
    def _(eng):
        Q.run("A", eng)

    @block.vector
    def _(eng):
        Q.run("V", eng)

    @block.tensor
    def _(eng):
        Q.run("P", eng)


_INS = ["x", "w_in", "pool_w", "pool_scale", "sgu_ln_g", "sgu_ln_b", "sgu_w", "sgu_b", "attn_sinks", "rel_bias",
        "conv_w", "conv_b", "conv_ln_g", "conv_ln_b", "w_branch", "w_out", "ln_g", "ln_b", "c_2", "ctx_2", "c_ctx_2",
        "w_ada_2", "b_ada_2", "g_attn_2", "g_ffn_2", "w_in_2", "w_out_2", "na_rpb_2", "gqa_gq_2", "gqa_gk_2",
        "mla_gq_2", "mla_gkv_2", "mla_wuq_2", "mla_wukv_2", "diff_lq1_2", "diff_lk1_2", "diff_lq2_2", "diff_lk2_2",
        "diff_gsub_2", "ffn_wg_2", "ffn_wu_2", "ffn_wd_2", "g_final_2"]


def kernel(**inputs):
    import numpy as _np
    import concourse.bacc as _bacc
    from concourse import mybir as _mybir
    from concourse.bass_utils import run_bass_kernel_spmd as _run

    nc = _bacc.Bacc("TRN2", target_bir_lowering=False, num_devices=1)
    given = {n: _np.ascontiguousarray(inputs[n]) for n in _INS}
    given.update(constants())
    arrays, aps = {}, {}
    for name, a in given.items():
        arrays[f"in_{name}"] = a
        aps[name] = nc.dram_tensor(f"in_{name}", a.shape, _mybir.dt.from_np(a.dtype), kind="ExternalInput").ap()
    out = nc.dram_tensor("out_0", (1, 256, 2048), _mybir.dt.float32, kind="ExternalOutput").ap()
    program(nc, aps, out)
    r = _run(nc, [arrays], core_ids=[0])
    return r.results[0]["out_0"]
```

```python
import math
from contextlib import ExitStack

import numpy as np
import concourse.bass as bass
from concourse import mybir

F32 = mybir.dt.float32
F32R = mybir.dt.float32r
ALU = mybir.AluOpType
ACT = mybir.ActivationFunctionType
AX = mybir.AxisListType.X

BASE = 16512
KB = 1024
NRAW = 3
NSPL = 5
LEAD = 3
NMAIN = 4
SLACK = 2.0
RESUME = 0.4
AHEAD = 4
ADA_RATE = dict(A=0.4, D=0.3, B=0.0, merge_D=0.2, merge_C=0.5, w_out=0.3, ctx=0.0, na_q=0.8,
                strips=0.7, mla=0.7, ffn=0.6)
NEG = -1e30
ALPHA = 2 ** 0.25
EPS_LN = 1e-5
EPS_RMS = 1e-6
LAM0 = 0.8 - 0.6 * math.exp(-0.3 * 0)


class DmaSlot:

    def __init__(self, sem):
        self.sem, self.n = sem, 0


class Queues:

    def __init__(self, sems):
        self.sems = sems
        self.cnt = {e: 0 for e in sems}
        self.q = {e: [] for e in sems}
        self.seen = {e: {} for e in sems}

    def _waits(self, e, waits):
        for w in waits:
            if w is None:
                continue
            if isinstance(w, list):
                self._waits(e, w)
                continue
            sem, v = w
            if self.seen[e].get(id(sem), 0) < v:
                self.seen[e][id(sem)] = v
                self.q[e].append(("wait", sem, v))

    def op(self, e, fn, *waits, sig=None):
        self._waits(e, waits)
        if sig is None:
            sig = e != "P"
        if sig:
            self.cnt[e] += 1
            self.q[e].append(("op", fn, self.sems[e], 1))
            return (self.sems[e], self.cnt[e])
        self.q[e].append(("op", fn, None, 0))
        return None

    def dma(self, e, dst, src, slot, *waits):
        self._waits(e, waits)
        slot.n += 16
        self.q[e].append(("op", lambda g: g.dma_start(dst, src), slot.sem, 16))
        return (slot.sem, slot.n)

    def wait(self, e, *waits):
        self._waits(e, waits)

    def run(self, e, eng):
        for item in self.q[e]:
            if item[0] == "wait":
                eng.wait_ge(item[1], item[2])
            else:
                ins = item[1](eng)
                if item[2] is not None:
                    ins.then_inc(item[2], item[3])


def t5_buckets():
    n = np.arange(128)
    nf = np.maximum(n, 1).astype(np.float32)
    large = 16 + (np.log(nf / np.float32(16)) / np.float32(math.log(8)) * np.float32(16)).astype(np.int32)
    return np.where(n < 16, n, np.minimum(large, 31))


def constants():
    c = {}
    pm = np.zeros((256, 4, 256), np.float32)
    for g, w in enumerate((2, 4, 8, 16)):
        for t in range(256):
            lo = max(t + 1 - w, 0)
            pm[lo:t + 1, g, t] = np.float32(1.0) / np.float32(min(t + 1, w))
            pm[t, g, t] -= np.float32(1.0)
    c["k_pool"] = pm
    oh = np.zeros((32, 128), np.float32)
    oh[t5_buckets()[127 - np.arange(128)], np.arange(128)] = 1.0
    c["k_bucket"] = oh
    q = np.arange(64)[:, None]
    k = np.arange(64)[None, :]
    st = np.clip(q - 8, 0, 48)
    m = np.where((k >= st) & (k < st + 16), 0.0, NEG).astype(np.float32)
    c["k_namask"] = np.concatenate([m, m], 0)

    def rope(dim):
        t = np.arange(256)
        row, col = (t // 64).astype(np.float32), (t % 64).astype(np.float32)
        da = dim // 2
        inv = (1.0 / (np.float32(10000.0) ** (np.arange(0, da, 2, dtype=np.float32) / np.float32(da)))).astype(np.float32)
        ang = np.concatenate([row[:, None] * inv, col[:, None] * inv], -1).astype(np.float32)
        co, si = np.cos(ang), np.sin(ang)
        return np.stack([np.concatenate([co, co], -1), np.concatenate([-si, si], -1)], 1).astype(np.float32)

    c["k_rope128"] = rope(128)
    c["k_rope64"] = rope(64)
    return c


def program(nc, I, out):
    ctx = ExitStack()
    with ctx:
        def sem(name):
            return ctx.enter_context(nc.semaphore(name))

        def at(name, off, shape, dt=F32):
            n = 4
            for s in shape[1:]:
                n *= s
            assert off % 32 == 0
            return nc.alloc_sbuf_tensor_at(name, shape, dt, offset=BASE + off)

        o = 0
        oRAW = o; o += NRAW * 8 * KB
        oHI = o; o += NSPL * 4 * KB
        oLO = o; o += NSPL * 4 * KB
        oFX = o; o += 32 * KB
        oFY = o; o += 16 * KB
        oMG = o; o += 16 * KB
        oR1 = o; o += 26 * KB
        oR2 = o; o += 20 * KB
        oSG = o; o += 4 * KB
        oSW = o; o += 4 * KB
        oEX = o; o += 4 * KB
        oAC = o; o += 4 * KB
        oS1 = o; o += 8 * KB
        oSM = o

        raw = at("raw", oRAW, [128, NRAW, 4, 512])
        whi = at("whi", oHI, [128, NSPL, 2, 512], F32R)
        wlo = at("wlo", oLO, [128, NSPL, 2, 512], F32R)
        sg = at("sg", oSG, [128, 2, 512])
        acc = at("acc", oAC, [128, 2, 512])

        sm = [oSM]

        def small(name, shape, dt=F32):
            n = 4
            for s in shape[1:]:
                n *= s
            r = at(name, sm[0], shape, dt)
            sm[0] += -(-n // 32) * 32
            return r

        ident = small("ident", [128, 128])
        ones = small("ones", [128, 128])
        par = small("par", [128, 112])
        mod = small("mod", [128, 8, 16])
        brow = small("brow", [128, 512])
        rope_off = sm[0]
        ropeA = small("ropeA", [128, 2, 2, 128])
        ropeB = small("ropeB", [128, 2, 2, 64])
        cw = at("cw", rope_off, [128, 8, 31])
        grow = small("grow", [128, 3, 128])
        nam = small("nam", [128, 64])
        st = small("st", [128, 4, 6])
        mv = small("mv", [128, 2])
        rs = small("rs", [128, 24])
        mhalf = small("half", [128, 24])
        silc = small("silc", [128, 2, 16])
        lamt = small("lamt", [128, 8])
        snk = small("snk", [128, 16])
        smx = small("smx", [128, 2, 5, 8])
        sm5 = small("sm5", [128, 2, 16])
        assert BASE + sm[0] <= 229368, (BASE + sm[0] - 229368)

        banks = [ctx.enter_context(nc.psum_tensor(f"pb{i}", [128, 512], F32)) for i in range(8)]
        sems = {e: sem("e" + e) for e in "PVAGS"}
        Q = Queues(sems)
        rawslot = [DmaSlot(sem(f"dw{i}")) for i in range(NRAW)]
        nslots = [0]

        def slot():
            nslots[0] += 1
            return DmaSlot(sem(f"dm{nslots[0]}"))

        def dram(name, shape):
            return nc.dram_tensor(name, shape, F32, kind="Internal").ap()

        scr_band = dram("scr_band", [128 * 16 * 384])
        scr_na = dram("scr_na", [64 * 60 * 128])
        scr_x1 = dram("scr_x1", [128, 2, 2048])

        clock = {"P": 0.0, "V": 0.0, "A": 0.0}

        def V(fn, *w, n=64, rate=0.96):
            clock["V"] += 0.07 + n / (1e3 * rate)
            return Q.op("V", fn, *w)

        def A(fn, *w, n=64):
            clock["A"] += 0.19 + n / 1.2e3
            return Q.op("A", fn, *w)

        def G(fn, *w): return Q.op("G", fn, *w)
        def P(fn, *w, sig=False): return Q.op("P", fn, *w, sig=sig)

        def act(dst, src, f, *w, **kw):
            return A(lambda e: e.activation(dst, src, f, **kw), *w, n=dst.free_size())

        def copyA(dst, src, *w):
            return act(dst, src, ACT.Copy, *w)

        def copyV(dst, src, *w):
            return V(lambda e: e.tensor_copy(dst, src), *w, n=dst.free_size())

        def tt(dst, a, b, op, *w):
            return V(lambda e: e.tensor_tensor(dst, a, b, op), *w, n=dst.free_size())

        def ts(dst, a, s1, s2, o1, o2, *w):
            return V(lambda e: e.tensor_scalar(dst, a, s1, s2, o1, o2), *w, n=dst.free_size())

        def ts1(dst, a, s1, o1, *w):
            return V(lambda e: e.tensor_scalar(dst, a, s1, None, o1), *w, n=dst.free_size())

        def stt(dst, a, s, b, o1, o2, *w):
            return V(lambda e: e.scalar_tensor_tensor(dst, a, s, b, o1, o2), *w, n=dst.free_size())

        def mm(dst, l, r, start, stop, *w, sig=False):
            clock["P"] += max(64, dst.free_size()) * (1 if l.dtype == F32R else 4) / 2.4e3
            return P(lambda e: e.matmul(dst, l, r, start=start, stop=stop), *w, sig=sig)

        def tr(dst, src, *w, sig=False):
            n = src.shape[0]
            clock["P"] += 0.054
            return P(lambda e: e.transpose(dst, src, ident[0:n, 0:n]), *w, sig=sig)

        def f32(ap):
            return ap.bitcast(F32)

        sidefree = {b: None for b in range(NMAIN, 8)}
        held = set()

        def take():
            while True:
                for b in sidefree:
                    if b not in held:
                        held.add(b)
                        return b
                yield False

        def take_n(n):
            while len(held) + n > len(sidefree):
                yield False
            bs = [b for b in sidefree if b not in held][:n]
            held.update(bs)
            return bs

        def give(b, tok):
            held.discard(b)
            del sidefree[b]
            sidefree[b] = tok

        ready = {}

        def rstd(dst, src, scale, eps, *w):
            n = src.shape[1]
            t = ts(dst, src, scale, eps, ALU.mult, ALU.add, *w)
            return G(lambda e: e.tensor_tensor(dst, dst, mhalf[:, 0:n], ALU.pow), t, ready["half"])

        main_free = [None] * NMAIN
        main_next = [0]
        spl_free = [None] * NSPL
        raw_free = [None] * NRAW
        raw_tok = {}

        loads = []
        subs = []
        jobs = []

        def gemm(src, kts, ncols, stat, tbs, evac, need=(), ktneed=None, evneed=(), ahead=0):
            j = dict(kts=kts, ncols=ncols, stat=stat, tbs=tbs, evac=evac, need=need, kind="mm",
                     ktneed=ktneed or {}, evneed=evneed, ahead=ahead)
            jobs.append(j)
            n = len(kts)
            for a in range(0, n, 4):
                c = min(4, n - a)
                r = kts[a] * 128
                assert list(kts[a:a + c]) == list(range(kts[a], kts[a] + c))
                loads.append((src[r:r + c * 128, :], c, ncols))
                for b in range(0, c, 2):
                    d = min(2, c - b)
                    subs.append((len(loads) - 1, b, d, j, a + b, a + b + d == n, b + d == c))
                ada_rate[1] += ada_rate[0]
                while ada_rate[1] >= 1:
                    ada_rate[1] -= 1
                    ada_some(1)

        adaq = []
        ada_rate = [0.0, 0.0]

        def ada(col0, two, fin, need=()):
            j = dict(kind="ada", two=two, fin=fin, col0=col0, need=need)
            for a in range(0, 16, 4):
                adaq.append((j, a))

        def ada_some(n):
            for _ in range(n):
                if adaq:
                    j, a = adaq.pop(0)
                    col0 = j["col0"]
                    loads.append((I["w_ada_2"][0, a * 128:(a + 4) * 128, col0:col0 + 512], 4, 512))
                    subs.append((len(loads) - 1, 0, 4, j, a, a == 12, True))

        emitted_loads = [0]

        def emit_load():
            l = emitted_loads[0]
            if l >= len(loads):
                return
            src, c, n = loads[l]
            s = l % NRAW
            raw_tok[l] = Q.dma("S", raw[:, s, 0:c, 0:n], src.rearrange("(k p) n -> p k n", p=128),
                               rawslot[s], raw_free[s])
            emitted_loads[0] += 1

        adafree = [None]
        brow_slot = slot()

        def emit_split(i):
            l, b, d, j, k0, last, lastofload = subs[i]
            s = l % NRAW
            n = loads[l][2]
            if j["kind"] == "mm":
                u = split_no[i] % NSPL
                h = whi[:, u, 0:d, 0:n]
                lo = wlo[:, u, 0:d, 0:n]
                r = raw[:, s, b:b + d, 0:n]
                ta = copyA(h, r, raw_tok[l], spl_free[u])
                tv = tt(lo, r, f32(h), ALU.subtract, ta, raw_tok[l], spl_free[u])
                split_tok[i] = [ta, tv]
                if lastofload:
                    raw_free[s] = [ta, tv]
            else:
                if k0 == 0:
                    j["brow"] = Q.dma("G", brow[0:1, :], I["b_ada_2"][0:1, j["col0"]:j["col0"] + 512],
                                      brow_slot, adafree[0])
                prev = j.get("acc", adafree[0])
                for k in range(4):
                    toks = []
                    for m in range(2 if j["two"] else 1):
                        a = acc[:, m, :]
                        r = raw[:, s, k, 0:n]
                        c = silc[:, m, k0 + k:k0 + k + 1]
                        if k0 + k == 0:
                            toks.append(ts1(a, r, c, ALU.mult, raw_tok[l], prev, ready["silc"]))
                        else:
                            toks.append(stt(a, r, c, a, ALU.mult, ALU.add, raw_tok[l], prev))
                    prev = toks
                j["acc"] = prev
                raw_free[s] = prev
                if last:
                    adapend.append(j)
                    adafree[0] = "open"
            if lastofload:
                emit_load()

        adapend = []

        def ada_side():
            while True:
                if not adapend:
                    yield False
                    continue
                j = adapend.pop(0)
                yield True
                yield from j["fin"](j)

        def ada_cols(row):
            def fin(j):
                b = yield from take()
                n = 2 if j["two"] else 1
                blk = (j["col0"] % 2048) // 128
                first = True
                for m in range(n):
                    for q in range(4):
                        d = banks[b][:, 4 * m + q:4 * m + q + 1]
                        mm(d, acc[:, m, q * 128:(q + 1) * 128], ones[:, 0:1], True, False,
                           j["acc"], sidefree[b] if first else None, ready["ones"], j["brow"])
                        t = mm(d, brow[0:1, q * 128:(q + 1) * 128], ones[0:1, 0:1], False, True, sig=True)
                        first = False
                adafree[0] = t
                yield True
                toks = []
                for m in range(n):
                    toks.append(copyV(mod[:, row[m], blk:blk + 4], banks[b][:, 4 * m:4 * m + 4], t))
                give(b, toks[-1])
                ready[("mod", row[0], blk // 4)] = toks
                yield True
            return fin

        def gate_rows(dst, row, n, key, war, after=()):
            while any(k not in ready for k in after) or ("mod", row, n) not in ready:
                yield False
            b = yield from take()
            tv = [V(lambda e, q=q: e.tensor_scalar(gcol[:, q, :], ones[:, :], mod[:, row, 4 * n + q:4 * n + q + 1],
                                                   None, ALU.mult), ready[("mod", row, n)], gfree[0], n=128)
                  for q in range(4)]
            yield True
            for q in range(4):
                t = mm(banks[b][:, q * 128:(q + 1) * 128], gcol[:, q, :], ident[:, :], True, True, tv, sidefree[b],
                       sig=q == 3)
            gfree[0] = t
            yield True
            tv = copyA(dst, banks[b][:, :], t, war() if war else None)
            give(b, tv)
            ready[key] = tv
            yield True

        gfree = [None]

        split_no = {}
        split_tok = {}
        sides = []
        first = []

        resume = {}

        makers = {"mT": "side_m", "hx": "side_x1", "h2": "side_h2"}

        def step(forced=True, want=None):
            order = sorted(sides, key=lambda g: (g.__name__ != want, resume.get(id(g), 0.0))) if forced else list(sides)
            for g in order:
                r = resume.get(id(g), 0.0)
                if not forced and r > clock["P"]:
                    continue
                try:
                    went = next(g)
                except StopIteration:
                    sides.remove(g)
                    return True
                if went:
                    if forced:
                        clock["P"] = max(clock["P"], r)
                    resume[id(g)] = max(clock["V"], clock["A"]) + RESUME
                    return True
            if forced:
                clock["P"] = max(clock.values())
            return False

        def tick():
            for e in "VA":
                clock[e] = max(clock[e], clock["P"])
            for _ in range(6):
                if max(clock["V"], clock["A"]) > clock["P"] + SLACK or not step(False):
                    break

        def drain_need(keys):
            for k in keys:
                n = 0
                while k not in ready:
                    if not step(want=makers.get(k[0]) if isinstance(k, tuple) else None):
                        n += 1
                        if n > 3:
                            raise RuntimeError(f"nothing can bring {k}")

        def toks_of(keys):
            return [ready[k] for k in keys if not isinstance(ready[k], bool)]

        def pe_sub(i):
            l, b, d, j, k0, last, _ = subs[i]
            if j["kind"] != "mm":
                return
            n = j["ncols"]
            if k0 == 0:
                drain_need(j["need"])
                Q.wait("P", toks_of(j["need"]))
                j["banks"] = {}
                for tb in j["tbs"]:
                    m = main_next[0] % NMAIN
                    main_next[0] += 1
                    j["banks"][tb] = m
                    Q.wait("P", main_free[m])
            u = split_no[i] % NSPL
            Q.wait("P", split_tok[i])
            t = None
            ntb = len(j["tbs"])
            for kk in range(d):
                kt = j["kts"][k0 + kk]
                if kt in j["ktneed"]:
                    drain_need((j["ktneed"][kt], j["ktneed"].get(kt + j["ahead"], j["ktneed"][kt])))
                    Q.wait("P", ready[j["ktneed"][kt]])
                for x, tb in enumerate(j["tbs"]):
                    hi, lo = j["stat"](kt, tb)
                    dst = banks[j["banks"][tb]][:, 0:n]
                    H, L = whi[:, u, kk, 0:n], wlo[:, u, kk, 0:n]
                    s = k0 + kk == 0
                    e = last and kk == d - 1
                    mm(dst, hi, H, s, False)
                    mm(dst, hi, L, False, False)
                    t = mm(dst, lo, H, False, e, sig=e or (kk == d - 1 and x == ntb - 1))
                    if e:
                        j.setdefault("done", {})[tb] = t
                if not (last and kk == d - 1):
                    tick()
            spl_free[u] = t
            if last:
                drain_need(j["evneed"])
                for tb in j["tbs"]:
                    m = j["banks"][tb]
                    main_free[m] = j["evac"](tb, banks[m][:, 0:n], j["done"][tb])

        def main():
            k = 0
            for i, s in enumerate(subs):
                if s[3]["kind"] == "mm":
                    split_no[i] = k
                    k += 1
            emit_load()
            load_x(1)
            for _ in range(NRAW - 1):
                emit_load()
            late = list(sides)
            sides.clear()
            for _ in range(4):
                next(first[0])
            done = 0
            for i in range(len(subs)):
                while done < len(subs):
                    if subs[done][3]["kind"] == "mm":
                        if split_no[done] > (split_no[i] if i in split_no else last_no) + LEAD:
                            break
                    elif subs[done][4] == 0 and any(k not in ready for k in subs[done][3]["need"]):
                        if done > i:
                            break
                        drain_need(subs[done][3]["need"])
                    elif subs[done][4] == 0 and adafree[0] == "open":
                        while adafree[0] == "open" and step():
                            pass
                        if adafree[0] == "open":
                            if done > i:
                                break
                            raise RuntimeError("a strip of w_ada waits for what comes after it")
                    emit_split(done)
                    done += 1
                if ("xT", 14) not in ready:
                    next(first[0])
                if i == 6:
                    next(first[0])
                    sides[0:0] = late
                    late.clear()
                if i in split_no:
                    last_no = split_no[i]
                    pe_sub(i)
                    tick()

        sgfree = [None, None]

        def ev_copy(dst, war=(), key=None):
            def f(tb, ps, t):
                w = toks_of(war)
                r = copyA(dst(tb), ps, t, w)
                if key:
                    ready.setdefault(key + "_", []).append(r)
                    if len(ready[key + "_"]) == key_n[key]:
                        ready[key] = ready[key + "_"]
                return r
            return f

        key_n = {}

        def note(key, tok):
            ready.setdefault(key + "_", []).append(tok)
            if len(ready[key + "_"]) == key_n[key]:
                ready[key] = ready[key + "_"]

        def ev_sig(dst, mul, war=(), key=None):
            def f(tb, ps, t):
                n = ps.shape[1]
                g = sg[:, tb, 0:n]
                a = act(g, ps, ACT.Sigmoid, t, sgfree[tb])
                w = toks_of(war)
                if mul == "silu":
                    r = tt(dst(tb), g, ps, ALU.mult, a, w)
                elif mul == "glu":
                    r = tt(dst(tb), g, dst(tb), ALU.mult, a, w)
                else:
                    r0 = tt(g, g, ps, ALU.mult, a, w)
                    r = tt(dst(tb), g, dst(tb), ALU.mult, r0)
                sgfree[tb] = r
                if key:
                    note(key, r)
                return [a, r]
            return f

        t = V(lambda e: e.memset(ones[:, :], 1.0))
        ready["ones"] = t
        ready["half"] = V(lambda e: e.memset(mhalf[:, :], -0.5))
        t = G(lambda e: e.memset(ident[:, :], 0.0))
        ready["ident"] = G(lambda e: e.affine_select(out=ident[:, :], in_=ident[:, :], compare_op=ALU.not_equal,
                                                     fill=1.0, base=0, pattern=[[-1, 128]],
                                                     channel_multiplier=1), t)
        xn = at("xn", oMG, [128, 2, 2048])
        xh = at("xh", oFX, [128, 16, 256], F32R)
        xl = at("xl", oFX + 16 * KB, [128, 16, 256], F32R)
        xv = I["x"][0].rearrange("(b p) d -> p b d", p=128)
        sx = [slot() for _ in range(4)]
        tx = []

        def load_x(c):
            cs = slice(c * 1024, (c + 1) * 1024)
            tx.append([Q.dma("S", xn[:, b, cs], xv[:, b, cs], sx[2 * b + c]) for b in range(2)])

        load_x(0)

        prow = at("prow", oSG, [128, 128])
        col = {}
        r = 0
        tp = []
        for name, src, n in (("c", I["c_2"].rearrange("a (r p) -> (a r) p", p=128), 16),
                             ("cc", I["c_ctx_2"].rearrange("(r p) -> r p", p=128), 16),
                             ("ga", I["g_attn_2"].rearrange("a (r p) -> (a r) p", p=128), 16),
                             ("gf", I["g_ffn_2"].rearrange("a (r p) -> (a r) p", p=128), 16),
                             ("cb", I["conv_b"].rearrange("a (r p) -> (a r) p", p=128), 8),
                             ("sb", I["sgu_b"][0], 8),
                             ("mq", I["mla_gq_2"].rearrange("a (r p) -> (a r) p", p=128), 4),
                             ("mk", I["mla_gkv_2"].rearrange("a (r p) -> (a r) p", p=128), 2)):
            tp.append(Q.dma("A", prow[r:r + n, :], src, slot()))
            col[name] = r
            r += n
        NPR = r
        cwn = at("cwn", oEX, [31, 1024])
        scw = slot()
        tcw = Q.dma("G", cwn[:, :], I["conv_w"][0], scw, tx[0])
        swn = at("swn", oS1, [128, 8, 128])
        swT = at("swT", oSW, [128, 8, 128])
        ssw = slot()
        tsw = Q.dma("G", swn[:, :, :], I["sgu_w"][0].rearrange("h t s -> t h s"), ssw, tx[0])
        for h in range(8):
            tsw = G(lambda e, h=h: e.affine_select(out=swn[:, h, :], in_=swn[:, h, :], compare_op=ALU.is_ge,
                                                   fill=0.0, base=0, pattern=[[-1, 128]],
                                                   channel_multiplier=1), tsw)
        bandt = at("bandt", oR2, [128, 8, 384])
        tband0 = G(lambda e: e.memset(bandt[:, :, :], NEG))
        ssk = slot()
        tsk = Q.dma("G", snk[:, :], I["attn_sinks"][0].partition_broadcast(128), ssk)
        relb = at("relb", oAC, [32, 16])
        relx = at("relx", oR2 + 12 * KB, [32, 16, 128])
        buck = at("buck", oAC + 512, [32, 128])
        trb = [Q.dma("A", relb[:, :], I["rel_bias"], slot()), Q.dma("A", buck[:, :], I["k_bucket"], slot())]
        nat = at("nat", oFY, [64, 30, 128])
        lrow = at("lrow", oFY + 15 * KB, [128, 4, 64])
        sl = [slot() for _ in range(4)]
        tlam = [Q.dma("A", lrow[:, i, :], I[n][0].partition_broadcast(128), sl[i])
                for i, n in enumerate(("diff_lq1_2", "diff_lk1_2", "diff_lq2_2", "diff_lk2_2"))]
        P60 = 60 * 128

        def side_natab():
            rpb = I["na_rpb_2"][0].rearrange("h m x -> (h m) x")
            sv = scr_na.rearrange("(c x) -> c x", x=P60)
            sna = slot()
            tn0 = G(lambda e: e.memset(nat[:, :, :], 0.0))
            tn = None
            for hh in range(2):
                yield True
                tn = Q.dma("G", nat[:, :, 48:79], rpb[30 * hh:30 * hh + 30, :].partition_broadcast(64), sna, tn0, tn)
                yield True
                yield True
                tn = Q.dma("G", sv[:, hh * 3840:hh * 3840 + 3840], nat[:, :, :].rearrange("p a b -> p (a b)"),
                           sna, tn)
                yield True
            ready["scr_na"] = tn

        def start_side():
            toks = []
            for kp in range(8):
                b = yield from take()
                for k in range(2):
                    for tb in range(2):
                        kt = 2 * kp + k
                        t = tr(banks[b][:, (2 * k + tb) * 128:(2 * k + tb + 1) * 128], xn[:, tb, kt * 128:(kt + 1) * 128],
                               tx[kp // 4], ready["ident"], sidefree[b], sig=(k == 1 and tb == 1))
                h = xh[:, 2 * kp:2 * kp + 2, :].rearrange("p a b -> p (a b)")
                l = xl[:, 2 * kp:2 * kp + 2, :].rearrange("p a b -> p (a b)")
                ta = copyA(h, banks[b][:, :], t)
                tv = tt(l, banks[b][:, :], f32(h), ALU.subtract, ta)
                toks += [ta, tv]
                give(b, tv)
                ready[("xT", 2 * kp)] = ready[("xT", 2 * kp + 1)] = [ta, tv]
                yield True
            ready["xT"] = toks
            ready["xn_free"] = t
            yield True

        def start_side2():
            b = yield from take()
            t = tr(banks[b][:, 0:NPR], prow[0:NPR, :], tp, ready["ident"], sidefree[b], sig=True)
            yield True
            tv = copyV(par[:, 0:NPR], banks[b][:, 0:NPR], t)
            sgfree[0] = sgfree[1] = tv
            give(b, tv)
            ready["par"] = tv
            a = act(silc[:, :, :].rearrange("p a b -> p (a b)"), par[:, 0:32], ACT.Sigmoid, tv)
            ready["silc"] = tt(silc[:, :, :].rearrange("p a b -> p (a b)"),
                               silc[:, :, :].rearrange("p a b -> p (a b)"), par[:, 0:32], ALU.mult, a)
            lv = lrow[:, :, :].rearrange("p (a b) d -> p a b d", b=2)
            t = tt(lv[:, :, 0, :], lv[:, :, 0, :], lv[:, :, 1, :], ALU.mult, tlam)
            t = V(lambda e: e.tensor_reduce(lamt[:, 0:2], lv[:, :, 0, :], AX, ALU.add), t)
            t = act(lamt[:, 2:4], lamt[:, 0:2], ACT.Exp, t)
            t = tt(lamt[:, 4:5], lamt[:, 3:4], lamt[:, 2:3], ALU.subtract, t)
            ready["lam"] = ts1(lamt[:, 0:1], lamt[:, 4:5], LAM0, ALU.subtract, t)
            for g in range(2):
                b = yield from take()
                for h in range(4):
                    t = tr(banks[b][:, h * 128:(h + 1) * 128], swn[:, 4 * g + h, :], tsw, sidefree[b], sig=h == 3)
                yield True
                tv = copyA(swT[:, 4 * g:4 * g + 4, :].rearrange("p a b -> p (a b)"), banks[b][:, :], t)
                give(b, tv)
            ready["swT"] = tv
            ready["swn_free"] = t
            b = yield from take()
            for f in range(8):
                t = tr(banks[b][:, f * 31:(f + 1) * 31], cwn[:, f * 128:(f + 1) * 128], tcw, sidefree[b], sig=f == 7)
            yield True
            tv = copyV(cw[:, :, :].rearrange("p a b -> p (a b)"), banks[b][:, 0:248], t)
            give(b, tv)
            ready["cw"] = tv
            ready["ex_free"] = t
            tv = copyV(relx[:, :, :], relb[:, :].unsqueeze(2).broadcast_to([32, 16, 128]), trb)
            yield True
            sb = slot()
            td = None
            for hf in range(2):
                toks = []
                for g in range(2):
                    b = yield from take()
                    for h in range(4):
                        t = mm(banks[b][:, h * 128:(h + 1) * 128], relx[:, 8 * hf + 4 * g + h, :], buck[:, :], True, True,
                               tv, sidefree[b], sig=h == 3)
                    yield True
                    ta = copyV(bandt[:, 4 * g:4 * g + 4, 128:256], banks[b][:, :].rearrange("p (h d) -> p h d", h=4),
                               t, tband0, td)
                    give(b, ta)
                    toks.append(ta)
                td = Q.dma("G", scr_band.rearrange("(p x) -> p x", x=6144)[:, hf * 3072:hf * 3072 + 3072],
                           bandt[:, :, :].rearrange("p a b -> p (a b)"), sb, toks)
                yield True
            ready["relx_free"] = t
            adafree[0] = t
            ready["scr_band"] = td
            yield True

        first.append(start_side())
        sides.append(start_side2())
        sides.append(ada_side())
        sides.append(side_natab())
        for n in range(4):
            for ch in (0, 1):
                ada(2048 * ch + 512 * n, True, ada_cols((ch, 2 + ch)), ("silc", "relx_free"))
        for ch, row in ((2, 6), (3, 4), (4, 5), (5, 7)):
            for n in range(4):
                ada(2048 * ch + 512 * n, False, ada_cols((row,)))

        W1 = I["w_in"][0]

        def stx(kt, tb):
            return (xh[:, kt, tb * 128:(tb + 1) * 128], xl[:, kt, tb * 128:(tb + 1) * 128])

        def win(c0, n, evac, need=("xT",)):
            gemm(W1[:, c0:c0 + n], list(range(16)), n, stx, (0, 1), evac, need)

        merged = at("merged", oMG, [128, 2, 2048])
        yh = at("yh", oFY, [128, 8, 256], F32R)
        yl = at("yl", oFY + 8 * KB, [128, 8, 256], F32R)
        exb = at("exb", oEX, [128, 1024])
        ext = [None]
        sex = slot()

        def load_ex(src, *w):
            ext[0] = Q.dma("G", exb[:, :], src.partition_broadcast(128), sex, ready["ex_free"], *w)
            return ext[0]

        def to_yT(src, key, toks, need):
            while need and need not in ready:
                yield False
            w = ready[need] if need else None
            out_ = []
            for kp in range(4):
                b = yield from take()
                for k in range(2):
                    for tb in range(2):
                        kt = 2 * kp + k
                        t = tr(banks[b][:, (2 * k + tb) * 128:(2 * k + tb + 1) * 128],
                               src(tb)[:, kt * 128:(kt + 1) * 128], toks, sidefree[b], sig=(k == 1 and tb == 1))
                yield True
                h = yh[:, 2 * kp:2 * kp + 2, :].rearrange("p a b -> p (a b)")
                l = yl[:, 2 * kp:2 * kp + 2, :].rearrange("p a b -> p (a b)")
                ta = copyA(h, banks[b][:, :], t, w)
                tv = tt(l, banks[b][:, :], f32(h), ALU.subtract, ta, w)
                out_ += [ta, tv]
                give(b, tv)
                yield True
            ready[key] = out_
            ready[key + "_src"] = t

        a_in = at("a_in", oR1, [128, 2, 1024])
        a_gt = at("a_gt", oR1 + 8 * KB, [128, 2, 1024])
        pgw = at("pgw", oR1 + 16 * KB, [128, 4, 2, 256])
        pm = at("pm", oMG, [128, 2, 4, 256])
        mixT = at("mixT", oMG + 8 * KB, [128, 8, 256])
        key_n.update(a_in=4, a_gt=4)
        for s in range(2):
            gemm(W1[:, 512 * s:512 * s + 512], list(range(16)), 512, stx, (0, 1),
                 ev_copy(lambda tb, s=s: a_in[:, tb, 512 * s:512 * s + 512], (), "a_in"),
                 ktneed={kt: ("xT", kt) for kt in range(16)})
        for s in range(2):
            win(1024 + 512 * s, 512, ev_sig(lambda tb, s=s: a_gt[:, tb, 512 * s:512 * s + 512], "silu",
                                            (), "a_gt"))

        def side_a():
            spm, spg = slot(), slot()
            while "xn_free" not in ready:
                yield False
            t1 = Q.dma("G", pm[:, :, :, :].rearrange("p k g t -> p k (g t)"),
                       I["k_pool"].rearrange("(k p) g t -> p k (g t)", p=128), spm, ready["xn_free"])
            t2 = Q.dma("G", pgw[:, :, :, :].rearrange("p g k n -> p (g k) n"),
                       I["pool_w"][0].rearrange("g (k p) n -> p (g k) n", p=128), spg)
            yield True
            while "a_in" not in ready:
                yield False
            toks = []
            for fp in range(4):
                b = yield from take()
                for f in range(2):
                    fb = 2 * fp + f
                    for k in range(2):
                        t = mm(banks[b][:, f * 256:(f + 1) * 256], a_in[:, k, fb * 128:(fb + 1) * 128],
                               pm[:, k, fb // 2, :], k == 0, k == 1, ready["a_in"], t1, sidefree[b],
                               sig=(f == 1 and k == 1))
                yield True
                tv = copyV(mixT[:, 2 * fp:2 * fp + 2, :].rearrange("p a b -> p (a b)"), banks[b][:, :], t)
                toks.append(tv)
                give(b, tv)
                yield True
            te = load_ex(I["pool_scale"][0])
            while "a_gt" not in ready:
                yield False
            rr = []
            for tb in range(2):
                for gp in range(2):
                    b = yield from take()
                    for g in range(2):
                        for k in range(2):
                            gg = 2 * gp + g
                            t = mm(banks[b][:, g * 256:(g + 1) * 256],
                                   mixT[:, 2 * gg + k, tb * 128:(tb + 1) * 128], pgw[:, gg, k, :], k == 0, k == 1,
                                   toks, t2, sidefree[b], sig=(g == 1 and k == 1))
                    yield True
                    d = a_in[:, tb, gp * 512:(gp + 1) * 512]
                    e = a_gt[:, tb, gp * 512:(gp + 1) * 512]
                    tv = tt(d, banks[b][:, :], exb[:, gp * 512:(gp + 1) * 512], ALU.mult, t, te)
                    give(b, tv)
                    rr.append(tt(d, d, e, ALU.mult, tv, ready["a_gt"]))
                    yield True
            ready["ex_free"] = rr[-1]
            ready["mg_free"] = t
            yield from to_yT(lambda tb: a_in[:, tb, :], "yA", rr, None)

        v_n = at("v_n", oR2, [128, 2, 1024])
        u_n = at("u_n", oR2 + 8 * KB, [128, 2, 1024])
        key_n.update(v_n=4, u_n=4, u_g=4)

        def layer_norm(x, n, tok, eps, ga, ba):
            toks = []
            for c in range(n // 512):
                toks.append(V(lambda e, c=c: e.bn_stats(st[:, c, :], x[:, c * 512:(c + 1) * 512]), tok, stfree[0]))
            t = V(lambda e: e.bn_aggr(mv[:, :], st[:, 0:n // 512, :].rearrange("p a b -> p (a b)")), toks)
            t = rstd(rs[:, 0:1], mv[:, 1:2], 1.0, eps, t)
            t = ts(x, x, mv[:, 0:1], rs[:, 0:1], ALU.subtract, ALU.mult, t)
            stfree[0] = t
            return t

        stfree = [None]
        stz = at("stz", oR1 + 25 * KB + 512, [128, 2, 4, 6])
        mvz = at("mvz", oR1 + 25 * KB + 704, [128, 2, 2])

        def ln_ex(xs, tok, g_src, b_src):
            tg = load_ex(g_src)
            yield True
            ts_ = []
            for tb in range(2):
                ts_.append(layer_norm(xs(tb), 1024, tok, EPS_LN, None, None))
                yield True
            t2 = [tt(xs(tb), xs(tb), exb[:, :], ALU.mult, ts_, tg) for tb in range(2)]
            ready["ex_free"] = t2[-1]
            yield True
            tb_ = load_ex(b_src)
            yield True
            yield True
            t3 = [tt(xs(tb), xs(tb), exb[:, :], ALU.add, t2, tb_) for tb in range(2)]
            ready["ex_free"] = t3[-1]
            yield True
            return t3

        for s in range(2):
            win(3072 + 512 * s, 512, ev_copy(lambda tb, s=s: v_n[:, tb, 512 * s:512 * s + 512],
                                             ("relx_free", "scr_band"), "v_n"), ("xT", "relx_free", "scr_band"))
        for s in range(2):
            win(2048 + 512 * s, 512, ev_copy(lambda tb, s=s: u_n[:, tb, 512 * s:512 * s + 512],
                                             ("relx_free", "scr_band"), "u_n"))
        for s in range(2):
            win(4096 + 512 * s, 512, ev_sig(lambda tb, s=s: u_n[:, tb, 512 * s:512 * s + 512], "silumul",
                                            ("u_n",), "u_g"))

        def side_b():
            while "v_n" not in ready or "yA" not in ready:
                yield False
            tn_ = yield from ln_ex(lambda tb: v_n[:, tb, :], ready["v_n"], I["sgu_ln_g"][0], I["sgu_ln_b"][0])
            res = []
            while "u_g" not in ready:
                yield False
            for tb in range(2):
                for hp in range(2):
                    b = yield from take()
                    for h in range(4):
                        hh = 4 * hp + h
                        t = mm(banks[b][:, h * 128:(h + 1) * 128], swT[:, hh, :],
                               v_n[:, tb, hh * 128:(hh + 1) * 128], True, True,
                               tn_, ready["swT"], sidefree[b], sig=h == 3)
                    yield True
                    for h in range(4):
                        hh = 4 * hp + h
                        u = u_n[:, tb, hh * 128:(hh + 1) * 128]
                        tv = stt(u, banks[b][:, h * 128:(h + 1) * 128], par[:, col["sb"] + hh:col["sb"] + hh + 1],
                                 u, ALU.add, ALU.mult, t, ready["u_g"], ready["par"])
                    res.append(tv)
                    give(b, tv)
                    yield True
            ready["swT_free"] = t
            yield from to_yT(lambda tb: u_n[:, tb, :], "yB", res, "mA")

        def merge(i, key, extra=()):
            key_n["m" + key] = 8
            ready_g = {}

            def sty(kt, tb):
                return (yh[:, kt, tb * 128:(tb + 1) * 128], yl[:, kt, tb * 128:(tb + 1) * 128])

            for n in range(4):
                def evg(tb, ps, t):
                    a = act(sg[:, tb, :], ps, ACT.Sigmoid, t, sgfree[tb])
                    sgfree[tb] = a
                    ready_g[tb] = a
                    return a

                def evb(tb, ps, t, n=n):
                    d = merged[:, tb, n * 512:(n + 1) * 512]
                    if i == 0:
                        r = tt(d, sg[:, tb, :], ps, ALU.mult, t, ready_g[tb], ready["mg_free"])
                    else:
                        r0 = tt(sg[:, tb, :], sg[:, tb, :], ps, ALU.mult, t, ready_g[tb])
                        r = tt(d, d, sg[:, tb, :], ALU.add, r0, ready.get(("mer", n, tb)))
                    ready[("mer", n, tb)] = r
                    sgfree[tb] = r
                    note("m" + key, [r, t])
                    return r

                win(10496 + 2048 * i + 512 * n, 512, evg)
                gemm(I["w_branch"][0, i, :, n * 512:(n + 1) * 512], list(range(8)), 512, sty, (0, 1), evb,
                     ("y" + key, "mg_free"))

        sides.append(side_a())
        ada_rate[0] = ADA_RATE["A"]
        merge(0, "A")
        sides.append(side_b())

        ada_rate[0] = ADA_RATE["D"]
        d_n = at("d_n", oR1, [128, 2, 1024])
        glT = at("glT", oR1 + 8 * KB, [128, 8, 286])
        d_o = at("d_o", oR1, [128, 8, 256])
        d_y = at("d_y", oR1 + 8 * KB, [128, 2, 1024])
        d_g = at("d_g", oR1 + 8 * KB + 9152, [128, 2, 1024])
        key_n.update(d_v=4, d_n=4, d_g=4)
        for s in range(2):
            win(7424 + 512 * s, 512, ev_copy(lambda tb, s=s: d_n[:, tb, 512 * s:512 * s + 512], ("yA_src",), "d_v"),
                ("yA_src", "xT"))
        for s in range(2):
            win(8448 + 512 * s, 512, ev_sig(lambda tb, s=s: d_n[:, tb, 512 * s:512 * s + 512], "glu", ("d_v",), "d_n"))
        for s in range(2):
            win(9472 + 512 * s, 512, ev_sig(lambda tb, s=s: d_g[:, tb, 512 * s:512 * s + 512], "silu", ("yA_src",), "d_g"))

        def side_d():
            while "d_n" not in ready or "yB" not in ready or "cw" not in ready or "yA_src" not in ready:
                yield False
            t0 = V(lambda e: e.memset(glT[:, :, 0:30], 0.0), ready["yA_src"])
            tg_ = []
            for f in range(8):
                b = yield from take()
                for tb in range(2):
                    t = tr(banks[b][:, tb * 128:(tb + 1) * 128], d_n[:, tb, f * 128:(f + 1) * 128],
                           ready["d_n"], sidefree[b], sig=tb == 1)
                yield True
                tv = copyA(glT[:, f, 30:286], banks[b][:, 0:256], t)
                give(b, tv)
                tg_.append(tv)
            yield True
            prev = [None] * 8
            for k in range(31):
                for f in range(8):
                    w = cw[:, f, k:k + 1]
                    if k == 0:
                        prev[f] = ts1(d_o[:, f, :], glT[:, f, k:k + 256], w, ALU.mult, tg_, t0, ready["cw"], t)
                    else:
                        prev[f] = stt(d_o[:, f, :], glT[:, f, k:k + 256], w, d_o[:, f, :], ALU.mult, ALU.add, prev[f])
                    if f % 4 == 3:
                        yield True
            ready["cw_free"] = list(prev)
            for f in range(8):
                prev[f] = ts1(d_o[:, f, :], d_o[:, f, :], par[:, col["cb"] + f:col["cb"] + f + 1], ALU.add, prev[f])
            yield True
            ty = []
            for tb in range(2):
                for fp in range(2):
                    b = yield from take()
                    for f in range(4):
                        t = tr(banks[b][:, f * 128:(f + 1) * 128], d_o[:, 4 * fp + f, tb * 128:(tb + 1) * 128],
                               prev, sidefree[b], sig=f == 3)
                    yield True
                    tv = copyA(d_y[:, tb, fp * 512:(fp + 1) * 512], banks[b][:, :], t, prev)
                    give(b, tv)
                    ty.append(tv)
            t3 = yield from ln_ex(lambda tb: d_y[:, tb, :], ty, I["conv_ln_g"][0], I["conv_ln_b"][0])
            res = []
            for tb in range(2):
                for s in range(2):
                    y = d_y[:, tb, s * 512:(s + 1) * 512]
                    g = d_o[:, 4 * tb + 2 * s:4 * tb + 2 * s + 2, :].rearrange("p a b -> p (a b)")
                    a = act(g, y, ACT.Sigmoid, t3, t)
                    r = tt(y, y, g, ALU.mult, a)
                    r = tt(y, y, d_g[:, tb, s * 512:(s + 1) * 512], ALU.mult, r, ready["d_g"])
                    res.append(r)
                    yield True
            yield from to_yT(lambda tb: d_y[:, tb, :], "yD", res, "mB")

        sides.append(side_d())
        ada_rate[0] = ADA_RATE["B"]
        merge(1, "B")

        q_n = at("q_n", oR2, [128, 2, 8, 128])
        c_g = at("c_g", oR2 + 8 * KB, [128, 2, 1024])
        kd = at("kd", oR2 + 16 * KB, [128, 2, 2, 2, 64])
        vv = at("vv", oR2 + 18 * KB, [128, 2, 128])
        key_n.update(c_kv=2, c_q=4, c_g=4)

        def ev_kv(tb, ps, t):
            k = ps[:, 0:128].rearrange("p (k d) -> p k d", k=2)
            w = ready["yB_src"]
            a = copyA(kd[:, tb, :, 0, :], k, t, w)
            a = copyA(kd[:, tb, :, 1, :], k, t, w)
            a = copyA(vv[:, tb, :], ps[:, 128:256], t, w)
            note("c_kv", a)
            return a

        win(6144, 256, ev_kv, ("yB_src",))
        for s in range(2):
            win(5120 + 512 * s, 512, ev_copy(
                lambda tb, s=s: q_n[:, tb, 4 * s:4 * s + 4, :].rearrange("p a b -> p (a b)"), ("yB_src",), "c_q"))
        for s in range(2):
            win(6400 + 512 * s, 512, ev_sig(lambda tb, s=s: c_g[:, tb, 512 * s:512 * s + 512], "silu", ("yB_src",), "c_g"))

        band = at("band", oR1, [128, 16, 256])
        pb1 = at("pb1", oR1 + 16 * KB, [128, 4, 384])
        pt1 = at("pt1", oR1 + 22 * KB, [128, 2, 384])

        def side_c():
            while "c_q" not in ready or "c_kv" not in ready:
                yield False
            tt_ = []
            for fb in range(0, 10, 2):
                bs = yield from take_n(2)
                for i in range(2):
                    for tb in range(2):
                        f = fb + i
                        s = q_n[:, tb, f, :] if f < 8 else kd[:, tb, f - 8, :, :].rearrange("p a b -> p (a b)")
                        t = tr(banks[bs[i]][:, tb * 128:(tb + 1) * 128], s, ready["c_q"], ready["c_kv"],
                               sidefree[bs[i]], sig=tb == 1)
                yield True
                for i in range(2):
                    f = fb + i
                    dst = q_n[:, :, f, :] if f < 8 else kd[:, :, f - 8, :, :].rearrange("p t a b -> p t (a b)")
                    tv = copyA(dst, banks[bs[i]][:, 0:256].rearrange("p (t c) -> p t c", t=2), t)
                    give(bs[i], tv)
                    tt_.append(tv)
            while "yD" not in ready or "scr_band" not in ready or "c_g" not in ready:
                yield False
            src = bass.AP(tensor=scr_band.tensor, offset=127, ap=[[6143, 128], [384, 16], [1, 256]])
            ready["band"] = Q.dma("G", band[:, :, :], src, slot(), ready["scr_band"], ready["yD_src"])
            ready["c_qk"] = tt_
            yield True

        def side_c_heads(u):
            while "band" not in ready:
                yield False
            tt_, tb_ = ready["c_qk"], ready["band"]
            pb, pt, sx = pbs[u], pts[u], smx[:, u, :, :]
            pfree = [ready["yD_src"], ready["swT_free"], ready["swn_free"]]
            ptfree = pfree
            for g in (u, u + 2):
                tl = []
                for hp in range(2):
                    bs = yield from take_n(2)
                    for i in range(2):
                        h = 4 * g + 2 * hp + i
                        kv, fb, off = h // 8, h // 2, (h % 2) * 64
                        b = bs[i]
                        mm(banks[b][:, 0:128], q_n[off:off + 64, 0, fb, :],
                           kd[off:off + 64, 0, kv, :, :].rearrange("p a b -> p (a b)"), True, True, tt_, sidefree[b])
                        t = mm(banks[b][:, 128:384], q_n[off:off + 64, 1, fb, :],
                               kd[off:off + 64, :, kv, :, :].rearrange("p t a b -> p t (a b)"), True, True, sig=True)
                    yield True
                    for i in range(2):
                        hh = 2 * hp + i
                        h = 4 * g + hh
                        b = bs[i]
                        tl.append(stt(pb[:, hh, 0:128], banks[b][:, 0:128], 0.125, band[:, h, 128:256],
                                      ALU.mult, ALU.add, t, tb_, pfree))
                        tv = stt(pb[:, hh, 128:384], banks[b][:, 128:384], 0.125, band[:, h, :],
                                 ALU.mult, ALU.add, t, tb_, pfree)
                        tl.append(tv)
                        give(b, tv)
                m = sx[:, 0, :].rearrange("p (b h) -> p b h", b=2)
                t1 = V(lambda e, m=m: e.tensor_reduce(m[:, 0, :], pb[:, :, 0:128], AX, ALU.max), tl, pfree, n=512)
                t2 = V(lambda e, m=m: e.tensor_reduce(m[:, 1, :], pb[:, :, 128:384], AX, ALU.max), tl, n=1024)
                sk = snk[:, 4 * g:4 * g + 4].unsqueeze(1).broadcast_to([128, 2, 4])
                t3 = tt(m, m, sk, ALU.max, t1, t2, tsk)
                t4 = ts1(sx[:, 1, :], sx[:, 0, :], -1.0, ALU.mult, t3)
                t5 = tt(sx[:, 3, :].rearrange("p (b h) -> p b h", b=2), sk, m, ALU.subtract, t3)
                te = []
                for bq in range(2):
                    for hh in range(4):
                        p = pb[:, hh, 0:128] if bq == 0 else pb[:, hh, 128:384]
                        n = 4 * bq + hh
                        te.append(act(p, p, ACT.Exp, t4, bias=sx[:, 1, n:n + 1], scale=1.0,
                                      accum_out=sx[:, 2, n:n + 1]))
                te.append(act(sx[:, 3, :], sx[:, 3, :], ACT.Exp, t5))
                yield True
                t6 = tt(sx[:, 2, :], sx[:, 2, :], sx[:, 3, :], ALU.add, te)
                t7 = V(lambda e: e.reciprocal(sx[:, 4, :], sx[:, 2, :]), t6)
                bo = yield from take()
                for hp in range(2):
                    bs = yield from take_n(2)
                    for i in range(2):
                        hh = 2 * hp + i
                        for c in range(3):
                            t = tr(banks[bs[i]][:, c * 128:(c + 1) * 128], pb[:, hh, c * 128:(c + 1) * 128], te,
                                   sidefree[bs[i]], sig=c == 2)
                    yield True
                    ta = []
                    for i in range(2):
                        ta.append(copyA(pt[:, i, :], banks[bs[i]][:, 0:384], t, ptfree))
                        give(bs[i], ta[i])
                    yield True
                    for i in range(2):
                        hh = 2 * hp + i
                        kv = (4 * g + hh) // 8
                        vk = slice(kv * 64, kv * 64 + 64)
                        o1 = banks[bo][:, hh * 64:hh * 64 + 64]
                        o2 = banks[bo][:, 256 + hh * 64:256 + hh * 64 + 64]
                        mm(o1, pt[:, i, 0:128], vv[:, 0, vk], True, True, ta[i], sidefree[bo], ready["c_kv"])
                        mm(o2, pt[:, i, 128:256], vv[:, 0, vk], True, False)
                        t = mm(o2, pt[:, i, 256:384], vv[:, 1, vk], False, True, sig=True)
                    ptfree = t
                yield True
                for bq in range(2):
                    ob = banks[bo][:, 256 * bq:256 * bq + 256].rearrange("p (h d) -> p h d", h=4)
                    ri = sx[:, 4, 4 * bq:4 * bq + 4].unsqueeze(2).broadcast_to([128, 4, 64])
                    od = pb[:, bq, 0:256].rearrange("p (h d) -> p h d", h=4)
                    tv = tt(od, ob, ri, ALU.mult, t, t7)
                    cg = c_g[:, bq, 256 * g:256 * g + 256]
                    r = tt(cg, cg, pb[:, bq, 0:256], ALU.mult, tv, ready["c_g"])
                    note("c_o", r)
                give(bo, tv)
                pfree = r
                yield True

        def side_c_end():
            while "c_o" not in ready:
                yield False
            yield from to_yT(lambda tb: c_g[:, tb, :], "yC", ready["c_o"], "mD")

        key_n["c_o"] = 8
        pbs = [pb1, at("pb2", oS1, [128, 4, 384])]
        pts = [pt1, at("pt2", oSW, [128, 2, 384])]
        sides.append(side_c())
        sides.append(side_c_heads(0))
        sides.append(side_c_heads(1))
        sides.append(side_c_end())
        ada_rate[0] = ADA_RATE["merge_D"]
        merge(3, "D")
        ada_rate[0] = ADA_RATE["merge_C"]
        merge(2, "C")
        while adaq[0][0]["two"]:
            ada_some(1)

        ada_rate[0] = ADA_RATE["w_out"]
        mh = at("mh", oFX, [128, 16, 256], F32R)
        ml = at("ml", oFX + 16 * KB, [128, 16, 256], F32R)
        x1 = at("x1", oR2, [128, 2, 2048])
        lnr = [at("lnr0", oS1, [128, 2048]), at("lnr1", oSW, [128, 2048])]

        def side_m():
            while "mC" not in ready:
                yield False
            toks = []
            w = ready["mC"]
            for kp in range(8):
                b = yield from take()
                for k in range(2):
                    for tb in range(2):
                        kt = 2 * kp + k
                        t = tr(banks[b][:, (2 * k + tb) * 128:(2 * k + tb + 1) * 128],
                               merged[:, tb, kt * 128:(kt + 1) * 128], w, sidefree[b], sig=(k == 1 and tb == 1))
                h = mh[:, 2 * kp:2 * kp + 2, :].rearrange("p a b -> p (a b)")
                l = ml[:, 2 * kp:2 * kp + 2, :].rearrange("p a b -> p (a b)")
                ta = copyA(h, banks[b][:, :], t)
                tv = tt(l, banks[b][:, :], f32(h), ALU.subtract, ta)
                toks += [ta, tv]
                give(b, tv)
                ready[("mT", 2 * kp)] = ready[("mT", 2 * kp + 1)] = [ta, tv]
                yield True
            ready["mT"] = toks
            ready["merged_free"] = t
            yield True

        def side_x():
            while "yC_src" not in ready:
                yield False
            s = slot()
            ready["x_again"] = Q.dma("G", x1[:, :, :], xv, s, ready["yC_src"])
            yield True

        sides.append(side_x())
        sides.append(side_m())

        def stm(kt, tb):
            return (mh[:, kt, tb * 128:(tb + 1) * 128], ml[:, kt, tb * 128:(tb + 1) * 128])

        key_n["z"] = 8
        for n in range(4):
            def evz(tb, ps, t, n=n):
                d = x1[:, tb, n * 512:(n + 1) * 512]
                r = stt(d, d, ALPHA, ps, ALU.mult, ALU.add, t, ready["x_again"])
                r2 = V(lambda e: e.bn_stats(stz[:, tb, n, :], d), r, n=512)
                note("z", [r, r2, t])
                return r
            gemm(I["w_out"][0, :, n * 512:(n + 1) * 512], list(range(16)), 512, stm, (0, 1), evz, (),
                 ktneed={kt: ("mT", kt) for kt in range(16)} if n == 0 else None, evneed=("x_again",), ahead=AHEAD)

        mod_keys = [("mod", 0, n) for n in range(4)] + [("mod", 1, n) for n in range(4)]

        def diag(dst, r, *w):
            return V(lambda e: e.tensor_scalar(dst, ident[:, :], r, None, ALU.mult), *w, n=128)

        def to_hT(src, tok, dg, Ac, Bc, hi, lo, tbs, war, key=None):
            toks = []
            nb = len(tbs)
            for kp in range(8):
                b = yield from take()
                for k in range(2):
                    for x, tb in enumerate(tbs):
                        kt = 2 * kp + k
                        t = mm(banks[b][:, (nb * k + x) * 128:(nb * k + x + 1) * 128],
                               src(tb)[:, kt * 128:(kt + 1) * 128], dg(tb), True, True, tok, sidefree[b],
                               sig=(k == 1 and x == nb - 1))
                w = nb * 128
                g = kp % 2
                for k in range(2):
                    kt = 2 * kp + k
                    tv = ts(sg[:, g, k * w:(k + 1) * w], banks[b][:, k * w:(k + 1) * w], Ac[:, kt:kt + 1],
                            Bc[:, kt:kt + 1], ALU.mult, ALU.add, t, sgfree[g])
                give(b, tv)
                s = sg[:, g, 0:2 * w].rearrange("p (k c) -> p k c", k=2)
                h = hi[:, 2 * kp:2 * kp + 2, tbs[0] * 128:tbs[0] * 128 + w]
                l = lo[:, 2 * kp:2 * kp + 2, tbs[0] * 128:tbs[0] * 128 + w]
                ta = copyA(h, s, tv, war)
                tl = tt(l, s, f32(h), ALU.subtract, ta, tv, war)
                sgfree[g] = tl
                toks += [ta, tl]
                if key:
                    ready[(key, 2 * kp)] = ready[(key, 2 * kp + 1)] = [ta, tl]
                yield True
            return toks, t

        hch = at("hch", oFY, [128, 16, 256], F32R)
        hcl = at("hcl", oFY + 16 * KB, [128, 16, 256], F32R)
        hxh, hxl = mh, ml
        acx = small("acx", [128, 2, 16])
        ctn = at("ctn", oR1, [128, 2048])
        sqt = at("sqt", oR1 + 8 * KB, [128, 2048])
        dgc = at("dgc", oR1 + 16 * KB, [128, 128])
        dgx = at("dgx", oR1, [128, 2, 128])

        def side_hc():
            while "yC_src" not in ready or "merged_free" not in ready or "mC" not in ready \
                    or any(k not in ready for k in mod_keys):
                yield False
            tm = [ready[k] for k in mod_keys]
            ga = par[:, col["ga"]:col["ga"] + 16]
            a1 = stt(acx[:, 0, :], mod[:, 1, :], 1.0, ga, ALU.add, ALU.mult, tm, ready["ex_free"])
            a2 = stt(acx[:, 1, :], mod[:, 3, :], 1.0, ga, ALU.add, ALU.mult, tm, ready["ex_free"])
            ready["acx"] = [a1, a2]
            s = slot()
            free = ready["yC_src"]
            alltoks = []
            for tb in range(2):
                tc = Q.dma("G", ctn[:, :], I["ctx_2"][0, tb * 128:(tb + 1) * 128, :], s, free, alltoks)
                yield True
                yield True
                t = act(sqt[:, :], ctn[:, :], ACT.Square, tc, stfree[0], accum_out=rs[:, 1:2])
                t = rstd(rs[:, 2:3], rs[:, 1:2], 1.0 / 2048, EPS_RMS, t)
                t = diag(dgc[:, :], rs[:, 2:3], t, free)
                stfree[0] = t
                yield True
                tk, free = yield from to_hT(lambda _: ctn[:, :], [t, tc], lambda _: dgc[:, :],
                                            acx[:, 1, :], mod[:, 2, :], hch, hcl, (tb,),
                                            [ready["merged_free"], ready["mC"], ready["acx"]])
                alltoks += tk
            ready["hc"] = alltoks
            ready["ctn_free"] = [free, t]

        def side_ln1():
            while "yC_src" not in ready:
                yield False
            ready["lnr"] = [Q.dma("G", lnr[i][:, :], I[n][0].partition_broadcast(128), slot(), ready["yC_src"],
                                  ready["ex_free"]) for i, n in enumerate(("ln_g", "ln_b"))]
            yield True

        def side_x1():
            while any(k not in ready for k in ("z", "lnr", "acx", "ctn_free")):
                yield False
            tl = []
            ta = []
            for tb in range(2):
                x = x1[:, tb, :]
                m = mvz[:, tb, :]
                t = V(lambda e, tb=tb: e.bn_aggr(mvz[:, tb, :], stz[:, tb, :, :].rearrange("p a b -> p (a b)")),
                      ready["z"])
                t = rstd(rs[:, 2 + tb:3 + tb], m[:, 1:2], 1.0, EPS_LN, t)
                ta.append(t)
            for tb in range(2):
                x = x1[:, tb, :]
                t = stt(x, x, mvz[:, tb, 0:1], lnr[0][:, :], ALU.subtract, ALU.mult, ta, ready["lnr"], ready["z"])
                t = stt(x, x, rs[:, 2 + tb:3 + tb], lnr[1][:, :], ALU.mult, ALU.add, t)
                tl.append(t)
            td = Q.dma("S", scr_x1, x1[:, :, :], slot(), tl)
            ready["scr_x1"] = td
            yield True
            tn_ = []
            for tb in range(2):
                t = act(lnr[tb][:, :], x1[:, tb, :], ACT.Square, tl, accum_out=rs[:, 4 + tb:5 + tb])
                t = rstd(rs[:, 6 + tb:7 + tb], rs[:, 4 + tb:5 + tb], 1.0 / 2048, EPS_RMS, t)
                tn_.append(diag(dgx[:, tb, :], rs[:, 6 + tb:7 + tb], t, ready["ctn_free"]))
            yield True
            tk, t = yield from to_hT(lambda tb: x1[:, tb, :], [tn_, tl], lambda tb: dgx[:, tb, :],
                                     acx[:, 0, :], mod[:, 0, :], hxh, hxl, (0, 1),
                                     [ready["z"], ready["acx"]], "hx")
            ready["x1_done"] = tk
            ready["hx"] = tk
            ready["r12_free"] = [t, tn_, td]

        sides.append(side_hc())
        sides.append(side_ln1())
        sides.append(side_x1())

        W2 = I["w_in_2"][0]

        def st2(kt, tb):
            if tb < 2:
                return (hxh[:, kt, tb * 128:(tb + 1) * 128], hxl[:, kt, tb * 128:(tb + 1) * 128])
            return (hch[:, kt, (tb - 2) * 128:(tb - 1) * 128], hcl[:, kt, (tb - 2) * 128:(tb - 1) * 128])

        def win2(c0, n, tbs, evac, need=("hx", "hc"), ktneed=None):
            gemm(W2[:, c0:c0 + n], list(range(16)), n, st2, tbs, evac, need, ktneed=ktneed, ahead=AHEAD)

        XT, ALL = (0, 1), (0, 1, 2, 3)
        ada_rate[0] = ADA_RATE["ctx"]
        ot = at("ot", oSW, [128, 8, 256])
        nb_ = [at(f"nab{i}", oR2 + (12 + 2 * i) * KB, [128, 2, 4, 64]) for i in range(2)]
        pp = at("pp", oR1 + 20 * KB, [128, 2, 512])
        rt = at("rt", oR1 + 24 * KB, [128, 512])
        streams = [dict(pp=pp, pT=at("pT", oSG, [128, 4, 256]), sx=sm5[:, 0, :], pf=None, tf=None, busy=False),
                   dict(pp=at("ppb", oS1, [128, 2, 512]), pT=at("pTb", oS1 + 4 * KB, [128, 4, 256]), sx=sm5[:, 1, :],
                        pf=None, tf=None, busy=False)]
        oh = at("oh", oFX, [128, 16, 256], F32R)
        ol = at("ol", oFX + 16 * KB, [128, 16, 256], F32R)

        M0, M1 = oR1, oR2
        na_q = at("na_q", M0, [128, 2, 4, 128])
        na_k = at("na_k", M0 + 4 * KB, [128, 4, 4, 128])
        na_v = at("na_v", M0 + 12 * KB, [128, 4, 512])
        gq_q = at("gq_q", M1, [128, 2, 4, 128])
        gq_kv = at("gq_kv", M1 + 4 * KB, [128, 4, 4, 128])
        ml_q = at("ml_q", M0, [128, 2, 512])
        ml_c = at("ml_c", M0 + 4 * KB, [128, 4, 320])
        cqh = at("cqh", M0 + 9 * KB, [128, 4, 256], F32R)
        cql = at("cql", M0 + 13 * KB, [128, 4, 256], F32R)
        ckh = at("ckh", M0, [128, 2, 512], F32R)
        ckl = at("ckl", M0 + 4 * KB, [128, 2, 512], F32R)
        kpT = at("kpT", M0 + 17 * KB, [64, 512])
        df_q = at("df_q", M1, [128, 2, 4, 128])
        df_k = at("df_k", M1 + 4 * KB, [128, 4, 4, 128])
        df_v = at("df_v", M1 + 12 * KB, [128, 4, 512])
        mq = at("mq", oFY, [128, 2, 768])
        mkv = at("mkv", oFY + 6 * KB, [128, 4, 1024])
        mqp = at("mqp", oFY + 22 * KB, [64, 4, 256])

        def flat(ap):
            return ap.rearrange("p a b -> p (a b)")

        def cp(view, key, n, war):
            key_n[key] = n
            return ev_copy(view, war, key)

        CT = (2, 3)
        cp_k = lambda n: cp(lambda tb: flat(na_k[:, tb, :, :]), "na_k", n, ("ctn_free",))
        cp_v = lambda n: cp(lambda tb: na_v[:, tb, :], "na_v", n, ("ctn_free",))
        win2(512, 512, CT, cp_k(4), ("hc", "ctn_free"))
        win2(1024, 512, CT, cp_v(4), ("hc", "ctn_free"))
        ada_rate[0] = ADA_RATE["na_q"]
        win2(0, 512, XT, cp(lambda tb: flat(na_q[:, tb, :, :]), "na_q", 2, ("ctn_free",)), (),
             {kt: ("hx", kt) for kt in range(16)})
        ada_rate[0] = ADA_RATE["strips"]
        win2(512, 512, XT, cp_k(4))
        win2(1024, 512, XT, cp_v(4))
        win2(1536, 512, XT, cp(lambda tb: flat(gq_q[:, tb, :, :]), "gq_q", 2, ("r12_free",)))
        win2(2048, 512, ALL, cp(lambda tb: flat(gq_kv[:, tb, :, :]), "gq_kv", 4, ("r12_free",)))
        win2(2560, 512, XT, cp(lambda tb: ml_q[:, tb, :], "ml_q", 2, ("o_na",)), ("hx", "hc", "o_na"))
        win2(3072, 320, ALL, cp(lambda tb: ml_c[:, tb, :], "ml_c", 4, ("o_na",)))
        win2(3392, 512, XT, cp(lambda tb: flat(df_q[:, tb, :, :]), "df_q", 2, ("o_gq", "o_na")), ("o_gq", "o_na"))
        win2(3904, 512, ALL, cp(lambda tb: flat(df_k[:, tb, :, :]), "df_k", 4, ("o_gq",)))
        win2(4416, 512, ALL, cp(lambda tb: df_v[:, tb, :], "df_v", 4, ("o_gq",)))

        ada_rate[0] = ADA_RATE["mla"]
        def stq(kt, tb):
            return (cqh[:, kt, tb * 128:(tb + 1) * 128], cql[:, kt, tb * 128:(tb + 1) * 128])

        def stk(kt, tb):
            return (ckh[:, kt, tb * 128:(tb + 1) * 128], ckl[:, kt, tb * 128:(tb + 1) * 128])

        gemm(I["mla_wukv_2"][0][:, 0:512], [0, 1], 512, stk, ALL,
             cp(lambda tb: mkv[:, tb, 0:512], "mkv0", 4, ("df_v",)), ("ml_T", "df_v"))
        gemm(I["mla_wukv_2"][0][:, 512:1024], [0, 1], 512, stk, ALL,
             cp(lambda tb: mkv[:, tb, 512:1024], "mkv1", 4, ("df_v",)))
        gemm(I["mla_wuq_2"][0][:, 0:512], [0, 1, 2, 3], 512, stq, XT,
             cp(lambda tb: mq[:, tb, 0:512], "mq0", 2, ("df_v",)))
        gemm(I["mla_wuq_2"][0][:, 512:768], [0, 1, 2, 3], 256, stq, XT,
             cp(lambda tb: mq[:, tb, 512:768], "mq1", 2, ("df_v",)))

        def in_place(blocks, tok):
            toks = []
            for i in range(0, len(blocks), 2):
                pair = blocks[i:i + 2]
                bs = yield from take_n(len(pair))
                for b, (src, dst) in zip(bs, pair):
                    n = len(src)
                    for x, s in enumerate(src):
                        t = tr(banks[b][0:s.shape[1], x * 128:(x + 1) * 128], s, tok, sidefree[b], sig=x == n - 1)
                yield True
                for k, (b, (src, dst)) in enumerate(zip(bs, pair)):
                    n, r = len(src), src[0].shape[1]
                    tv = copyA(dst, banks[b][0:r, 0:n * 128].rearrange("p (t c) -> p t c", t=n), t)
                    give(b, tv)
                    toks.append(tv)
            return toks

        rtfree = [None]

        def rope(x, cs, d, tok):
            g = x.shape[1]
            hd = d // 2
            tmp = rt[:, 0:g * d].rearrange("p (g d) -> p g d", g=g)
            s1 = cs[:, 1, 0:hd].unsqueeze(1).broadcast_to([128, g, hd])
            s2 = cs[:, 1, hd:d].unsqueeze(1).broadcast_to([128, g, hd])
            co = cs[:, 0, 0:d].unsqueeze(1).broadcast_to([128, g, d])
            a = tt(tmp[:, :, 0:hd], x[:, :, hd:d], s1, ALU.mult, tok, rtfree[0], ready["rope"])
            b = tt(tmp[:, :, hd:d], x[:, :, 0:hd], s2, ALU.mult, tok)
            c = tt(x, x, co, ALU.mult, a, b)
            r = tt(x, x, tmp, ALU.add, c)
            rtfree[0] = r
            return r

        def head_norm(x, g, grow_, tok, w):
            tmp = rt[:, 0:g * 128].rearrange("p (g d) -> p g d", g=g)
            a = tt(tmp, x, x, ALU.mult, tok, rtfree[0])
            c = V(lambda e: e.tensor_reduce(rs[:, w:w + g], tmp, AX, ALU.add), a)
            t = rstd(rs[:, w:w + g], rs[:, w:w + g], 1.0 / 128, EPS_RMS, c)
            r = None
            for h in range(g):
                r = stt(x[:, h, :], x[:, h, :], rs[:, w + h:w + h + 1], grow_, ALU.mult, ALU.mult, t, ready["grow"])
            rtfree[0] = r
            return r

        def softmax(S, bs, t, scale, bias=None):
            pp, sx, pf = S["pp"], S["sx"], [S["pf"], ready["x1_done"]]
            src = [banks[b][:, :] for b in bs]
            lt = [t, t]
            if bias is not None:
                for x in range(2):
                    r0 = stt(pp[:, x, 0:256], src[x][:, 0:256], scale, bias[x], ALU.mult, ALU.add, t, pf)
                    r1 = ts1(pp[:, x, 256:512], src[x][:, 256:512], scale, ALU.mult, t, pf)
                    give(bs[x], r1)
                    src[x] = pp[:, x, :]
                    lt[x] = [r0, r1]
            for x in range(2):
                lt[x] = V(lambda e, x=x: e.tensor_reduce(sx[:, x:x + 1], src[x], AX, ALU.max), lt[x], pf, n=512)
            sc = 1.0 if bias is not None else scale
            tn_ = ts1(sx[:, 2:4], sx[:, 0:2], -sc, ALU.mult, lt)
            te = []
            for x in range(2):
                te.append(act(pp[:, x, :], src[x], ACT.Exp, tn_, pf, bias=sx[:, 2 + x:3 + x], scale=sc,
                              accum_out=sx[:, 4 + x:5 + x]))
                if bias is None:
                    give(bs[x], te[-1])
            yield True
            return V(lambda e: e.reciprocal(sx[:, 6:8], sx[:, 4:6]), te)

        def pT_copy(S, x, b, t):
            ta = copyA(S["pT"][:, :, x * 128:(x + 1) * 128], banks[b][:, :].rearrange("p (c q) -> p c q", c=4), t,
                       S["tf"], sgfree, ready["x1_done"])
            give(b, ta)
            return ta

        def pT_trans(b, src, tok):
            for c in range(4):
                t = tr(banks[b][:, c * 128:(c + 1) * 128], src[:, c * 128:(c + 1) * 128], tok, sidefree[b], sig=c == 3)
            return t

        def grab():
            while True:
                for S in streams:
                    if not S["busy"]:
                        S["busy"] = True
                        return S
                yield False

        def attend(pairs, scale, vcols, dest, w, bias=None):
            S = yield from grab()
            bs = yield from take_n(2)
            for x in range(2):
                pr = pairs(x)
                for n, (l, r) in enumerate(pr):
                    t = mm(banks[bs[x]][:, :], l, r, n == 0, n == len(pr) - 1, w, sidefree[bs[x]],
                           sig=n == len(pr) - 1)
            yield True
            tr_ = yield from softmax(S, bs, t, scale, bias)
            pp, sx = S["pp"], S["sx"]
            tn_ = [ts1(pp[:, x, :], pp[:, x, :], sx[:, 6 + x:7 + x], ALU.mult, tr_) for x in range(2)]
            bs = yield from take_n(2)
            yield True
            tl = [pT_trans(bs[x], pp[:, x, :], tn_[x]) for x in range(2)]
            S["pf"] = tl[1]
            yield True
            tp_ = [pT_copy(S, x, bs[x], tl[x]) for x in range(2)]
            yield True
            b = yield from take()
            for c in range(4):
                t = mm(banks[b][:, 0:256], vcols(c), S["pT"][:, c, :], c == 0, c == 3, tp_, sidefree[b], sig=c == 3)
            S["tf"] = t
            S["busy"] = False
            yield True
            give(b, dest(banks[b][:, 0:256], t))
            yield True

        def dest_ot(h):
            def f(ps, t):
                r = copyA(ot[:, h, :], ps, t)
                ready[("ot", h)] = r
                return r
            return f

        def dest_oT(h):
            def f(ps, t):
                a = copyA(oh[:, h, :], ps, t, ready["df_v"])
                r = tt(ol[:, h, :], ps, f32(oh[:, h, :]), ALU.subtract, a, t, ready["df_v"])
                ready[("oT", h)] = [a, r]
                return r
            return f

        def side_tables():
            while "cw_free" not in ready:
                yield False
            s = [slot() for _ in range(6)]
            w = ready["cw_free"]
            ready["rope"] = [
                Q.dma("G", ropeA[:, :, :, :].rearrange("p t a b -> p t (a b)"),
                      I["k_rope128"].rearrange("(t p) a b -> p t (a b)", p=128), s[0], w),
                Q.dma("G", ropeB[:, :, :, :].rearrange("p t a b -> p t (a b)"),
                      I["k_rope64"].rearrange("(t p) a b -> p t (a b)", p=128), s[1], w)]
            tg = [Q.dma("G", grow[:, i, :], I[n][0].partition_broadcast(128), s[2 + i])
                  for i, n in enumerate(("gqa_gq_2", "gqa_gk_2", "diff_gsub_2"))]
            tm = ts1(grow[:, 2, :], grow[:, 2, :], 1.0 - LAM0, ALU.mult, tg)
            ready["grow"] = [tg, tm]
            ready["nam"] = Q.dma("G", nam[:, :], I["k_namask"], s[5])
            yield True

        def all_done(key, part, hs):
            if all((part, h) in ready for h in hs):
                ready[key] = [ready[(part, h)] for h in hs]

        def spawn(heads):
            sides.extend([heads(0), heads(1)])

        def side_na():
            while any(k not in ready for k in ("na_q", "na_k", "nam", "r12_free", "x1_done")):
                yield False
            snav = scr_na.tensor

            def load_bias(h):
                n = h % 2
                toks = []
                for r in range(4):
                    src = bass.AP(tensor=snav, offset=(h * 15 + 7 - r) * 128 + 63,
                                  ap=[[P60 - 1, 64], [128, 4], [1, 64]])
                    toks.append(Q.dma("G", nb_[n][(r % 2) * 64:(r % 2) * 64 + 64, r // 2, :, :], src, nbs[n][r],
                                      ready["scr_na"], nbfree[n]))
                v = nb_[n][:, :, :, :].rearrange("p a b c -> p (a b) c")
                return tt(v, v, nam[:, :].unsqueeze(1).broadcast_to([128, 8, 64]), ALU.add, toks, ready["nam"])

            nbs = [[slot() for _ in range(4)] for _ in range(2)]
            nbfree = [ready["r12_free"]] * 2
            tq = yield from in_place([([na_q[:, tb, h, :] for tb in XT], na_q[:, :, h, :]) for h in range(4)],
                                     ready["na_q"])
            tk = yield from in_place([([na_k[:, tb, h, :] for tb in ALL], na_k[:, :, h, :]) for h in range(4)],
                                     ready["na_k"])
            while "na_v" not in ready:
                yield False

            def heads(u):
                for h in (u, u + 2):
                    tb_ = load_bias(h)
                    yield True
                    bias = [nb_[u][:, x, :, :].rearrange("p a b -> p (a b)") for x in range(2)]
                    yield from attend(lambda x: [(na_q[:, x, h, :], na_k[:, :, h, :])], 128 ** -0.5,
                                      lambda c: na_v[:, c, h * 128:(h + 1) * 128], dest_ot(h),
                                      [tq, tk, tb_, ready["na_v"]], bias)
                    nbfree[u] = ready[("ot", h)]
                all_done("o_na", "ot", range(4))

            spawn(heads)

        def side_gq():
            while any(k not in ready for k in ("gq_q", "gq_kv", "x1_done", "rope", "grow")):
                yield False
            tq = []
            for tb in XT:
                t = head_norm(gq_q[:, tb, :, :], 4, grow[:, 0, :], ready["gq_q"], 0)
                tq.append(rope(gq_q[:, tb, :, :], ropeA[:, tb, :, :], 128, t))
                yield True
            tk = []
            for tb in ALL:
                t = head_norm(gq_kv[:, tb, 0:2, :], 2, grow[:, 1, :], ready["gq_kv"], 4)
                if tb < 2:
                    t = rope(gq_kv[:, tb, 0:2, :], ropeA[:, tb, :, :], 128, t)
                tk.append(t)
                yield True
            tq = yield from in_place([([gq_q[:, tb, h, :] for tb in XT], gq_q[:, :, h, :]) for h in range(4)], tq)
            tk = yield from in_place([([gq_kv[:, tb, h, :] for tb in ALL], gq_kv[:, :, h, :]) for h in range(2)], tk)

            def heads(u):
                for h in (u, u + 2):
                    yield from attend(lambda x: [(gq_q[:, x, h, :], gq_kv[:, :, h // 2, :])], 128 ** -0.5,
                                      lambda c: gq_kv[:, c, 2 + h // 2, :], dest_ot(4 + h),
                                      [tq, tk, ready["gq_kv"]])
                all_done("o_gq", "ot", range(4, 8))

            spawn(heads)

        def side_ml1():
            while any(k not in ready for k in ("ml_q", "ml_c", "o_na", "rope")):
                yield False
            tq = []
            for tb in XT:
                a = act(rt[:, :], ml_q[:, tb, :], ACT.Square, ready["ml_q"], rtfree[0], accum_out=rs[:, 8 + tb:9 + tb])
                rtfree[0] = a
                t = rstd(rs[:, 8 + tb:9 + tb], rs[:, 8 + tb:9 + tb], 1.0 / 512, EPS_RMS, a)
                tq.append(ts1(ml_q[:, tb, :], ml_q[:, tb, :], rs[:, 8 + tb:9 + tb], ALU.mult, t))
            yield True
            tc = []
            for tb in ALL:
                x = ml_c[:, tb, 0:256]
                a = act(rt[:, 0:256], x, ACT.Square, ready["ml_c"], rtfree[0], accum_out=rs[:, 10 + tb:11 + tb])
                rtfree[0] = a
                t = rstd(rs[:, 10 + tb:11 + tb], rs[:, 10 + tb:11 + tb], 1.0 / 256, EPS_RMS, a)
                tc.append(ts1(x, x, rs[:, 10 + tb:11 + tb], ALU.mult, t))
                if tb < 2:
                    tc.append(rope(ml_c[:, tb, 256:320].unsqueeze(1), ropeB[:, tb, :, :], 64, ready["ml_c"]))
                yield True
            toks = []
            for kp in range(2):
                b = yield from take()
                for k in range(2):
                    for tb in XT:
                        kt = 2 * kp + k
                        t = tr(banks[b][:, (2 * k + tb) * 128:(2 * k + tb + 1) * 128], ml_q[:, tb, kt * 128:(kt + 1) * 128],
                               tq, sidefree[b], sig=(k == 1 and tb == 1))
                yield True
                def gk(k):
                    kt = 2 * kp + k
                    return kt, par[:, col["mq"] + kt:col["mq"] + kt + 1], banks[b][:, k * 256:(k + 1) * 256]

                a = []
                for k in range(2):
                    kt, g, ps = gk(k)
                    a.append(act(cqh[:, kt, :], ps, ACT.Copy, t, ready["o_na"], scale=g))
                for k in range(2):
                    kt, g, ps = gk(k)
                    r = stt(cql[:, kt, :], ps, g, f32(cqh[:, kt, :]), ALU.mult, ALU.subtract, a, t)
                    toks += [a[k], r]
                give(b, r)
            tq_done = t
            yield True
            bs = yield from take_n(3)
            for kt in range(3):
                b = bs[kt]
                w = 64 if kt == 2 else 128
                for tb in ALL:
                    t = tr(banks[b][0:w, tb * 128:(tb + 1) * 128], ml_c[:, tb, kt * 128:kt * 128 + w],
                           tc, sidefree[b], sig=tb == 3)
            yield True
            for kt in range(2):
                g = par[:, col["mk"] + kt:col["mk"] + kt + 1]
                ps = banks[bs[kt]][:, :]
                a = act(ckh[:, kt, :], ps, ACT.Copy, t, tq_done, scale=g)
                r = stt(ckl[:, kt, :], ps, g, f32(ckh[:, kt, :]), ALU.mult, ALU.subtract, a, t)
                toks += [a, r]
                give(bs[kt], r)
            a = copyA(kpT[:, :], banks[bs[2]][0:64, :], t)
            give(bs[2], a)
            toks.append(a)
            ready["ml_T"] = toks
            yield True

        def side_df():
            while any(k not in ready for k in ("df_q", "df_k", "o_gq", "rope", "lam", "ml_T")):
                yield False
            tq, tk = [], []
            for tb in XT:
                tq.append(rope(df_q[:, tb, :, :].rearrange("p h (i d) -> p (h i) d", i=2), ropeB[:, tb, :, :], 64,
                               ready["df_q"]))
                yield True
                tk.append(rope(df_k[:, tb, :, :].rearrange("p h (i d) -> p (h i) d", i=2), ropeB[:, tb, :, :], 64,
                               ready["df_k"]))
                yield True
            tq = yield from in_place([([df_q[:, tb, h, :] for tb in XT], df_q[:, :, h, :]) for h in range(4)], tq)
            tk = yield from in_place([([df_k[:, tb, h, :] for tb in ALL], df_k[:, :, h, :]) for h in range(4)],
                                     [tk, ready["df_k"]])
            while "df_v" not in ready:
                yield False

            def heads(u):
                for h in (u, u + 2):
                    S = yield from grab()
                    pp, sx = S["pp"], S["sx"]
                    bo = yield from take()
                    for x in range(2):
                        bs = yield from take_n(2)
                        for i in range(2):
                            p = slice(64 * i, 64 * i + 64)
                            t = mm(banks[bs[i]][:, :], df_q[p, x, h, :], df_k[p, :, h, :], True, True, tq, tk,
                                   sidefree[bs[i]], sig=True)
                        yield True
                        tr_ = yield from softmax(S, bs, t, 0.125)
                        t1 = tt(sx[:, 8:9], sx[:, 7:8], lamt[:, 0:1], ALU.mult, tr_, ready["lam"])
                        t2 = ts1(pp[:, 0, :], pp[:, 0, :], sx[:, 6:7], ALU.mult, tr_)
                        t3 = stt(pp[:, 0, :], pp[:, 1, :], sx[:, 8:9], pp[:, 0, :], ALU.mult, ALU.add, t1, t2)
                        b = yield from take()
                        yield True
                        tl = pT_trans(b, pp[:, 0, :], t3)
                        S["pf"] = [tl, t3]
                        yield True
                        ta = pT_copy(S, x, b, tl)
                        yield True
                        for c in range(4):
                            t = mm(banks[bo][:, x * 128:(x + 1) * 128], S["pT"][:, c, x * 128:(x + 1) * 128],
                                   df_v[:, c, h * 128:(h + 1) * 128], c == 0, c == 3, ta, ready["df_v"], sidefree[bo],
                                   sig=c == 3)
                        S["tf"] = t
                    yield True
                    tn_ = []
                    a = copyA(pp[:, 0, 0:256], banks[bo][:, 0:256], t, S["pf"])
                    give(bo, a)
                    for x in range(2):
                        o_ = pp[:, 0, x * 128:(x + 1) * 128]
                        s = act(pp[:, 1, x * 128:x * 128 + 128], o_, ACT.Square, a, S["pf"], accum_out=sx[:, 10 + x:11 + x])
                        s = rstd(sx[:, 10 + x:11 + x], sx[:, 10 + x:11 + x], 1.0 / 128, EPS_RMS, s)
                        tn_.append(stt(o_, o_, sx[:, 10 + x:11 + x], grow[:, 2, :], ALU.mult, ALU.mult, s, ready["grow"]))
                    yield True
                    b = yield from take()
                    for x in range(2):
                        t = tr(banks[b][:, x * 128:(x + 1) * 128], pp[:, 0, x * 128:(x + 1) * 128], tn_, sidefree[b], sig=x == 1)
                    S["pf"] = [t, s]
                    S["busy"] = False
                    yield True
                    give(b, dest_oT(12 + h)(banks[b][:, 0:256], t))
                    yield True

            spawn(heads)

        def side_ml2():
            while any(k not in ready for k in ("mkv0", "mkv1", "mq0", "mq1")):
                yield False
            mw = [ready[k] for k in ("mkv0", "mkv1", "mq0", "mq1")]
            tr_ = []
            q4 = mq[:, :, :].rearrange("p t (h e) -> p t h e", h=4)
            k4 = mkv[:, :, :].rearrange("p t (h e) -> p t h e", h=4)
            for tb in XT:
                tr_.append(rope(q4[:, tb, :, 128:192], ropeB[:, tb, :, :], 64, mw))
                yield True
            t1 = yield from in_place([([q4[:, tb, h, 0:128] for tb in XT], q4[:, :, h, 0:128]) for h in range(4)], mw)
            t2 = yield from in_place([([q4[:, tb, h, 128:192] for tb in XT],
                                       mqp[:, h, :].rearrange("p (t c) -> p t c", t=2)) for h in range(4)], tr_)
            t3 = yield from in_place([([k4[:, tb, h, 0:128] for tb in ALL], k4[:, :, h, 0:128]) for h in range(4)], mw)

            def heads(u):
                for h in (u, u + 2):
                    yield from attend(lambda x: [(q4[:, x, h, 0:128], k4[:, :, h, 0:128]),
                                                 (mqp[:, h, x * 128:(x + 1) * 128], kpT[:, :])], 192 ** -0.5,
                                      lambda c: k4[:, c, h, 128:256], dest_oT(8 + h),
                                      [t1, t2, t3, ready["ml_T"], mw])
                all_done("mla_free", "oT", range(8, 12))

            spawn(heads)

        def side_ot():
            while "o_gq" not in ready or "df_v" not in ready:
                yield False
            for h in range(8):
                a = copyA(oh[:, h, :], ot[:, h, :], ready[("ot", h)], ready["df_v"])
                r = tt(ol[:, h, :], ot[:, h, :], f32(oh[:, h, :]), ALU.subtract, a, ready[("ot", h)], ready["df_v"])
                ready[("oT", h)] = [a, r]
                if h % 2:
                    yield True

        sides.append(side_tables())
        sides.append(side_na())
        sides.append(side_gq())
        sides.append(side_ml1())
        sides.append(side_ot())
        sides.append(side_df())
        sides.append(side_ml2())

        x2 = at("x2", oMG, [128, 2, 2048])
        gta = at("gta", oSW, [128, 2, 512])
        x2p = at("x2p", M0, [128, 2, 2048])
        gtfree = [None, None]

        def side_x2():
            while "mla_free" not in ready:
                yield False
            ready["x2"] = Q.dma("G", x2[:, :, :], scr_x1, slot(), ready["scr_x1"], ready["mla_free"])
            yield True

        sides.append(side_x2())

        def sto(kt, tb):
            return (oh[:, kt, tb * 128:(tb + 1) * 128], ol[:, kt, tb * 128:(tb + 1) * 128])

        key_n["x2o"] = 8

        sqj = at("sqj", oFY + 2 * KB, [128, 2, 512])
        sqfree = [None, None]

        def out2(n):
            def ev(tb, ps, t):
                d = x2[:, tb, n * 512:(n + 1) * 512]
                p = x2p[:, tb, n * 512:(n + 1) * 512]
                r0 = tt(sg[:, tb, :], p, ps, ALU.add, t, ready[("x2p", n, tb)], streams[0]["tf"], sgfree[tb])
                r1 = tt(sg[:, tb, :], gta[:, n % 2, :], sg[:, tb, :], ALU.mult, ready[("gta", n)], r0)
                r = tt(d, d, sg[:, tb, :], ALU.add, r1, ready["x2"])
                q = act(sqj[:, tb, :], d, ACT.Square, r, sqfree[tb], ready["mla_free"],
                        accum_out=smx[:, 0, 0, 4 * tb + n:4 * tb + n + 1])
                sqfree[tb] = q
                sgfree[tb] = r
                gtfree[n % 2] = r1
                if tb == 1:
                    ready[("o2", n)] = r1
                note("x2o", [r, t, q])
                return r0
            return ev

        def part2(n):
            def ev(tb, ps, t):
                w = toks_of(("mkv0", "mkv1", "mq0", "mq1"))
                d = x2p[:, tb, n * 512:(n + 1) * 512]
                r = copyA(d, ps, t, w)
                ready[("x2p", n, tb)] = r
                return r
            return ev

        parts = [list(range(8)), [12, 13, 14, 15, 8, 9, 10, 11]]
        gcol = at("gcol", oEX, [128, 4, 128])

        def side_gta():
            while ("oT", 7) not in ready:
                yield False
            gfree0 = gfree[0] = [ready[("oT", h)] for h in range(8)]
            for n in range(4):
                while n >= 2 and ("o2", n - 2) not in ready:
                    yield False
                yield from gate_rows(gta[:, n % 2, :], 6, n, ("gta", n), lambda n=n: [gtfree[n % 2], gfree0])

        sides.append(side_gta())
        for n in range(4):
            gemm(I["w_out_2"][0][:, n * 512:(n + 1) * 512], parts[0], 512, sto, XT, part2(n),
                 ("mkv0", "mkv1", "mq0", "mq1"), ktneed={kt: ("oT", kt) for kt in parts[0]})
        for n in range(4):
            gemm(I["w_out_2"][0][:, n * 512:(n + 1) * 512], parts[1], 512, sto, XT, out2(n),
                 (), ktneed={kt: ("oT", kt) for kt in parts[1]},
                 evneed=("x2", ("gta", n)))

        fh, fl = (at("fh", oFX, [128, 16, 256], F32R), at("fl", oFX + 16 * KB, [128, 16, 256], F32R))
        sil = at("sil", oFY, [128, 2, 512])
        hn = at("hn", oFY + 4 * KB, [128, 2, 512])
        gtf = at("gtf", oFY + 8 * KB, [128, 4, 512])
        idh = at("idh", oR1, [128, 24, 256], F32R)
        idl = at("idl", oR1 + 24 * KB, [128, 24, 256], F32R)
        acf = acx[:, 0, :]

        def side_h2():
            while "x2o" not in ready or any(("mod", 5, n) not in ready or ("mod", 4, n) not in ready for n in range(4)):
                yield False
            tm = [ready[("mod", c, n)] for c in (4, 5) for n in range(4)]
            a0 = stt(acf, mod[:, 5, :], 1.0, par[:, col["gf"]:col["gf"] + 16], ALU.add, ALU.mult, tm,
                     [ready[("oT", h)] for h in range(8)])
            toks = []
            free = None
            dgf = at("dgf", oFY, [128, 2, 128])
            tn_ = []
            for tb in XT:
                t = V(lambda e, tb=tb: e.tensor_reduce(rs[:, 16 + tb:17 + tb], smx[:, 0, 0, 4 * tb:4 * tb + 4], AX,
                                                       ALU.add), ready["x2o"])
                t = rstd(rs[:, 18 + tb:19 + tb], rs[:, 16 + tb:17 + tb], 1.0 / 2048, EPS_RMS, t)
                tn_.append(diag(dgf[:, tb, :], rs[:, 18 + tb:19 + tb], t, ready["mla_free"]))
            tk, t = yield from to_hT(lambda tb: x2[:, tb, :], [tn_, ready["x2o"]], lambda tb: dgf[:, tb, :],
                                     acf, mod[:, 4, :], fh, fl, (0, 1),
                                     [ready["x2o"], a0], "h2")
            ready["h2"] = tk
            ready["fy_free"] = [t, tk]
            yield True

        sides.append(side_h2())

        def stf(kt, tb):
            return (fh[:, kt, tb * 128:(tb + 1) * 128], fl[:, kt, tb * 128:(tb + 1) * 128])

        def sti(kt, tb):
            return (idh[:, kt % 24, tb * 128:(tb + 1) * 128], idl[:, kt % 24, tb * 128:(tb + 1) * 128])

        silfree = [None, None]
        hnfree = [None]
        gtok = {}

        def ev_gate(s):
            def f(tb, ps, t):
                a = act(sil[:, tb, :], ps, ACT.Sigmoid, t, silfree[tb], ready["fy_free"])
                r = tt(sil[:, tb, :], sil[:, tb, :], ps, ALU.mult, a)
                gtok[s, tb] = r
                return r
            return f

        def ev_up(s):
            key_n[f"hn{s}"] = 2

            def f(tb, ps, t):
                r = tt(hn[:, tb, :], sil[:, tb, :], ps, ALU.mult, t, gtok[s, tb], hnfree[0], ready["fy_free"])
                silfree[tb] = r
                note(f"hn{s}", r)
                return r
            return f

        def side_id():
            for s in range(11):
                while f"hn{s}" not in ready:
                    yield False
                while s >= 6 and "dn0" not in ready:
                    yield False
                w = ready["dn0"] if s >= 6 else [ready["x2o"], ready["mla_free"], ready["h2"]]
                toks = []
                for cp_ in range(2):
                    b = yield from take()
                    for c in range(2):
                        for tb in XT:
                            k = 2 * cp_ + c
                            t = tr(banks[b][:, (2 * c + tb) * 128:(2 * c + tb + 1) * 128],
                                   hn[:, tb, k * 128:(k + 1) * 128], ready[f"hn{s}"], sidefree[b],
                                   sig=(c == 1 and tb == 1))
                    yield True
                    kt = (4 * s + 2 * cp_) % 24
                    h = idh[:, kt:kt + 2, :].rearrange("p a b -> p (a b)")
                    l = idl[:, kt:kt + 2, :].rearrange("p a b -> p (a b)")
                    ta = copyA(h, banks[b][:, :], t, w)
                    tv = tt(l, banks[b][:, :], f32(h), ALU.subtract, ta, w)
                    give(b, tv)
                    toks += [ta, tv]
                hnfree[0] = t
                ready[f"id{s}"] = toks
                yield True

        def side_gtf():
            while "h2" not in ready:
                yield False
            for n in range(4):
                yield from gate_rows(gtf[:, n, :], 7, n, ("gtf", n), lambda: ready["fy_free"])

        sides.append(side_id())
        sides.append(side_gtf())
        ada_rate[0] = ADA_RATE["ffn"]

        gfin = at("gfin", oS1, [128, 2048])
        gfx = at("gfx", oSG, [128, 2, 512])
        gfy = at("gfy", oFX, [128, 2, 2048])
        qfree = [None, None]

        def side_gfin():
            while "h2" not in ready:
                yield False
            ready["gfin"] = Q.dma("G", gfin[:, :], I["g_final_2"].partition_broadcast(128), slot(), ready["x2o"],
                                  ready["h2"], [ready[("oT", h)] for h in range(16)])
            qfree[0] = qfree[1] = [sgfree[0], sgfree[1], ready["h2"]]
            yield True

        sides.append(side_gfin())

        def down(half, n):
            key_n[f"dn{half}"] = 8

            def f(tb, ps, t):
                d = x2[:, tb, n * 512:(n + 1) * 512]
                r0 = tt(sil[:, tb, :], gtf[:, n, :], ps, ALU.mult, t, ready[("gtf", n)], silfree[tb], gtok[10 if half else 5, tb])
                r = tt(d, d, sil[:, tb, :], ALU.add, r0)
                silfree[tb] = r
                q = None
                if half:
                    q = act(gfx[:, tb, 0:512], d, ACT.Square, r, qfree[tb],
                            accum_out=smx[:, 1, 0, 4 * tb + n:4 * tb + n + 1])
                    qfree[tb] = q
                note(f"dn{half}", [r, t, q])
                return r0
            return f

        for half, ss in ((0, range(6)), (1, range(6, 11))):
            for s in ss:
                gemm(I["ffn_wg_2"][0][:, 512 * s:512 * s + 512], list(range(16)), 512, stf, XT, ev_gate(s), (),
                     ktneed={kt: ("h2", kt) for kt in range(16)} if s == 0 else None, evneed=("h2",), ahead=AHEAD)
                gemm(I["ffn_wu_2"][0][:, 512 * s:512 * s + 512], list(range(16)), 512, stf, XT, ev_up(s), ())
            k0 = 4 * ss[0]
            kts = list(range(k0, k0 + 4 * len(ss)))
            for n in range(4):
                gemm(I["ffn_wd_2"][0][:, n * 512:(n + 1) * 512], kts, 512, sti, XT, down(half, n), (),
                     ktneed={kt: f"id{kt // 4}" for kt in kts}, evneed=(("gtf", n),))

        assert not adaq
        main()
        drain_need(("dn1",))
        last = []
        outv = out[0].rearrange("(b p) d -> p b d", p=128)
        for tb in XT:
            t = V(lambda e, tb=tb: e.tensor_reduce(rs[:, 20 + tb:21 + tb], smx[:, 1, 0, 4 * tb:4 * tb + 4], AX, ALU.add),
                  ready["dn1"])
            t = rstd(rs[:, 22 + tb:23 + tb], rs[:, 20 + tb:21 + tb], 1.0 / 2048, EPS_RMS, t)
            for c in range(2):
                cs = slice(c * 1024, (c + 1) * 1024)
                t2 = stt(gfy[:, tb, cs], x2[:, tb, cs], rs[:, 22 + tb:23 + tb], gfin[:, cs], ALU.mult, ALU.mult, t,
                         ready["gfin"])
                last.append(Q.dma("S", outv[:, tb, cs], gfy[:, tb, cs], slot(), t2))
        fin(nc, ctx, Q, last)


def fin(nc, ctx, Q, last):
    block = ctx.enter_context(nc.Block())
    Q.wait("S", last)

    @block.sync
    def _(eng):
        Q.run("S", eng)

    @block.gpsimd
    def _(eng):
        Q.run("G", eng)

    @block.scalar
    def _(eng):
        Q.run("A", eng)

    @block.vector
    def _(eng):
        Q.run("V", eng)

    @block.tensor
    def _(eng):
        Q.run("P", eng)


_INS = ["x", "w_in", "pool_w", "pool_scale", "sgu_ln_g", "sgu_ln_b", "sgu_w", "sgu_b", "attn_sinks", "rel_bias",
        "conv_w", "conv_b", "conv_ln_g", "conv_ln_b", "w_branch", "w_out", "ln_g", "ln_b", "c_2", "ctx_2", "c_ctx_2",
        "w_ada_2", "b_ada_2", "g_attn_2", "g_ffn_2", "w_in_2", "w_out_2", "na_rpb_2", "gqa_gq_2", "gqa_gk_2",
        "mla_gq_2", "mla_gkv_2", "mla_wuq_2", "mla_wukv_2", "diff_lq1_2", "diff_lk1_2", "diff_lq2_2", "diff_lk2_2",
        "diff_gsub_2", "ffn_wg_2", "ffn_wu_2", "ffn_wd_2", "g_final_2"]


def kernel(**inputs):
    import numpy as _np
    import concourse.bacc as _bacc
    from concourse import mybir as _mybir
    from concourse.bass_utils import run_bass_kernel_spmd as _run

    nc = _bacc.Bacc("TRN2", target_bir_lowering=False, num_devices=1)
    given = {n: _np.ascontiguousarray(inputs[n]) for n in _INS}
    given.update(constants())
    arrays, aps = {}, {}
    for name, a in given.items():
        arrays[f"in_{name}"] = a
        aps[name] = nc.dram_tensor(f"in_{name}", a.shape, _mybir.dt.from_np(a.dtype), kind="ExternalInput").ap()
    out = nc.dram_tensor("out_0", (1, 256, 2048), _mybir.dt.float32, kind="ExternalOutput").ap()
    program(nc, aps, out)
    r = _run(nc, [arrays], core_ids=[0])
    return r.results[0]["out_0"]
```
